# Optimizing a Trainium2 kernel written in Bass

```python
import math
import jax, jax.numpy as jnp
from jax import lax
import numpy as np

D_MODEL = 1024
BATCH = 1
SEQ = 512
DEPTH = 1

D_RNN = 1536
LRU_HEADS = 16
LRU_HEAD_DIM = D_RNN // LRU_HEADS
CONV_WIDTH = 4
LRU_C = 8.0
D_S5 = D_MODEL
S5_GROUP = 16
S5_GROUPS = D_S5 // S5_GROUP
S5_STATE = 64
S5_CHUNK = 128
SPLITS = (D_RNN, 2 * D_RNN, 2 * D_RNN + D_S5, 2 * D_RNN + D_S5 + D_MODEL)
D_IN = 2 * D_RNN + D_S5 + 2 * D_MODEL
N_EXPERTS = 64
TOP_K = 8
N_EXPERT_GROUPS = 8
TOPK_GROUPS = 4
D_EXPERT = 256
ROUTED_SCALE = 2.5
EXPERT_CHUNK = 8
D_PLE = 256
LN_EPS = 1e-5
ALPHA = (2 * DEPTH) ** 0.25
BETA = (8 * DEPTH) ** -0.25

kernel_name = 'hybrid_rglru_s5_moe_deepnorm'

def layer_norm(x, g, b):
    xf = x.astype(jnp.float32)
    mu = xf.mean(-1, keepdims=True)
    var = jnp.square(xf - mu).mean(-1, keepdims=True)
    y = (xf - mu) * lax.rsqrt(var + LN_EPS)
    return (y * g.astype(jnp.float32) + b.astype(jnp.float32)).astype(x.dtype)

def causal_depthwise_conv(x, w, b):
    c = x.shape[-1]
    y = lax.conv_general_dilated(x, w[:, None, :], window_strides=(1,),
                                 padding=[(CONV_WIDTH - 1, 0)],
                                 dimension_numbers=('NWC', 'WIO', 'NWC'),
                                 feature_group_count=c)
    return y + b

def _linear_op(e1, e2):
    a1, b1 = e1
    a2, b2 = e2
    return a2 * a1, a2 * b1 + b2

def rg_lru(x, wa, ba, wx, bx, lam):
    bsz, seq, _ = x.shape
    f32 = jnp.float32
    xf = x.astype(f32)
    xh = xf.reshape(bsz, seq, LRU_HEADS, LRU_HEAD_DIM)
    r = jax.nn.sigmoid(jnp.einsum('blhi,hij->blhj', xh, wa.astype(f32)) + ba.astype(f32)).reshape(bsz, seq, D_RNN)
    i = jax.nn.sigmoid(jnp.einsum('blhi,hij->blhj', xh, wx.astype(f32)) + bx.astype(f32)).reshape(bsz, seq, D_RNN)
    log_a = -LRU_C * r * jax.nn.softplus(-lam.astype(f32))
    a = jnp.exp(log_a)
    mult = jnp.sqrt(-jnp.expm1(2.0 * log_a))
    mult = jnp.where(jnp.arange(seq)[None, :, None] == 0, 1.0, mult)
    b = mult * (i * xf)
    _, h = lax.associative_scan(_linear_op, (a, b), axis=1)
    return h.astype(x.dtype)

def _complex_op(e1, e2):
    a1r, a1i, b1r, b1i = e1
    a2r, a2i, b2r, b2i = e2
    ar = a2r * a1r - a2i * a1i
    ai = a2r * a1i + a2i * a1r
    br = a2r * b1r - a2i * b1i + b2r
    bi = a2r * b1i + a2i * b1r + b2i
    return ar, ai, br, bi

def s5_ssm(u, a_re, a_im, b_re, b_im, c_re, c_im, d, log_dt):
    bsz, seq, _ = u.shape
    f32 = jnp.float32
    uf = u.astype(f32)
    ar, ai = a_re.astype(f32), a_im.astype(f32)
    dt = jnp.exp(log_dt.astype(f32))[:, None]
    mag, ph = jnp.exp(dt * ar), dt * ai
    abar_re, abar_im = mag * jnp.cos(ph), mag * jnp.sin(ph)
    den = ar * ar + ai * ai
    z_re = ((abar_re - 1.0) * ar + abar_im * ai) / den
    z_im = (abar_im * ar - (abar_re - 1.0) * ai) / den
    br, bi = b_re.astype(f32), b_im.astype(f32)
    bb_re = z_re[..., None] * br - z_im[..., None] * bi
    bb_im = z_re[..., None] * bi + z_im[..., None] * br
    cr, ci = c_re.astype(f32), c_im.astype(f32)
    steps = jnp.arange(1, S5_CHUNK + 1, dtype=f32)[:, None, None]
    pmag, pph = jnp.exp(steps * dt * ar), steps * dt * ai
    pw_re, pw_im = pmag * jnp.cos(pph), pmag * jnp.sin(pph)
    blk = (bsz, S5_CHUNK, S5_GROUPS, S5_STATE)
    a_blk_re = jnp.broadcast_to(abar_re, blk)
    a_blk_im = jnp.broadcast_to(abar_im, blk)
    n_chunks = seq // S5_CHUNK
    u_chunks = uf.reshape(bsz, n_chunks, S5_CHUNK, S5_GROUPS, S5_GROUP).transpose(1, 0, 2, 3, 4)

    def chunk_step(carry, uc):
        h_re, h_im = carry
        bu_re = jnp.einsum('btgp,gnp->btgn', uc, bb_re)
        bu_im = jnp.einsum('btgp,gnp->btgn', uc, bb_im)
        _, _, hl_re, hl_im = lax.associative_scan(_complex_op, (a_blk_re, a_blk_im, bu_re, bu_im), axis=1)
        hr = hl_re + pw_re * h_re[:, None] - pw_im * h_im[:, None]
        hi = hl_im + pw_re * h_im[:, None] + pw_im * h_re[:, None]
        y = jnp.einsum('gpn,btgn->btgp', cr, hr) - jnp.einsum('gpn,btgn->btgp', ci, hi)
        return (hr[:, -1], hi[:, -1]), y

    init = (jnp.zeros((bsz, S5_GROUPS, S5_STATE), f32), jnp.zeros((bsz, S5_GROUPS, S5_STATE), f32))
    _, ys = lax.scan(chunk_step, init, u_chunks)
    y = ys.transpose(1, 0, 2, 3, 4).reshape(bsz, seq, D_S5)
    y = y + d.astype(f32) * uf
    return y.astype(u.dtype)

def token_mixer(h, w_in, conv_w, conv_b, wa, ba, wx, bx, lam, w_lru_out,
                a_re, a_im, b_re, b_im, c_re, c_im, d, log_dt, w_glu, b_glu, w_out):
    z = jnp.einsum('bld,de->ble', h, w_in)
    x_lru, g_lru, u_s5, gate_a, gate_b = jnp.split(z, SPLITS, axis=-1)
    y_a = jax.nn.gelu(g_lru) * rg_lru(causal_depthwise_conv(x_lru, conv_w, conv_b), wa, ba, wx, bx, lam)
    y_a = jnp.einsum('blr,rd->bld', y_a, w_lru_out)
    y_s = jax.nn.gelu(s5_ssm(u_s5, a_re, a_im, b_re, b_im, c_re, c_im, d, log_dt))
    glu = jnp.einsum('bls,se->ble', y_s, w_glu) + b_glu
    lin, gl = jnp.split(glu, 2, axis=-1)
    y_b = lin * jax.nn.sigmoid(gl)
    merged = jax.nn.sigmoid(gate_a) * y_a + jax.nn.sigmoid(gate_b) * y_b
    return jnp.einsum('bld,de->ble', merged, w_out)

def routed_moe(x, router_w, router_bias, w_gate, w_up, w_down, ws_gate, ws_up, ws_down):
    bsz, seq, d = x.shape
    xt = x.reshape(bsz * seq, d)
    f32 = jnp.float32
    scores = jax.nn.sigmoid(jnp.einsum('td,de->te', xt.astype(f32), router_w.astype(f32)))
    biased = scores + router_bias.astype(f32)
    per_group = N_EXPERTS // N_EXPERT_GROUPS
    grouped = biased.reshape(-1, N_EXPERT_GROUPS, per_group)
    group_score = lax.top_k(grouped, 2)[0].sum(-1)
    _, group_idx = lax.top_k(group_score, TOPK_GROUPS)
    group_mask = jax.nn.one_hot(group_idx, N_EXPERT_GROUPS, dtype=f32).sum(1)
    expert_mask = jnp.repeat(group_mask, per_group, axis=1)
    masked = jnp.where(expert_mask > 0, biased, -jnp.inf)
    _, expert_idx = lax.top_k(masked, TOP_K)
    gate = jnp.take_along_axis(scores, expert_idx, axis=-1)
    gate = ROUTED_SCALE * gate / gate.sum(-1, keepdims=True)
    combine = jnp.einsum('tk,tke->te', gate, jax.nn.one_hot(expert_idx, N_EXPERTS, dtype=f32)).astype(x.dtype)
    y = jnp.einsum('tf,fd->td', jax.nn.silu(xt @ ws_gate) * (xt @ ws_up), ws_down)
    for c in range(N_EXPERTS // EXPERT_CHUNK):
        sl = slice(c * EXPERT_CHUNK, (c + 1) * EXPERT_CHUNK)
        g = jnp.einsum('td,edf->tef', xt, w_gate[sl])
        u = jnp.einsum('td,edf->tef', xt, w_up[sl])
        hdn = jax.nn.silu(g) * u * combine[:, sl, None]
        y = y + jnp.einsum('tef,efd->td', hdn, w_down[sl])
    return y.reshape(bsz, seq, d)

def setup_inputs(seed: int = 0) -> dict:
    key = jax.random.key(seed)
    ks = iter(jax.random.split(key, 48))
    f32 = jnp.float32

    def nrm(shape, scale):
        return jax.random.normal(next(ks), shape, f32) * scale

    L = DEPTH
    x = nrm((BATCH, SEQ, D_MODEL), 1.0)
    p = nrm((DEPTH, BATCH, SEQ, D_PLE), 1.0)
    w_in = nrm((L, D_MODEL, D_IN), D_MODEL ** -0.5)
    conv_w = nrm((L, CONV_WIDTH, D_RNN), CONV_WIDTH ** -0.5)
    conv_b = nrm((L, D_RNN), 0.02)
    lru_wa = nrm((L, LRU_HEADS, LRU_HEAD_DIM, LRU_HEAD_DIM), LRU_HEAD_DIM ** -0.5)
    lru_ba = nrm((L, LRU_HEADS, LRU_HEAD_DIM), 0.02)
    lru_wx = nrm((L, LRU_HEADS, LRU_HEAD_DIM, LRU_HEAD_DIM), LRU_HEAD_DIM ** -0.5)
    lru_bx = nrm((L, LRU_HEADS, LRU_HEAD_DIM), 0.02)
    a_c = jax.random.uniform(next(ks), (L, D_RNN), f32, 0.9, 0.999)
    a0 = a_c ** (1.0 / LRU_C)
    lru_lambda = jnp.log(a0) - jnp.log1p(-a0)
    w_lru_out = nrm((L, D_RNN, D_MODEL), D_RNN ** -0.5)
    s5_a_re = -0.5 * (1.0 + nrm((L, S5_GROUPS, S5_STATE), 0.02))
    s5_a_im = math.pi * jnp.arange(S5_STATE, dtype=f32) + nrm((L, S5_GROUPS, S5_STATE), 0.01)
    s5_b_re = nrm((L, S5_GROUPS, S5_STATE, S5_GROUP), (2 * S5_GROUP) ** -0.5)
    s5_b_im = nrm((L, S5_GROUPS, S5_STATE, S5_GROUP), (2 * S5_GROUP) ** -0.5)
    s5_c_re = nrm((L, S5_GROUPS, S5_GROUP, S5_STATE), S5_STATE ** -0.5)
    s5_c_im = nrm((L, S5_GROUPS, S5_GROUP, S5_STATE), S5_STATE ** -0.5)
    s5_d = nrm((L, D_S5), 0.5)
    s5_log_dt = jax.random.uniform(next(ks), (L, S5_GROUPS), f32, math.log(0.001), math.log(0.1))
    w_glu = nrm((L, D_S5, 2 * D_MODEL), D_S5 ** -0.5)
    b_glu = nrm((L, 2 * D_MODEL), 0.02)
    w_out = nrm((L, D_MODEL, D_MODEL), BETA * D_MODEL ** -0.5)
    ln1_g = 1.0 + nrm((L, D_MODEL), 0.02)
    ln1_b = nrm((L, D_MODEL), 0.02)
    router_w = nrm((L, D_MODEL, N_EXPERTS), D_MODEL ** -0.5)
    router_bias = nrm((L, N_EXPERTS), 0.01)
    moe_w_gate = nrm((L, N_EXPERTS, D_MODEL, D_EXPERT), D_MODEL ** -0.5)
    moe_w_up = nrm((L, N_EXPERTS, D_MODEL, D_EXPERT), D_MODEL ** -0.5)
    moe_w_down = nrm((L, N_EXPERTS, D_EXPERT, D_MODEL), BETA * D_EXPERT ** -0.5)
    shared_w_gate = nrm((L, D_MODEL, D_EXPERT), D_MODEL ** -0.5)
    shared_w_up = nrm((L, D_MODEL, D_EXPERT), D_MODEL ** -0.5)
    shared_w_down = nrm((L, D_EXPERT, D_MODEL), BETA * D_EXPERT ** -0.5)
    ple_w = nrm((L, D_PLE, D_MODEL), BETA * D_PLE ** -0.5)
    ple_gate_w = nrm((L, D_MODEL, D_MODEL), D_MODEL ** -0.5)
    ple_gate_b = nrm((L, D_MODEL), 0.02)
    ln2_g = 1.0 + nrm((L, D_MODEL), 0.02)
    ln2_b = nrm((L, D_MODEL), 0.02)
    return {'x': x, 'p': p, 'w_in': w_in, 'conv_w': conv_w, 'conv_b': conv_b,
            'lru_wa': lru_wa, 'lru_ba': lru_ba, 'lru_wx': lru_wx, 'lru_bx': lru_bx,
            'lru_lambda': lru_lambda, 'w_lru_out': w_lru_out,
            's5_a_re': s5_a_re, 's5_a_im': s5_a_im, 's5_b_re': s5_b_re, 's5_b_im': s5_b_im,
            's5_c_re': s5_c_re, 's5_c_im': s5_c_im, 's5_d': s5_d, 's5_log_dt': s5_log_dt,
            'w_glu': w_glu, 'b_glu': b_glu, 'w_out': w_out, 'ln1_g': ln1_g, 'ln1_b': ln1_b,
            'router_w': router_w, 'router_bias': router_bias,
            'moe_w_gate': moe_w_gate, 'moe_w_up': moe_w_up, 'moe_w_down': moe_w_down,
            'shared_w_gate': shared_w_gate, 'shared_w_up': shared_w_up, 'shared_w_down': shared_w_down,
            'ple_w': ple_w, 'ple_gate_w': ple_gate_w, 'ple_gate_b': ple_gate_b,
            'ln2_g': ln2_g, 'ln2_b': ln2_b}

def reference(x, p, w_in, conv_w, conv_b, lru_wa, lru_ba, lru_wx, lru_bx, lru_lambda, w_lru_out,
              s5_a_re, s5_a_im, s5_b_re, s5_b_im, s5_c_re, s5_c_im, s5_d, s5_log_dt,
              w_glu, b_glu, w_out, ln1_g, ln1_b, router_w, router_bias,
              moe_w_gate, moe_w_up, moe_w_down, shared_w_gate, shared_w_up, shared_w_down,
              ple_w, ple_gate_w, ple_gate_b, ln2_g, ln2_b):
    for i in range(DEPTH):
        mix = token_mixer(x, w_in[i], conv_w[i], conv_b[i], lru_wa[i], lru_ba[i], lru_wx[i], lru_bx[i],
                          lru_lambda[i], w_lru_out[i], s5_a_re[i], s5_a_im[i], s5_b_re[i], s5_b_im[i],
                          s5_c_re[i], s5_c_im[i], s5_d[i], s5_log_dt[i], w_glu[i], b_glu[i], w_out[i])
        x = layer_norm(ALPHA * x + mix, ln1_g[i], ln1_b[i])
        ffn = routed_moe(x, router_w[i], router_bias[i], moe_w_gate[i], moe_w_up[i], moe_w_down[i],
                         shared_w_gate[i], shared_w_up[i], shared_w_down[i])
        ple = jax.nn.sigmoid(jnp.einsum('bld,de->ble', x, ple_gate_w[i]) + ple_gate_b[i]) * \
            jnp.einsum('blq,qd->bld', p[i], ple_w[i])
        x = layer_norm(ALPHA * x + ffn + ple, ln2_g[i], ln2_b[i])
    return x


_drawn_inputs = setup_inputs


def setup_inputs(seed=0):
    import zlib

    import numpy as np

    out = dict(_drawn_inputs(seed))
    spreads = {}
    factors = {'lru_ba': 24.576,
     'lru_bx': 21.848,
     's5_a_re': 64.0,
     's5_b_re': 7.248,
     'b_glu': 3.955,
     'ple_gate_b': 30.011,
     'ln2_g': 8.67,
     'ln2_b': 7.914,
     's5_b_im': 4.004,
     's5_c_re': 3.085,
     's5_c_im': 3.284}
    for name, (base, spread) in spreads.items():
        noise = np.random.default_rng([zlib.crc32(name.encode()), seed]).standard_normal(out[name].shape)
        drawn = base * np.exp(spread * noise) if base else spread * noise
        out[name] = __import__('jax').numpy.asarray(drawn.astype(out[name].dtype))
    for name, factor in factors.items():
        out[name] = (out[name] * factor).astype(out[name].dtype)
    return out
```

```python
import concourse.bass as bass
from concourse import mybir
from contextlib import ExitStack
import math

P = 128
T = 512
TT = T // P
D = 1024
KD = D // P
D_RNN = 1536
MR = D_RNN // P
NB = 4
ML = MR // NB
CB = ML * P
HD = 96
G = 64
GP = 16
NS = 64
L = 8
NC = T // L
NQ = G // 2
QB = NQ // NB
GB = G // NB
E = 64
EG = 8
TOPG = 4
K = 8
F = 256
ALPHA = 2.0 ** 0.25
EPS = 1e-5
SCALE = 2.5
OV = (T * K - E) // P
ROWS = (E + OV + 1) * P
NT = ROWS // P
BIG = 1e30
TWO_PI = 2 * math.pi
MAGIC = 12582912.0
C1 = 6.28125
C2 = round((TWO_PI - C1) * 2 ** 21) / 2 ** 21
C3 = TWO_PI - C1 - C2
PI_IN = 3.1415925


INPUTS = ["x", "p", "w_in", "conv_w", "conv_b", "lru_wa", "lru_ba", "lru_wx", "lru_bx", "lru_lambda",
          "w_lru_out", "s5_a_re", "s5_a_im", "s5_b_re", "s5_b_im", "s5_c_re", "s5_c_im", "s5_d",
          "s5_log_dt", "w_glu", "b_glu", "w_out", "ln1_g", "ln1_b", "router_w", "router_bias",
          "moe_w_gate", "moe_w_up", "moe_w_down", "shared_w_gate", "shared_w_up", "shared_w_down",
          "ple_w", "ple_gate_w", "ple_gate_b", "ln2_g", "ln2_b"]


def decoder_layer(nc, A, out):
    f32 = mybir.dt.float32
    i32 = mybir.dt.int32
    u32 = mybir.dt.uint32
    ALU = mybir.AluOpType
    ACT = mybir.ActivationFunctionType
    AX = mybir.AxisListType.X

    ctx = ExitStack()
    with ctx:
        COLS = 52600
        arena = ctx.enter_context(nc.sbuf_tensor("arena", [P, COLS], f32))
        banks = [ctx.enter_context(nc.psum_tensor(f"bank{i}", [P, 512], f32)) for i in range(8)]

        def dram(name, shape, dt=f32):
            return nc.dram_tensor(name, shape, dt, kind="Internal").ap()

        u_dram = dram("u_dram", (T, D))
        k_dram = dram("k_dram", (NB, GB, GP, (2 * L - 1) * GP))
        x1_dram = dram("x1_dram", (T, D))
        tok_dram = dram("tok_dram", (ROWS, 1))
        y_dram = dram("y_dram", (ROWS, D))

        def sem(name):
            return ctx.enter_context(nc.semaphore(name))

        top = [0]

        def at(off, cols, parts=P):
            assert off + cols <= COLS, (off, cols)
            return arena[0:parts, off:off + cols]

        def new(cols, parts=P):
            off = top[0]
            top[0] += cols
            return at(off, cols, parts)

        ident = new(P)
        ones = new(P)
        strict = new(P)
        chan = new(112)
        c_lru = new(2 * MR)
        lnt = new(8 * MR)
        eps_t = new(8)
        zero256 = new(256)
        xT = new(KD * T).rearrange("p (k t) -> p k t", k=KD)

        base_a = top[0]
        ylru_off = top[0]
        ylru = new(MR * T).rearrange("p (m t) -> p m t", m=MR)
        ysT = new(KD * T).rearrange("p (m t) -> p m t", m=KD)
        wx = new(KD * CB).rearrange("p (k c) -> p k c", k=KD)
        wg = new(KD * CB).rearrange("p (k c) -> p k c", k=KD)
        bd = new(2 * ML * CB).rearrange("p (g k c) -> p g k c", g=2, k=ML)
        lru_off = top[0]
        xc = new(ML * T).rearrange("p (m t) -> p m t", m=ML)
        rr = new(ML * T).rearrange("p (m t) -> p m t", m=ML)
        ii = new(ML * T).rearrange("p (m t) -> p m t", m=ML)
        aa = new(ML * T).rearrange("p (m t) -> p m t", m=ML)
        th = new(ML * T).rearrange("p (m t) -> p m t", m=ML)
        bT = new(2 * GP * NQ).rearrange("p (c j q) -> p c j q", c=2, j=GP)
        cT = new(2 * GP * NQ).rearrange("p (c j q) -> p c j q", c=2, j=GP)
        pw = new((L + 1) * 2 * NQ).rearrange("p (j c q) -> p j c q", j=L + 1, c=2)
        misc = new(5 * NQ).rearrange("p (v q) -> p v q", v=5)
        dT = new(G, GP)
        dI = new(GB * GP, GP).rearrange("p (g j) -> p g j", g=GB)
        qc_off = top[0]
        Q = new(2 * QB * (L + 1) * GP).rearrange("p (c q j o) -> p c q j o", c=2, q=QB, j=L + 1)
        r_off = top[0]
        R = new(2 * QB * P).rearrange("p (c q x) -> p c q x", c=2, q=QB)
        uy_off = top[0]
        U2 = at(uy_off, L * GB * GP, NC).rearrange("p (l x) -> p l x", l=L)
        Y2 = U2
        new(L * GB * GP)
        Kp = at(r_off, GB * (2 * L - 1) * GP, GP).rearrange("p (g x) -> p g x", g=GB)
        rt_off = top[0]
        RT = new(2 * QB * P).rearrange("p (q c x) -> p q c x", q=QB, c=2)
        U2g = at(top[0], GB * P, NC).rearrange("p (g x) -> p g x", g=GB)
        M = new(GB * P).rearrange("p (g x) -> p g x", g=GB)
        U = new(GB * NC).rearrange("p (g c) -> p g c", g=GB)
        Et = new(2 * QB * NC).rearrange("p (c q n) -> p c q n", c=2, q=QB)
        V = new(4 * QB).rearrange("p (c q) -> p c q", c=4)
        hp_off = top[0]
        hp = new(2 * QB * (NC + 1)).rearrange("p (c q n) -> p c q n", c=2, q=QB)
        mag = new(QB * NC).rearrange("p (q n) -> p q n", q=QB)
        tq = QB * (L + 1) * GP
        tmp_off = top[0]
        new(2 * tq)
        tA = at(tmp_off, tq)
        tB = at(tmp_off + tq, tq)
        t5 = [at(tmp_off + n * QB * NC, QB * NC).rearrange("p (q n) -> p q n", q=QB) for n in range(4)]
        wu = at(ylru_off, KD * D).rearrange("p (k c) -> p k c", k=KD)
        xtok0 = at(r_off, TT * D).rearrange("p (t d) -> p t d", t=TT)
        usb = at(rt_off, TT * D).rearrange("p (t d) -> p t d", t=TT)
        braw = at(lru_off, 2 * NS * 2 * GP, NQ).rearrange("p (c x j) -> p c x j", c=2, j=GP)
        craw = [at(o, GP * P, NQ).rearrange("p (j x) -> p j x", j=GP) for o in (lru_off + 4096, ylru_off + 8192)]
        rows = at(tmp_off, P, 112)
        drow = at(tmp_off + P, GP, G)
        s_base = lru_off + 6144
        p_are, p_aim, p_dar, p_ph, p_mg, p_t0, p_t1 = (at(s_base + n * P, P, NQ) for n in range(7))
        pr = at(qc_off, (L + 1) * 2 * P, NQ).rearrange("p (j c x) -> p j c x", j=L + 1, c=2)
        sm = at(tmp_off + 256, 12 * P, NQ).rearrange("p (v x) -> p v x", v=12)
        ldt = at(tmp_off + 256 + 12 * P, 4, NQ)


        pq0, pq1 = (at(o, 4 * P, NQ).rearrange("q (j x) -> q j x", j=4) for o in (hp_off, hp_off + 512))
        mid = ylru_off + MR * T + KD * T
        WB = 4 * KD * 2 * P + MR * 2 * P
        b0, b1 = mid, mid + WB
        wfour = [at(o, 4 * KD * 2 * P).rearrange("p (w k c) -> p w k c", w=4, k=KD) for o in (b0, b1)]
        wlo = [at(o + 4 * KD * 2 * P, MR * 2 * P).rearrange("p (k c) -> p k c", k=MR) for o in (b0, b1)]
        m_off = mid + 2 * WB
        merged = at(m_off, KD * T).rearrange("p (m t) -> p m t", m=KD)
        sg_off = m_off + KD * T
        sg = [[at(sg_off + (5 * n + j) * T, T) for j in range(5)] for n in range(2)]
        tail = sg_off + 10 * T

        x1 = at(ylru_off, TT * D).rearrange("p (t d) -> p t d", t=TT)
        x1T = at(ylru_off + 4096, KD * T).rearrange("p (k t) -> p k t", k=KD)
        plew = at(ylru_off + 8192, 2 * D).rearrange("p (k c) -> p k c", k=2)
        wout = at(b0, KD * D).rearrange("p (k c) -> p k c", k=KD)
        pleg = at(b1, KD * D).rearrange("p (k c) -> p k c", k=KD)
        ptok = at(b1 + 8192, TT * 2 * P).rearrange("p (t c) -> p t c", t=TT)
        pT = at(b1 + 9216, 2 * T).rearrange("p (k t) -> p k t", k=2)
        tmpd = [at(b1 + 10240, D), at(tail + 4096, D)]
        xtok = at(tail, TT * D).rearrange("p (t d) -> p t d", t=TT)
        acc = at(m_off, TT * D).rearrange("p (t d) -> p t d", t=TT)
        lnp = at(sg_off, 5 * D).rearrange("p (v d) -> p v d", v=5)
        wrt = at(tail + 5120, KD * E).rearrange("p (k e) -> p k e", k=KD)
        gu = [at(o, KD * 2 * F).rearrange("p (k w f) -> p k w f", k=KD, w=2)
              for o in (b0, b1, tail, ylru_off + 4096)]
        dn = [at(o, 2 * D).rearrange("p (k c) -> p k c", k=2)
              for o in (b0 + 4096, b1 + 4096, b0 + 6144, b1 + 6144)]
        xg = [at(ylru_off + n * D, D) for n in range(4)]
        xgT = [at(b1 + 8192 + n * D, D).rearrange("p (k s) -> p k s", k=KD) for n in range(2)]
        yb = [at(ylru_off + 8192 + n * D, D) for n in range(2)]
        sil = [at(tail + 4096 + n * F, F) for n in range(2)]
        hdn = [at(tail + 4608 + n * F, F) for n in range(2)]
        hT = [at(tail + 5120 + n * F, F).rearrange("p (k s) -> p k s", k=2) for n in range(2)]
        sil_s = [at(b1 + 10240 + n * F, F) for n in range(2)]
        yg = [at(b0 + n * D, D) for n in range(4)] + [at(b1 + n * D, D) for n in range(4)]
        small = b0 + 8192

        def sc(off, cols, parts=P):
            return at(small + off, cols, parts)

        def te(off, n=E):
            return sc(off, TT * n).rearrange("p (t e) -> p t e", t=TT)

        stats = sc(0, 16)
        rbias = sc(16, E)
        iota_e = sc(80, E)
        score, biased, mask, row, repl = (te(144 + 256 * n) for n in range(5))
        gtop = sc(1424, TT * EG * 8).rearrange("p (g x) -> p g x", g=TT * EG)
        gsum = te(1680, EG)
        gsel = te(1712, EG)
        top8, idx8, idx8f, slotf, sloti, gate = (te(1744 + 32 * n, K) for n in range(6))
        cnt, ovc, ovi, e128, cbase, ones_e = (sc(1936 + E * n, E) for n in range(6))
        tokf = sc(2320, TT)
        gsc = sc(2324, TT)
        novi = sc(2328, 1)
        texpf, texpi, iota_i = (sc(2336 + 32 * n, 32) for n in range(3))
        tokR = sc(2432, P, NT)
        idxT = sc(2560, NT)
        idxcol = sc(2656, 4)
        idxov = sc(2660, 1)
        lt = sc(2664, EG * EG).rearrange("p (a b) -> p a b", a=EG)
        zrow = sc(2728, P, NT)
        zf = sc(2856, 1)
        eqt = at(b0 + 6144, TT * K * E).rearrange("p (t k e) -> p t k e", t=TT, k=K)
        eqp = at(tail, TT * K * E).rearrange("p (t k e) -> p t k e", t=TT, k=K)
        pair = at(tail + 2048, TT * EG * EG).rearrange("p (t a b) -> p t a b", t=TT, a=EG)
        pair2 = at(tail + 2304, TT * EG * EG).rearrange("p (t a b) -> p t a b", t=TT, a=EG)
        texw = at(tail + 2560, 32 * E, 1).rearrange("p (i e) -> p i e", i=32)

        s_x = [sem(f"x_tile_loaded{t}") for t in range(TT)]
        names = """y_zeroed U2_turned b_val o_xT_act rows_loaded s5_loaded bc_loaded wu_loaded const_ready xT_put xT_act xT_dve rows_put rows_kept
            bc_put bc_kept u_put u_kept u_stored dt_ready dar_ready mag_ready trig_ready
            powers_ready powers_put powers_kept lru_exp lru_c_ready
            u2_loaded wx_loaded wg_loaded bd_loaded bd_zeroed U_put U_kept xproj_put conv_begun conv_done
            R_ready RT_put RT_kept gproj_put g_kept Q_ready K_put K_ready k_stored M_loaded S_put h_ready
            gates_put gates_kept decay_ready square_ready ix_ready mult2_ready mult_ready lru_done
            Y_put Y_kept yT_put yT_kept
            wb0_loaded wb1_loaded b_sig b_done xtok_loaded wout_loaded lnp_loaded pleg_loaded
            ple_loaded shared_loaded tab_zeroed res_put res_added var_ready std_ready x1_ready x1_stored
            x1T_put x1T_kept pT_put pT_kept router_put score_ready mask_ready rank_put slot_ready
            tok_stored tok_loaded tokT_put idx_ready ple_put pg_biased pg_sig ple_done
            sh_put sh_silu sh_hid sh_hT_put sh_hT sh_y_put sh_done texp_ready 
            xT_e_put xT_e_act xT_e_dve g_e_put silu_e hid_e hT_e_put hT_e_kept y_e_put y_e_act y_e_dve
            o_gath o_w o_xT_put o_xT_kept o_g_put o_silu o_hid o_hT_put o_hT_kept o_y_put o_y_kept o_y_stored
            over_done out_ready out_stored acc_added""".split()
        S = {n: sem(n) for n in names}
        s_wgu = [sem(f"expert_in{u}") for u in range(4)]
        s_wdn = [sem(f"expert_down{u}") for u in range(4)]
        s_gath = [sem(f"rows_gathered{u}") for u in range(4)]
        s_ys = [sem(f"expert_rows_stored{u}") for u in range(2)]
        s_yg = [sem(f"own_rows_gathered{u}") for u in range(8)]

        def need(eng, name, v):
            if v > 0:
                eng.wait_ge(S[name], v)

        def wait(eng, s, v):
            if not isinstance(v, int) or v > 0:
                eng.wait_ge(s, v)

        block = ctx.enter_context(nc.Block())

        def bc(ap, axis, n):
            shape = list(ap.shape)
            shape.insert(axis, n)
            return ap.unsqueeze(axis).to_broadcast(shape)

        w_in, w_glu, w_lo, w_out = A["w_in"][0], A["w_glu"][0], A["w_lru_out"][0], A["w_out"][0]
        x_tok = A["x"][0].rearrange("(t p) d -> p t d", p=P)
        w_in_k = w_in.rearrange("(p k) c -> p k c", k=KD)
        w_glu_k = w_glu.rearrange("(k p) c -> p k c", p=P)
        w_lo_k = w_lo.rearrange("(k p) c -> p k c", p=P)
        X_COL, G_COL, U_COL, GA_COL, GB_COL = 0, D_RNN, 2 * D_RNN, 2 * D_RNN + D, 2 * D_RNN + 2 * D
        PIECES = []
        for h in range(CB // HD):
            r0 = h * HD
            while r0 < (h + 1) * HD:
                n = min((h + 1) * HD, (r0 // P + 1) * P) - r0
                PIECES.append((h, r0 - h * HD, n, r0 // P, r0 % P))
                r0 += n
        PAIRS = [(k, m) for m in range(ML) for k in range(ML)
                 if any(t == k and h * HD < (m + 1) * P and (h + 1) * HD > m * P for h, _, _, t, _ in PIECES)]
        LRU_BANKS = [2, 3, 0, 1, 2, 3]
        G_BANKS = [3, 0, 1]

        @block.sync
        def _(sp):
            for t in range(TT):
                sp.dma_start(xtok0[:, t, :], x_tok[:, t, :]).then_inc(s_x[t], 16)
            srcs = [(A["conv_w"][0].rearrange("w (m p) -> (w m) p", p=P), 4 * MR)]
            srcs += [(A[n][0].rearrange("(m p) -> m p", p=P), MR) for n in ("conv_b",)]
            srcs += [(A[n][0].rearrange("h j -> (h j)").rearrange("(m p) -> m p", p=P), MR) for n in ("lru_ba", "lru_bx")]
            srcs += [(A["lru_lambda"][0].rearrange("(m p) -> m p", p=P), MR)]
            srcs += [(A["b_glu"][0].rearrange("(m p) -> m p", p=P), 2 * KD)]
            r0 = 0
            for src, n in srcs:
                sp.dma_start(rows[r0:r0 + n, :], src).then_inc(S["rows_loaded"], 16)
                r0 += n
            sp.dma_start(drow, A["s5_d"][0].rearrange("(g j) -> g j", j=GP)).then_inc(S["rows_loaded"], 16)
            sp.dma_start(p_are, A["s5_a_re"][0].rearrange("(q h) n -> q (h n)", h=2)).then_inc(S["s5_loaded"], 16)
            sp.dma_start(p_aim, A["s5_a_im"][0].rearrange("(q h) n -> q (h n)", h=2)).then_inc(S["s5_loaded"], 16)
            sp.dma_start(ldt[:, 0:2], A["s5_log_dt"][0].rearrange("(q h) -> q h", h=2)).then_inc(S["s5_loaded"], 16)
            for hf in range(2):
                sp.dma_start(wu[:, :, hf * 512:(hf + 1) * 512],
                             w_in_k[:, :, U_COL + hf * 512:U_COL + (hf + 1) * 512]).then_inc(S["wu_loaded"], 16)
            for c, n in enumerate(("s5_b_re", "s5_b_im")):
                sp.dma_start(braw[:, c].rearrange("p x j -> p (x j)"),
                             A[n][0].rearrange("(q h) n j -> q (h n j)", h=2)).then_inc(S["bc_loaded"], 16)
            for c, n in enumerate(("s5_c_re", "s5_c_im")):
                for h in range(2):
                    sp.dma_start(craw[c][:, :, h * NS:(h + 1) * NS],
                                 A[n][0].rearrange("(q h) j n -> h q j n", h=2)[h]).then_inc(S["bc_loaded"], 16)

            def load_x(b):
                sp.dma_start(wx, w_in_k[:, :, X_COL + b * CB:X_COL + (b + 1) * CB]).then_inc(S["wx_loaded"], 16)

            def load_g(b):
                sp.dma_start(wg, w_in_k[:, :, G_COL + b * CB:G_COL + (b + 1) * CB]).then_inc(S["wg_loaded"], 16)

            def load_bd(b):
                for g, n in enumerate(("lru_wa", "lru_wx")):
                    for h, i0, cnt_, t, p0 in PIECES:
                        sp.dma_start(bd[p0:p0 + cnt_, g, t, h * HD:(h + 1) * HD],
                                     A[n][0, b * (CB // HD) + h, i0:i0 + cnt_, :]).then_inc(S["bd_loaded"], 16)

            def load_u2(b):
                sp.dma_start(U2, u_dram.rearrange("(c l) x -> c l x", l=L)[:, :, b * GB * GP:(b + 1) * GB * GP]
                             ).then_inc(S["u2_loaded"], 16)

            load_x(0)
            load_g(0)
            sp.wait_ge(S["bd_zeroed"], 1)
            load_bd(0)
            sp.wait_ge(S["u_kept"], 2 * TT)
            sp.dma_start(u_dram.rearrange("(t p) d -> p t d", p=P), usb).then_inc(S["u_stored"], 16)
            sp.wait_ge(S["u_stored"], 16)
            sp.wait_ge(S["const_ready"], 1)
            sp.wait_ge(S["xT_put"], 2 * TT)
            load_u2(0)
            for n in range(E, NT):
                sp.dma_start(y_dram[n * P:(n + 1) * P, :].rearrange("p (r x) -> p r x", x=256),
                             bc(zero256, 1, D // 256)).then_inc(S["y_zeroed"], 16)
            for b in range(NB):
                if b + 1 < NB:
                    sp.wait_ge(S["xproj_put"], ML * (b + 1))
                    load_x(b + 1)
                    sp.wait_ge(S["gproj_put"], ML * (b + 1))
                    load_g(b + 1)
                sp.wait_ge(S["K_ready"], b + 1)
                sp.dma_start(k_dram[b].rearrange("g j x -> j g x"), Kp).then_inc(S["k_stored"], 16)
                sp.wait_ge(S["k_stored"], 16 * (b + 1))
                need(sp, "Y_put", 2 * b)
                for l in range(L):
                    sp.dma_start(M[l * GP:(l + 1) * GP],
                                 k_dram[b, :, :, (L - 1 - l) * GP:(L - 1 - l) * GP + L * GP]
                                 .rearrange("g j x -> j g x")).then_inc(S["M_loaded"], 16)
                if b + 1 < NB:
                    sp.wait_ge(S["gates_put"], 2 * ML * (b + 1))
                    load_bd(b + 1)
                    sp.wait_ge(S["yT_put"], 2 * (b + 1))
                    load_u2(b + 1)

            def load_b(m):
                n = m % 2
                cols = 2 * P * m
                for w, (src, c0) in enumerate(((w_in_k, GA_COL), (w_in_k, GB_COL), (w_glu_k, 0), (w_glu_k, D))):
                    sp.dma_start(wfour[n][:, w], src[:, :, c0 + cols:c0 + cols + 2 * P]).then_inc(S[f"wb{n}_loaded"], 16)
                sp.dma_start(wlo[n], w_lo_k[:, :, cols:cols + 2 * P]).then_inc(S[f"wb{n}_loaded"], 16)

            sp.wait_ge(S["lru_done"], MR)
            sp.wait_ge(S["yT_kept"], 2 * NB)
            load_b(0)
            load_b(1)
            sp.dma_start(xtok, x_tok).then_inc(S["xtok_loaded"], 16)
            for m in range(2, 4):
                sp.wait_ge(S["b_val"], 10 * (m - 1))
                load_b(m)
            sp.wait_ge(S["b_val"], 30)
            sp.dma_start(wout, w_out.rearrange("(k p) c -> p k c", p=P)).then_inc(S["wout_loaded"], 16)
            sp.dma_start(rbias, A["router_bias"][0].partition_broadcast(P)).then_inc(S["lnp_loaded"], 16)
            sp.wait_ge(S["b_val"], 40)
            sp.dma_start(plew, A["ple_w"][0].rearrange("(p k) c -> p k c", k=2)).then_inc(S["ple_loaded"], 16)
            sp.dma_start(ptok, A["p"][0, 0].rearrange("(t p) c -> p t c", p=P)).then_inc(S["ple_loaded"], 16)
            sp.dma_start(wrt, A["router_w"][0].rearrange("(p k) e -> p k e", k=KD)).then_inc(S["ple_loaded"], 16)
            sp.dma_start(pleg, A["ple_gate_w"][0].rearrange("(p k) c -> p k c", k=KD)).then_inc(S["pleg_loaded"], 16)
            sp.wait_ge(S["b_done"], KD)
            for v, n in enumerate(("ln1_g", "ln1_b", "ln2_g", "ln2_b", "ple_gate_b")):
                sp.dma_start(lnp[:, v, :], A[n][0].partition_broadcast(P)).then_inc(S["lnp_loaded"], 16)
            sp.wait_ge(S["res_put"], 2 * TT)
            for w, n in enumerate(("shared_w_gate", "shared_w_up")):
                sp.dma_start(gu[0][:, :, w, :], A[n][0].rearrange("(p k) f -> p k f", k=KD)).then_inc(S["shared_loaded"], 16)
            sp.dma_start(dn[0], A["shared_w_down"][0].rearrange("(p k) c -> p k c", k=2)).then_inc(S["shared_loaded"], 16)
            for t in range(TT):
                sp.wait_ge(S["x1_ready"], t + 1)
                sp.dma_start(x1_dram[t * P:(t + 1) * P, :], x1[:, t, :]).then_inc(S["x1_stored"], 16)

            w_gate_e = A["moe_w_gate"][0].rearrange("e (p k) f -> e p k f", k=KD)
            w_up_e = A["moe_w_up"][0].rearrange("e (p k) f -> e p k f", k=KD)
            w_down_e = A["moe_w_down"][0].rearrange("e (p k) c -> e p k c", k=2)

            def load_in(e, u, done):
                for w, src in enumerate((w_gate_e, w_up_e)):
                    sp.dma_start(gu[u][:, :, w, :], src[bass.ds(e, 1)].rearrange("o p k f -> p (o k) f")).then_inc(done, 16)

            def load_down(e, u, done):
                sp.dma_start(dn[u], w_down_e[bass.ds(e, 1)].rearrange("o p k c -> p (o k) c")).then_inc(done, 16)

            def load_expert(e, u, in_done, down_done):
                load_in(e, u, in_done)
                load_down(e, u, down_done)

            sp.wait_ge(S["ple_done"], TT)
            sp.wait_ge(S["idx_ready"], 1)
            load_expert(1, 1, s_wgu[1], s_wdn[1])
            load_expert(2, 2, s_wgu[2], s_wdn[2])
            sp.wait_ge(S["sh_done"], TT)
            load_expert(0, 0, s_wgu[0], s_wdn[0])
            load_expert(3, 3, s_wgu[3], s_wdn[3])
            with sp.Fori(0, E // 4 - 1) as i:
                for u in range(4):
                    sp.wait_ge(S["g_e_put"], 4 * i + (u + 1))
                    load_in(4 * i + (4 + u), u, s_wgu[u])
                    sp.wait_ge(S["y_e_put"], 4 * i + (u + 1))
                    load_down(4 * i + (4 + u), u, s_wdn[u])
            sp.wait_ge(S["y_e_put"], E)
            sp.wait_ge(S["texp_ready"], 1)
            n_over = sp.value_load(novi[0:1, 0:1].bitcast(i32), min_val=0, max_val=OV)
            with sp.Fori(0, OV) as i:
                with sp.If(i < n_over):
                    e = sp.value_load(texpi[0:1, bass.ds(i, 1)].bitcast(i32), min_val=0, max_val=E - 1)
                    sp.wait_ge(S["o_y_kept"], i + 1)
                    load_expert(e, 0, S["o_w"], S["o_w"])
                    sp.wait_ge(S["o_y_kept"], i + 2)
                    sp.dma_start(y_dram[bass.ds(E * P + i * P, P), :], yb[0]).then_inc(S["o_y_stored"], 16)
                    sp.wait_ge(S["o_y_stored"], 16 * (i + 1))
                    sp.sem_inc(S["over_done"], 1)
                sp.nop()
            sp.sem_inc(S["over_done"], 1)
            for t in range(TT):
                sp.wait_ge(S["out_ready"], t + 1)
                sp.dma_start(out[0, t * P:(t + 1) * P, :], acc[:, t, :]).then_inc(S["out_stored"], 16)
            sp.wait_ge(S["out_stored"], 16 * TT)
            sp.wait_ge(S["x1_stored"], 16 * TT)
            sp.wait_ge(S["y_zeroed"], 16 * (NT - E))
            for u in range(2):
                sp.wait_ge(s_ys[u], 16 * E // 2)

        @block.gpsimd
        def _(pool):
            nc.gpsimd.memset(ident, 0.0)
            nc.gpsimd.memset(ones, 1.0)
            nc.gpsimd.memset(strict, 1.0)
            nc.gpsimd.memset(eps_t, EPS)
            nc.gpsimd.memset(zero256, 0.0)
            pool.drain()
            nc.gpsimd.affine_select(out=ident, in_=ident, compare_op=ALU.not_equal, fill=1.0, base=0,
                                    pattern=[[-1, P]], channel_multiplier=1)
            nc.gpsimd.affine_select(out=strict, in_=strict, compare_op=ALU.is_gt, fill=0.0, base=0,
                                    pattern=[[1, P]], channel_multiplier=-1)
            pool.drain()
            pool.sem_inc(S["const_ready"], 1)
            nc.gpsimd.memset(bd.rearrange("p g k c -> p (g k c)"), 0.0).then_inc(S["bd_zeroed"], 1)
            for b in range(NB):
                pool.wait_ge(S["u2_loaded"], 16 * (b + 1))
                if b == 0:
                    pool.wait_ge(S["u_stored"], 16)
                need(pool, "Y_put", 2 * b)
                nc.gpsimd.tensor_copy(U2g.rearrange("c g (l o) -> c l g o", l=L),
                                      U2.rearrange("c l (g o) -> c l g o", g=GB)).then_inc(S["U2_turned"], 1)
                for m in range(ML):
                    pool.wait_ge(S["decay_ready"], ML * b + m + 1)
                    nc.gpsimd.tensor_tensor(rr[:, m], aa[:, m], aa[:, m], ALU.mult).then_inc(S["square_ready"], 1)
                    nc.gpsimd.tensor_tensor(ii[:, m], ii[:, m], xc[:, m], ALU.mult).then_inc(S["ix_ready"], 1)
            pool.wait_ge(S["b_val"], 30)
            nc.gpsimd.memset(zrow, 0.0)
            nc.gpsimd.memset(ones_e, 1.0)
            nc.gpsimd.iota(iota_e, [[1, E]], base=0, channel_multiplier=0, allow_small_or_imprecise_dtypes=True)
            nc.gpsimd.iota(e128, [[P, E]], base=0, channel_multiplier=0, allow_small_or_imprecise_dtypes=True)
            nc.gpsimd.iota(tokf, [[P, TT]], base=0, channel_multiplier=1, allow_small_or_imprecise_dtypes=True)
            nc.gpsimd.iota(iota_i, [[1, 32]], base=0, channel_multiplier=0, allow_small_or_imprecise_dtypes=True)
            nc.gpsimd.memset(lt.rearrange("p a b -> p (a b)"), 1.0)
            pool.drain()
            nc.gpsimd.affine_select(out=lt, in_=lt, compare_op=ALU.is_gt, fill=0.0, base=0,
                                    pattern=[[1, EG], [-1, EG]], channel_multiplier=0)
            nc.gpsimd.dma_start(tok_dram.rearrange("(n p) o -> n (p o)", p=P), zrow).then_inc(S["tab_zeroed"], 16)
            pool.drain()
            pool.sem_inc(S["const_ready"], 1)
            pool.wait_ge(S["tab_zeroed"], 16)
            pool.wait_ge(S["slot_ready"], 1)
            for t in range(TT):
                for k in range(K):
                    nc.gpsimd.indirect_dma_start(
                        out=tok_dram, out_offset=bass.IndirectOffsetOnAxis(ap=sloti[:, t, k:k + 1].bitcast(u32), axis=0),
                        in_=tokf[:, t:t + 1], in_offset=None).then_inc(S["tok_stored"], 16)
            pool.wait_ge(S["tok_stored"], 16 * TT * K)
            nc.gpsimd.dma_start(tokR, tok_dram.rearrange("(n p) o -> n (p o)", p=P)).then_inc(S["tok_loaded"], 16)

            def gather(e, u):
                nc.gpsimd.tensor_copy(idxcol[:, u:u + 1].bitcast(i32), idxT[:, bass.ds(e, 1)].bitcast(i32))
                pool.drain()
                nc.gpsimd.indirect_dma_start(
                    out=xg[u], out_offset=None, in_=x1_dram,
                    in_offset=bass.IndirectOffsetOnAxis(ap=idxcol[:, u:u + 1].bitcast(u32), axis=0)).then_inc(s_gath[u], 16)

            pool.wait_ge(S["idx_ready"], 1)
            pool.wait_ge(S["x1_stored"], 16 * TT)
            pool.wait_ge(S["sh_done"], TT)
            for u in range(4):
                gather(u, u)
            with pool.Fori(0, E // 4 - 1) as i:
                for u in range(4):
                    pool.wait_ge(S["xT_e_put"], 4 * i + (u + 1))
                    gather(4 * i + (4 + u), u)
            pool.wait_ge(S["xT_e_put"], E)
            pool.wait_ge(S["texp_ready"], 1)
            n_over = pool.value_load(novi[0:1, 0:1].bitcast(i32), min_val=0, max_val=OV)
            with pool.Fori(0, OV) as i:
                with pool.If(i < n_over):
                    pool.wait_ge(S["o_y_kept"], i + 1)
                    nc.gpsimd.tensor_copy(idxov.bitcast(i32), idxT[:, bass.ds(i + E, 1)].bitcast(i32))
                    pool.drain()
                    nc.gpsimd.indirect_dma_start(
                        out=xg[0], out_offset=None, in_=x1_dram,
                        in_offset=bass.IndirectOffsetOnAxis(ap=idxov.bitcast(u32), axis=0)).then_inc(S["o_gath"], 16)
                pool.nop()
            for u in range(2):
                pool.wait_ge(s_ys[u], 16 * E // 2)
            pool.wait_ge(S["over_done"], n_over + 1)
            pool.sem_inc(S["over_done"], 1)
            for n in range(TT * K):
                t, k = divmod(n, K)
                if n >= K:
                    pool.wait_ge(S["acc_added"], n - K + 1)
                nc.gpsimd.indirect_dma_start(
                    out=yg[n % K], out_offset=None, in_=y_dram,
                    in_offset=bass.IndirectOffsetOnAxis(ap=sloti[:, t, k:k + 1].bitcast(u32), axis=0)).then_inc(s_yg[n % K], 16)

        mm = nc.tensor.matmul

        @block.tensor
        def _(pe):
            def tp(dst, src, n):
                return nc.tensor.transpose(dst, src, ident[0:n, 0:n])

            pe.wait_ge(S["const_ready"], 1)
            for t in range(TT):
                pe.wait_ge(s_x[t], 16)
                xv = xtok0[:, t, :].rearrange("p (d k) -> p k d", k=KD)
                for h in range(2):
                    for k in range(4):
                        last = tp(banks[2 * t + h][:, k * P:(k + 1) * P], xv[:, 4 * h + k, :], P)
                    last.then_inc(S["xT_put"], 1)
            pe.wait_ge(S["rows_loaded"], 16 * 7)
            pe.wait_ge(S["xT_act"], 1)
            tp(banks[0][:, 0:112], rows, 112)
            tp(banks[0][0:GP, P:P + G], drow, G).then_inc(S["rows_put"], 1)
            pe.wait_ge(S["bc_loaded"], 16 * 6)
            pe.wait_ge(S["xT_dve"], 2)
            pe.wait_ge(S["xT_act"], 3)
            for c in range(4):
                for j in range(GP):
                    src = braw[:, c, :, j] if c < 2 else craw[c - 2][:, j, :]
                    last = tp(banks[1 + c][:, j * NQ:(j + 1) * NQ], src, NQ)
                last.then_inc(S["bc_put"], 1)
            pe.wait_ge(S["wu_loaded"], 32)
            pe.wait_ge(S["xT_act"], TT)
            pe.wait_ge(S["xT_dve"], TT)
            for n in range(2 * TT):
                hf, t = divmod(n, TT)
                if n == 3:
                    pe.wait_ge(S["rows_kept"], 1)
                if n > 3:
                    pe.wait_ge(S["bc_kept"], 4)
                for k in range(KD):
                    last = mm(banks[(5 + n) % 8][:, :], xT[:, k, t * P:(t + 1) * P], wu[:, k, hf * 512:(hf + 1) * 512],
                              start=(k == 0), stop=(k == KD - 1))
                last.then_inc(S["u_put"], 1)
            pe.wait_ge(S["powers_ready"], 1)
            pe.wait_ge(S["u_kept"], 2)
            for j in range(1, L + 1):
                for c in range(2):
                    n = 2 * (j - 1) + c
                    tp(banks[5][:, n * NQ:(n + 1) * NQ], pr[:, j, c, :], NQ)
            for n, v in enumerate((8, 10, 7, 3, 2)):
                last = tp(banks[6][:, n * NQ:(n + 1) * NQ], sm[:, v, :], NQ)
            last.then_inc(S["powers_put"], 1)

            for b in range(NB):
                pe.wait_ge(S["U2_turned"], b + 1)
                if b == 0:
                    pe.wait_ge(S["u_kept"], 2 * TT)
                    pe.wait_ge(S["powers_kept"], 1)
                else:
                    pe.wait_ge(S["yT_kept"], 2 * b)
                for g in range(GB):
                    last = tp(banks[4 + g // 8][:, (g % 8) * NC:(g % 8 + 1) * NC], U2g[:, g, :], NC)
                    if g % 8 == 7:
                        last.then_inc(S["U_put"], 1)
                pe.wait_ge(S["wx_loaded"], 16 * (b + 1))
                need(pe, "gates_kept", 6 * b)
                for m in range(ML):
                    for k in range(KD):
                        last = mm(banks[m][:, :], wx[:, k, m * P:(m + 1) * P], xT[:, k, :], start=(k == 0), stop=(k == KD - 1))
                    last.then_inc(S["xproj_put"], 1)
                pe.wait_ge(S["R_ready"], b + 1)
                pe.wait_ge(S["U_kept"], 2 * (b + 1))
                need(pe, "Y_kept", 4 * b)
                for n in range(2 * QB):
                    q, c = divmod(n, 2)
                    last = tp(banks[4 + n // 4][:, (n % 4) * P:(n % 4 + 1) * P], R[:, c, q, :], P)
                    if n % 4 == 3:
                        last.then_inc(S["RT_put"], 1)
                pe.wait_ge(S["wg_loaded"], 16 * (b + 1))
                for m in range(ML):
                    if m:
                        pe.wait_ge(S["conv_done"], ML * b + m)
                    for k in range(KD):
                        last = mm(banks[G_BANKS[m]][:, :], wg[:, k, m * P:(m + 1) * P], xT[:, k, :],
                                  start=(k == 0), stop=(k == KD - 1))
                    last.then_inc(S["gproj_put"], 1)
                pe.wait_ge(S["Q_ready"], b + 1)
                for g in range(GB):
                    q, h = divmod(g, 2)
                    hs = slice(h * NS, (h + 1) * NS)
                    if g == 0:
                        pe.wait_ge(S["RT_kept"], 4 * (b + 1))
                    for c in range(2):
                        last = mm(banks[4 + 2 * h + q // 4][0:GP, (q % 4) * P:(q % 4 + 1) * P], bT[hs, c, :, b * QB + q],
                                  Q[hs, c, q, 0:L, :], start=(c == 0), stop=(c == 1))
                    if g % 8 == 7:
                        last.then_inc(S["K_put"], 1)
                pe.wait_ge(S["K_ready"], b + 1)
                for c in range(2):
                    for q in range(QB):
                        for h in range(2):
                            last = mm(banks[4 + c][h * NS:(h + 1) * NS, q * NC:(q + 1) * NC],
                                      RT[:, q, c, h * NS:(h + 1) * NS], U[:, 2 * q + h, :], start=True, stop=True)
                last.then_inc(S["S_put"], 1)
                pe.wait_ge(S["bd_loaded"], 16 * 2 * len(PIECES) * (b + 1))
                pe.wait_ge(S["conv_done"], ML * (b + 1))
                for n in range(2 * ML):
                    g, m = divmod(n, ML)
                    if n in (1, 2, 3):
                        pe.wait_ge(S["g_kept"], ML * b + n)
                    if n > 3:
                        pe.wait_ge(S["gates_kept"], 6 * b + n - 3)
                    ks = [k for k, mt in PAIRS if mt == m]
                    for k in ks:
                        last = mm(banks[LRU_BANKS[n]][:, :], bd[:, g, k, m * P:(m + 1) * P], xc[:, k, :],
                                  start=(k == ks[0]), stop=(k == ks[-1]))
                    last.then_inc(S["gates_put"], 1)
                pe.wait_ge(S["h_ready"], b + 1)
                pe.wait_ge(S["M_loaded"], 16 * L * (b + 1))
                for g in range(GB):
                    q, h = divmod(g, 2)
                    hs = slice(h * NS, (h + 1) * NS)
                    dst = banks[4 + 2 * h + q // 4][0:NC, (q % 4) * P:(q % 4 + 1) * P]
                    mm(dst, U[:, g, :], M[:, g, :], start=True, stop=False)
                    mm(dst, hp[hs, 0, q, 0:NC], Q[hs, 0, q, 1:L + 1, :], start=False, stop=False)
                    last = mm(dst, hp[hs, 1, q, 0:NC], Q[hs, 1, q, 1:L + 1, :], start=False, stop=True)
                    if g % 8 == 7:
                        last.then_inc(S["Y_put"], 1)
                pe.wait_ge(S["Y_kept"], 4 * (b + 1))
                for s in range(2):
                    for l in range(L):
                        last = tp(banks[4 + s][:, l * NC:(l + 1) * NC], Y2[:, l, s * P:(s + 1) * P], NC)
                    last.then_inc(S["yT_put"], 1)

            for m in range(KD):
                if m == 0:
                    pe.wait_ge(S["yT_kept"], 2 * NB)
                    pe.wait_ge(S["lru_done"], MR)
                    pe.wait_ge(S["gates_kept"], 6 * NB)
                if m % 2 == 0:
                    pe.wait_ge(S[f"wb{m // 2 % 2}_loaded"], 16 * 5 * (m // 4 + 1))
                n = m // 2 % 2
                cs = slice((m % 2) * P, (m % 2 + 1) * P)
                for j, w in enumerate((0, 1, 3, 2, 4)):
                    v = 5 * m + j
                    if v >= 8:
                        pv = v - 8
                        pm, pj = divmod(pv, 5)
                        if pj < 3:
                            pe.wait_ge(S["b_sig"], 3 * pm + pj + 1)
                        else:
                            pe.wait_ge(S["b_done"], pm + 1)
                    nk = MR if w == 4 else KD
                    for k in range(nk):
                        lhs = wlo[n][:, k, cs] if w == 4 else wfour[n][:, w, k, cs]
                        rhs = ylru[:, k, :] if w == 4 else (xT[:, k, :] if w < 2 else ysT[:, k, :])
                        last = mm(banks[v % 8][:, :], lhs, rhs, start=(k == 0), stop=(k == nk - 1))
                    last.then_inc(S["b_val"], 1)
            pe.wait_ge(S["wout_loaded"], 16)
            pe.wait_ge(S["b_done"], KD)
            for n in range(2 * TT):
                t, hf = divmod(n, 2)
                if n >= 4:
                    pe.wait_ge(S["res_added"], n - 3)
                for k in range(KD):
                    last = mm(banks[n % 4][:, :], merged[:, k, t * P:(t + 1) * P], wout[:, k, hf * 512:(hf + 1) * 512],
                              start=(k == 0), stop=(k == KD - 1))
                last.then_inc(S["res_put"], 1)
            pe.wait_ge(S["ple_loaded"], 48)
            for c in range(2):
                for t in range(TT):
                    last = tp(banks[6 + c][:, t * P:(t + 1) * P], ptok[:, t, :].rearrange("p (d k) -> p k d", k=2)[:, c, :], P)
            last.then_inc(S["pT_put"], 1)
            for t in range(TT):
                pe.wait_ge(S["x1_ready"], t + 1)
                if t:
                    pe.wait_ge(S["x1T_kept"], 2 * t)
                xv = x1[:, t, :].rearrange("p (d k) -> p k d", k=KD)
                for h in range(2):
                    for k in range(4):
                        last = tp(banks[4 + h][:, k * P:(k + 1) * P], xv[:, 4 * h + k, :], P)
                last.then_inc(S["x1T_put"], 1)
            pe.wait_ge(S["x1T_kept"], 2 * TT)
            pe.wait_ge(S["pT_kept"], 2)
            for t in range(TT):
                for k in range(KD):
                    last = mm(banks[6][:, t * E:(t + 1) * E], x1T[:, k, t * P:(t + 1) * P], wrt[:, k, :],
                              start=(k == 0), stop=(k == KD - 1))
            last.then_inc(S["router_put"], 1)

            def ple(t):
                for hf in range(2):
                    if t:
                        pe.wait_ge(S["pg_biased"], 2 * (t - 1) + hf + 1)
                    else:
                        pe.wait_ge(S["res_added"], 2 * TT)
                    for k in range(KD):
                        last = mm(banks[hf][:, :], x1T[:, k, t * P:(t + 1) * P], pleg[:, k, hf * 512:(hf + 1) * 512],
                                  start=(k == 0), stop=(k == KD - 1))
                    last.then_inc(S["ple_put"], 1)
                if t:
                    pe.wait_ge(S["ple_done"], t)
                for hf in range(2):
                    for k in range(2):
                        last = mm(banks[2 + hf][:, :], pT[:, k, t * P:(t + 1) * P], plew[:, k, hf * 512:(hf + 1) * 512],
                                  start=(k == 0), stop=(k == 1))
                last.then_inc(S["ple_put"], 1)

            pe.wait_ge(S["pleg_loaded"], 16)
            ple(0)
            ple(1)
            pe.wait_ge(S["mask_ready"], 1)
            for t in range(TT):
                for s in range(t + 1):
                    mm(banks[7][:, t * E:(t + 1) * E], strict if s == t else ones, mask[:, s, :], start=(s == 0), stop=(s == t))
            for s in range(TT):
                last = mm(banks[7][:, TT * E:(TT + 1) * E], ones, mask[:, s, :], start=(s == 0), stop=(s == TT - 1))
            last.then_inc(S["rank_put"], 1)
            ple(2)
            ple(3)
            pe.wait_ge(S["shared_loaded"], 48)

            def sh_in(t):
                if t >= 2:
                    pe.wait_ge(S["sh_hid"], t - 1)
                for k in range(KD):
                    last = mm(banks[4 + t % 2][:, :], x1T[:, k, t * P:(t + 1) * P], gu[0][:, k, :, :],
                              start=(k == 0), stop=(k == KD - 1))
                last.then_inc(S["sh_put"], 1)

            def sh_out(t):
                pe.wait_ge(S["sh_hid"], t + 1)
                if t == 0:
                    pe.wait_ge(S["ple_done"], TT)
                else:
                    pe.wait_ge(S["sh_hT"], t)
                hv = hdn[t % 2].rearrange("p (d k) -> p k d", k=2)
                for k in range(2):
                    last = tp(banks[0][:, k * P:(k + 1) * P], hv[:, k, :], P)
                last.then_inc(S["sh_hT_put"], 1)
                pe.wait_ge(S["sh_hT"], t + 1)
                pe.wait_ge(S["slot_ready"], 1)
                if t:
                    pe.wait_ge(S["sh_done"], t)
                for hf in range(2):
                    for k in range(2):
                        last = mm(banks[6 + hf][:, :], hT[t % 2][:, k, :], dn[0][:, k, hf * 512:(hf + 1) * 512],
                                  start=(k == 0), stop=(k == 1))
                last.then_inc(S["sh_y_put"], 1)

            sh_in(0)
            for t in range(TT):
                if t + 1 < TT:
                    sh_in(t + 1)
                sh_out(t)
            pe.wait_ge(S["tok_loaded"], 16)
            tp(banks[1][:, 0:NT], tokR, NT).then_inc(S["tokT_put"], 1)

            def x_turn(i, u):
                pe.wait_ge(s_gath[u % 4], 16 * i + 16 * (u // 4 + 1))
                wait(pe, S["xT_e_act"], 4 * i + u)
                wait(pe, S["xT_e_dve"], 4 * i + u)
                xv = xg[u % 4].rearrange("p (d k) -> p k d", k=KD)
                for h in range(2):
                    for k in range(4):
                        last = tp(banks[h][:, k * P:(k + 1) * P], xv[:, 4 * h + k, :], P)
                last.then_inc(S["xT_e_put"], 1)

            def gate_up(i, u):
                pe.wait_ge(s_wgu[u % 4], 32 * i + 32 * (u // 4 + 1))
                pe.wait_ge(S["xT_e_act"], 4 * i + u + 1)
                pe.wait_ge(S["xT_e_dve"], 4 * i + u + 1)
                for k in range(KD):
                    last = mm(banks[2 + u % 2][:, :], xgT[u % 2][:, k, :], gu[u % 4][:, k, :, :],
                              start=(k == 0), stop=(k == KD - 1))
                last.then_inc(S["g_e_put"], 1)

            def hid_turn(i, u):
                pe.wait_ge(S["hid_e"], 4 * i + u + 1)
                hv = hdn[u % 2].rearrange("p (d k) -> p k d", k=2)
                for k in range(2):
                    last = tp(banks[4][:, k * P:(k + 1) * P], hv[:, k, :], P)
                last.then_inc(S["hT_e_put"], 1)

            def down(i, u):
                pe.wait_ge(s_wdn[u % 4], 16 * i + 16 * (u // 4 + 1))
                pe.wait_ge(S["hT_e_kept"], 4 * i + u + 1)
                wait(pe, S["y_e_act"], 4 * i + u)
                wait(pe, S["y_e_dve"], 4 * i + u)
                for hf in range(2):
                    for k in range(2):
                        last = mm(banks[5 + hf][:, :], hT[u % 2][:, k, :], dn[u % 4][:, k, hf * 512:(hf + 1) * 512],
                                  start=(k == 0), stop=(k == 1))
                last.then_inc(S["y_e_put"], 1)

            def expert(i, u, more=True):
                gate_up(i, u)
                if more:
                    x_turn(i, u + 1)
                if not isinstance(i, int) or u:
                    down(i, u - 1)
                hid_turn(i, u)

            pe.wait_ge(S["idx_ready"], 1)
            pe.wait_ge(S["sh_done"], TT)
            x_turn(0, 0)
            for u in range(0, 5):
                expert(0, u)
            with pe.Fori(1, E // 4 - 1) as i:
                for u in range(1, 5):
                    expert(i, u)
            for n in range(E - 3, E):
                expert(0, n, more=n + 1 < E)
            down(0, E - 1)
            pe.wait_ge(S["y_e_act"], E)
            pe.wait_ge(S["y_e_dve"], E)
            pe.wait_ge(S["texp_ready"], 1)
            n_over = pe.value_load(novi[0:1, 0:1].bitcast(i32), min_val=0, max_val=OV)
            with pe.Fori(0, OV) as i:
                with pe.If(i < n_over):
                    pe.wait_ge(S["o_gath"], 16 * i + 16)
                    xv = xg[0].rearrange("p (d k) -> p k d", k=KD)
                    for h in range(2):
                        for k in range(4):
                            last = tp(banks[h][:, k * P:(k + 1) * P], xv[:, 4 * h + k, :], P)
                    last.then_inc(S["o_xT_put"], 1)
                    pe.wait_ge(S["o_xT_kept"], i + 1)
                    pe.wait_ge(S["o_w"], 48 * i + 48)
                    for k in range(KD):
                        last = mm(banks[2][:, :], xgT[0][:, k, :], gu[0][:, k, :, :], start=(k == 0), stop=(k == KD - 1))
                    last.then_inc(S["o_g_put"], 1)
                    pe.wait_ge(S["o_hid"], i + 1)
                    hv = hdn[0].rearrange("p (d k) -> p k d", k=2)
                    for k in range(2):
                        last = tp(banks[4][:, k * P:(k + 1) * P], hv[:, k, :], P)
                    last.then_inc(S["o_hT_put"], 1)
                    pe.wait_ge(S["o_hT_kept"], i + 1)
                    for hf in range(2):
                        for k in range(2):
                            last = mm(banks[5 + hf][:, :], hT[0][:, k, :], dn[0][:, k, hf * 512:(hf + 1) * 512],
                                      start=(k == 0), stop=(k == 1))
                    last.then_inc(S["o_y_put"], 1)
                pe.nop()

        @block.scalar
        def _(act):
            def f(out_, in_, func, **kw):
                return nc.scalar.activation(out_, in_, func, **kw)

            for t in range(TT):
                act.wait_ge(S["xT_put"], 2 * t + 1)
                f(xT[:, 0:4, t * P:(t + 1) * P], banks[2 * t][:, :].rearrange("p (k x) -> p k x", k=4),
                  ACT.Copy).then_inc(S["xT_act"], 1)
            act.wait_ge(S["s5_loaded"], 48)
            f(ldt[:, 2:4], ldt[:, 0:2], ACT.Exp).then_inc(S["dt_ready"], 1)
            act.wait_ge(S["dar_ready"], 1)
            f(p_mg, p_dar, ACT.Exp)
            f(sm[:, 7, :], p_dar, ACT.Exp, scale=float(L)).then_inc(S["mag_ready"], 1)
            act.wait_ge(S["dar_ready"], 2)
            f(sm[:, 2, :], p_t1, ACT.Sin)
            f(sm[:, 3, :], sm[:, 1, :], ACT.Sin).then_inc(S["trig_ready"], 1)
            act.wait_ge(S["rows_kept"], 1)
            f(lnt[:, MR:2 * MR], lnt[:, 0:MR], ACT.Exp, scale=-1.0).then_inc(S["lru_exp"], 1)
            for c in (1, 3):
                act.wait_ge(S["bc_put"], c + 1)
                f((bT if c < 2 else cT)[:, 1].rearrange("p j q -> p (j q)"), banks[1 + c][:, :], ACT.Copy).then_inc(S["bc_kept"], 1)
            for n in range(2 * TT):
                hf, t = divmod(n, TT)
                act.wait_ge(S["u_put"], n + 1)
                f(usb[:, t, hf * 512:(hf + 1) * 512], banks[(5 + n) % 8][:, :], ACT.Copy).then_inc(S["u_kept"], 1)
            act.wait_ge(S["lru_c_ready"], 1)
            for b in range(NB):
                for s in range(2):
                    act.wait_ge(S["U_put"], 2 * b + s + 1)
                    f(U[:, 8 * s:8 * s + 8, :].rearrange("p g c -> p (g c)"), banks[4 + s][:, :], ACT.Copy).then_inc(S["U_kept"], 1)
                for m in range(ML):
                    ch = ML * b + m
                    act.wait_ge(S["xproj_put"], ML * b + m + 1)
                    need(act, "lru_done", ML * b)
                    f(xc[:, m, :], banks[m][:, :], ACT.Identity, scale=chan[:, 3 * MR + ch:3 * MR + ch + 1],
                      bias=chan[:, 4 * MR + ch:4 * MR + ch + 1]).then_inc(S["conv_begun"], 1)
                for j in range(4):
                    act.wait_ge(S["RT_put"], 4 * b + j + 1)
                    f(RT[:, 2 * j:2 * j + 2].rearrange("p q c x -> p (q c x)"), banks[4 + j][:, :], ACT.Copy).then_inc(S["RT_kept"], 1)
                for m in range(ML):
                    act.wait_ge(S["gproj_put"], ML * b + m + 1)
                    f(ylru[:, ML * b + m, :], banks[G_BANKS[m]][:, :], ACT.Gelu_apprx_tanh).then_inc(S["g_kept"], 1)
                for n in range(2 * ML):
                    g, m = divmod(n, ML)
                    ch = (5 + g) * MR + ML * b + m
                    act.wait_ge(S["gates_put"], 6 * b + n + 1)
                    f((rr, ii)[g][:, m, :], banks[LRU_BANKS[n]][:, :], ACT.Sigmoid, bias=chan[:, ch:ch + 1]).then_inc(S["gates_kept"], 1)
                act.drain()
                for m in range(ML):
                    ch = ML * b + m
                    f(aa[:, m, :], rr[:, m, :], ACT.Exp, scale=c_lru[:, ch:ch + 1])
                    f(th[:, m, :], rr[:, m, :], ACT.Tanh, scale=c_lru[:, MR + ch:MR + ch + 1]).then_inc(S["decay_ready"], 1)
                for m in range(ML):
                    act.wait_ge(S["mult2_ready"], ML * b + m + 1)
                    f(th[:, m, :], th[:, m, :], ACT.Sqrt).then_inc(S["mult_ready"], 1)
                act.wait_ge(S["k_stored"], 16 * (b + 1))
                for n in range(4):
                    j, h = divmod(n, 2)
                    act.wait_ge(S["Y_put"], 2 * b + j + 1)
                    f(Y2.rearrange("c l (j q h o) -> c j h q l o", j=2, q=4, h=2)[:, j, h],
                      banks[4 + 2 * h + j][0:NC, :].rearrange("c (q l o) -> c q l o", q=4, l=L),
                      ACT.Gelu_apprx_tanh).then_inc(S["Y_kept"], 1)
                for s in range(2):
                    act.wait_ge(S["yT_put"], 2 * b + s + 1)
                    f(ysT[:, 2 * b + s, :].rearrange("p (c l) -> p l c", l=L),
                      banks[4 + s][:, :].rearrange("p (l c) -> p l c", l=L), ACT.Copy).then_inc(S["yT_kept"], 1)
            for m in range(KD):
                need(act, "b_done", m - 1)
                for j in range(3):
                    act.wait_ge(S["b_val"], 5 * m + j + 1)
                    kw = {"bias": chan[:, 8 * MR + KD + m:8 * MR + KD + m + 1]} if j == 2 else {}
                    f(sg[m % 2][j], banks[(5 * m + j) % 8][:, :], ACT.Sigmoid, **kw).then_inc(S["b_sig"], 1)
            for t in range(TT):
                act.wait_ge(S["var_ready"], t + 1)
                f(stats[:, 4 * t + 2:4 * t + 3], stats[:, 4 * t + 1:4 * t + 2], ACT.Sqrt, bias=eps_t[:, 0:1]).then_inc(S["std_ready"], 1)
                if t == 0:
                    act.wait_ge(S["pT_put"], 1)
                    f(pT[:, 0, :], banks[6][:, :], ACT.Copy)
                    f(pT[:, 1, :], banks[7][:, :], ACT.Copy)
                    act.drain()
                    act.sem_inc(S["pT_kept"], 2)
            for t in range(TT):
                act.wait_ge(S["x1T_put"], t + 1)
                f(x1T[:, 0:4, t * P:(t + 1) * P], banks[4][:, :].rearrange("p (k x) -> p k x", k=4), ACT.Copy).then_inc(S["x1T_kept"], 1)
            act.wait_ge(S["router_put"], 1)
            f(score.rearrange("p t e -> p (t e)"), banks[6][:, 0:TT * E], ACT.Sigmoid).then_inc(S["score_ready"], 1)
            for t in range(TT):
                act.wait_ge(S["pg_biased"], 2 * t + 2)
                f(tmpd[t % 2], tmpd[t % 2], ACT.Sigmoid).then_inc(S["pg_sig"], 1)
            act.wait_ge(S["ple_done"], TT)
            for t in range(TT):
                act.wait_ge(S["sh_put"], t + 1)
                need(act, "sh_hid", t - 1)
                f(sil[t % 2], banks[4 + t % 2][:, 0:F], ACT.Silu).then_inc(S["sh_silu"], 1)
            def rows_kept(i, u):
                act.wait_ge(S["xT_e_put"], 4 * i + u + 1)
                f(xgT[u % 2][:, 0:4, :], banks[0][:, :].rearrange("p (k x) -> p k x", k=4), ACT.Copy).then_inc(S["xT_e_act"], 1)

            def store(i, u):
                act.wait_ge(S["y_e_act"], 4 * i + u + 1)
                act.wait_ge(S["y_e_dve"], 4 * i + u + 1)
                act.dma_start(y_dram[bass.ds((4 * i + u) * P, P), :], yb[u % 2]).then_inc(s_ys[u % 2], 16)

            def expert(i, u, more=True):
                static = isinstance(i, int)
                if not static or u >= 2:
                    store(i, u - 2)
                act.wait_ge(S["g_e_put"], 4 * i + u + 1)
                wait(act, S["hid_e"], 4 * i + u - 1)
                f(sil[u % 2], banks[2 + u % 2][:, 0:F], ACT.Silu).then_inc(S["silu_e"], 1)
                if more:
                    rows_kept(i, u + 1)
                if not static or u >= 1:
                    wait(act, s_ys[(u - 1) % 2], 32 * i + 16 * ((u - 1) // 2))
                    act.wait_ge(S["y_e_put"], 4 * i + u)
                    f(yb[(u - 1) % 2][:, 0:512], banks[5][:, :], ACT.Copy).then_inc(S["y_e_act"], 1)

            rows_kept(0, 0)
            for u in range(0, 5):
                expert(0, u)
            with act.Fori(1, E // 4 - 1) as i:
                for u in range(1, 5):
                    expert(i, u)
            for n in range(E - 3, E):
                expert(0, n, more=n + 1 < E)
            store(0, E - 2)
            act.wait_ge(s_ys[(E - 1) % 2], 16 * (E // 2 - 1))
            act.wait_ge(S["y_e_put"], E)
            f(yb[(E - 1) % 2][:, 0:512], banks[5][:, :], ACT.Copy).then_inc(S["y_e_act"], 1)
            store(0, E - 1)
            for u in range(2):
                act.wait_ge(s_ys[u], 16 * E // 2)
            act.wait_ge(S["texp_ready"], 1)
            n_over = act.value_load(novi[0:1, 0:1].bitcast(i32), min_val=0, max_val=OV)
            with act.Fori(0, OV) as i:
                with act.If(i < n_over):
                    act.wait_ge(S["o_xT_put"], i + 1)
                    f(xgT[0][:, 0:4, :], banks[0][:, :].rearrange("p (k x) -> p k x", k=4), ACT.Copy).then_inc(S["o_xT_act"], 1)
                    act.wait_ge(S["o_g_put"], i + 1)
                    f(sil[0], banks[2][:, 0:F], ACT.Silu).then_inc(S["o_silu"], 1)
                act.nop()
            for t in range(TT):
                act.wait_ge(S["var_ready"], TT + t + 1)
                f(stats[:, 4 * t + 2:4 * t + 3], stats[:, 4 * t + 1:4 * t + 2], ACT.Sqrt, bias=eps_t[:, 0:1]).then_inc(S["std_ready"], 1)

        @block.vector
        def _(dve):
            V_ = nc.vector

            def d():
                dve.drain()

            def tt(out_, a, b_, op):
                return V_.tensor_tensor(out_, a, b_, op)

            def ts(out_, a, s1, s2, op0, op1=ALU.bypass):
                return V_.tensor_scalar(out_, a, s1, s2, op0, op1)

            def stt(out_, a, s, b_, op0, op1):
                return V_.scalar_tensor_tensor(out_, a, s, b_, op0, op1)

            for t in range(TT):
                dve.wait_ge(S["xT_put"], 2 * t + 2)
                V_.tensor_copy(xT[:, 4:8, t * P:(t + 1) * P],
                               banks[2 * t + 1][:, :].rearrange("p (k x) -> p k x", k=4)).then_inc(S["xT_dve"], 1)
            dve.wait_ge(S["dt_ready"], 1)
            for h in range(2):
                hs = slice(h * NS, (h + 1) * NS)
                ts(p_dar[:, hs], p_are[:, hs], ldt[:, 2 + h:3 + h], None, ALU.mult)
                ts(p_ph[:, hs], p_aim[:, hs], ldt[:, 2 + h:3 + h], None, ALU.mult)
            d()
            dve.sem_inc(S["dar_ready"], 1)
            ts(p_t0, p_ph, 1.0 / TWO_PI, MAGIC, ALU.mult, ALU.add)
            d()
            ts(p_t0, p_t0, -MAGIC, None, ALU.add)
            d()
            stt(p_t1, p_t0, -C1, p_ph, ALU.mult, ALU.add)
            d()
            stt(p_t1, p_t0, -C2, p_t1, ALU.mult, ALU.add)
            d()
            stt(p_t1, p_t0, -C3, p_t1, ALU.mult, ALU.add)
            d()
            ts(p_t1, p_t1, PI_IN, -PI_IN, ALU.min, ALU.max)
            d()
            stt(sm[:, 1, :], p_t1, -1.0, p_t1, ALU.mult, ALU.max)
            d()
            ts(sm[:, 1, :], sm[:, 1, :], -1.0, math.pi / 2, ALU.mult, ALU.add).then_inc(S["dar_ready"], 1)
            dve.wait_ge(S["rows_put"], 1)
            V_.tensor_copy(chan, banks[0][:, 0:112])
            V_.tensor_copy(dT, banks[0][0:GP, P:P + G])
            d()
            lam = chan[:, 7 * MR:8 * MR]
            stt(lnt[:, 0:MR], lam, -1.0, lam, ALU.mult, ALU.max)
            d()
            dve.sem_inc(S["rows_kept"], 1)
            ex, w1, w2, w3, w4 = (lnt[:, n * MR:(n + 1) * MR] for n in (1, 2, 3, 4, 5))
            dve.wait_ge(S["lru_exp"], 1)
            ts(w1, ex, 2.0, None, ALU.add)
            d()
            V_.reciprocal(w2, w1)
            d()
            tt(w1, ex, w2, ALU.mult)
            d()
            tt(w2, w1, w1, ALU.mult)
            V_.memset(w3, 1.0 / 17)
            d()
            for n in range(15, 0, -2):
                tt(w3, w3, w2, ALU.mult)
                d()
                ts(w3, w3, 1.0 / n, None, ALU.add)
                d()
            stt(w3, w3, 2.0, w1, ALU.mult, ALU.mult)
            ts(w4, lam, -1.0, 0.0, ALU.mult, ALU.max)
            d()
            tt(w3, w3, w4, ALU.add)
            d()
            ts(c_lru[:, 0:MR], w3, -8.0, None, ALU.mult)
            ts(c_lru[:, MR:2 * MR], w3, 8.0, None, ALU.mult).then_inc(S["lru_c_ready"], 1)
            for c in (0, 2):
                dve.wait_ge(S["bc_put"], c + 1)
                V_.tensor_copy((bT if c < 2 else cT)[:, 0].rearrange("p j q -> p (j q)"), banks[1 + c][:, :]).then_inc(S["bc_kept"], 1)
            dve.wait_ge(S["bc_kept"], 4)
            dve.wait_ge(S["mag_ready"], 1)
            dve.wait_ge(S["trig_ready"], 1)
            sin, cos = sm[:, 2, :], sm[:, 3, :]
            tt(pr[:, 1, 0, :], p_mg, cos, ALU.mult)
            tt(pr[:, 1, 1, :], p_mg, sin, ALU.mult)
            tt(sm[:, 5, :], p_are, p_are, ALU.mult)
            tt(sm[:, 6, :], p_aim, p_aim, ALU.mult)
            d()
            ts(sm[:, 4, :], pr[:, 1, 0, :], -1.0, None, ALU.add)
            tt(sm[:, 5, :], sm[:, 5, :], sm[:, 6, :], ALU.add)
            d()
            V_.reciprocal(sm[:, 6, :], sm[:, 5, :])
            tt(sm[:, 8, :], sm[:, 4, :], p_are, ALU.mult)
            tt(sm[:, 9, :], pr[:, 1, 1, :], p_aim, ALU.mult)
            tt(sm[:, 10, :], pr[:, 1, 1, :], p_are, ALU.mult)
            tt(sm[:, 11, :], sm[:, 4, :], p_aim, ALU.mult)
            d()
            tt(sm[:, 8, :], sm[:, 8, :], sm[:, 9, :], ALU.add)
            tt(sm[:, 10, :], sm[:, 10, :], sm[:, 11, :], ALU.subtract)
            d()
            tt(sm[:, 8, :], sm[:, 8, :], sm[:, 6, :], ALU.mult)
            tt(sm[:, 10, :], sm[:, 10, :], sm[:, 6, :], ALU.mult)
            for _ in range(3):
                tt(sm[:, 0, :], cos, cos, ALU.mult)
                tt(sm[:, 1, :], sin, sin, ALU.mult)
                tt(sm[:, 4, :], cos, sin, ALU.mult)
                d()
                tt(cos, sm[:, 0, :], sm[:, 1, :], ALU.subtract)
                ts(sin, sm[:, 4, :], 2.0, None, ALU.mult)
                d()
            for n in (1, 2, 4):
                src, one = pr[:, 1:n + 1], pr[:, n]
                x, y = (tA[0:NQ, k * 512:k * 512 + n * P].rearrange("q (j x) -> q j x", j=n) for k in range(2))
                cr, ci = bc(one[:, 0, :], 1, n), bc(one[:, 1, :], 1, n)
                dst = pr[:, n + 1:2 * n + 1]
                for c, (f0, f1, op) in enumerate(((cr, ci, ALU.subtract), (ci, cr, ALU.add))):
                    tt(pq0[:, 0:n], src[:, :, 0, :], f0, ALU.mult)
                    tt(pq1[:, 0:n], src[:, :, 1, :], f1, ALU.mult)
                    d()
                    tt(dst[:, :, c, :], pq0[:, 0:n], pq1[:, 0:n], op)
                    d()
            dve.sem_inc(S["powers_ready"], 1)
            dve.wait_ge(S["powers_put"], 1)
            V_.tensor_copy(pw[:, 1:L + 1].rearrange("p j c q -> p (j c q)"), banks[5][:, :])
            V_.tensor_copy(misc.rearrange("p v q -> p (v q)"), banks[6][:, 0:5 * NQ])
            V_.memset(pw[:, 0, 0, :], 1.0)
            V_.memset(pw[:, 0, 1, :], 0.0)
            d()
            dve.sem_inc(S["powers_kept"], 1)
            zr, zi = bc(misc[:, 0, :], 1, GP), bc(misc[:, 1, :], 1, GP)
            w = [at(tmp_off + n * 512, 512).rearrange("p (j q) -> p j q", j=GP) for n in range(4)]
            tt(w[0], bT[:, 0], zr, ALU.mult)
            tt(w[1], bT[:, 1], zi, ALU.mult)
            tt(w[2], bT[:, 1], zr, ALU.mult)
            tt(w[3], bT[:, 0], zi, ALU.mult)
            d()
            tt(bT[:, 0], w[0], w[1], ALU.subtract)
            tt(bT[:, 1], w[2], w[3], ALU.add)
            d()

            def tables(b):
                qs = slice(b * QB, (b + 1) * QB)
                need(dve, "k_stored", 16 * b)
                if b == 0:
                    dve.wait_ge(S["xT_put"], 2 * TT)
                    dve.wait_ge(S["u_stored"], 16)
                shp = [P, QB, L, GP]
                for c in range(2):
                    for q in range(QB):
                        pass
                x, y = (tm.rearrange("p (q j o) -> p q j o", q=QB, j=L + 1) for tm in (tA, tB))
                x8, y8 = (at(o, QB * P).rearrange("p (q l o) -> p q l o", q=QB, l=L) for o in (tmp_off, tmp_off + tq))
                Rv = R.rearrange("p c q (l o) -> p c q l o", l=L)
                bb = [bT[:, c, :, qs].rearrange("p o q -> p q o") for c in range(2)]
                for c, (c0, c1, op) in enumerate(((0, 1, ALU.subtract), (1, 0, ALU.add))):
                    for l in range(L):
                        pv = [bc(pw[:, L - 1 - l, k, qs], 2, GP) for k in range(2)]
                        tt(x8[:, :, l, :], bb[0], pv[c0], ALU.mult)
                        tt(y8[:, :, l, :], bb[1], pv[c1], ALU.mult)
                    d()
                    ins = tt(Rv[:, c], x8, y8, op)
                    d()
                ins = None
                dve.sem_inc(S["R_ready"], 1)
                need(dve, "Y_put", 2 * b)
                cc = [cT[:, c, :, qs].rearrange("p o q -> p q o") for c in range(2)]
                for c in range(2):
                    for j in range(L + 1):
                        pv = [bc(pw[:, j, k, qs], 2, GP) for k in range(2)]
                        tt(x[:, :, j, :], cc[0], pv[c], ALU.mult)
                        tt(y[:, :, j, :], cc[1], pv[1 - c], ALU.mult)
                    d()
                    if c == 0:
                        tt(Q[:, 0], x, y, ALU.subtract)
                    else:
                        stt(Q[:, 1].rearrange("p q j o -> p (q j o)"), tA, -1.0, tB, ALU.mult, ALU.subtract)
                    d()
                dve.sem_inc(S["Q_ready"], 1)
                V_.memset(Et[:, 0, :, 0:1], 1.0)
                V_.memset(Et[:, 1, :, 0:1], 0.0)
                V_.tensor_copy(V[:, 0, :], misc[:, 3, qs])
                V_.tensor_copy(V[:, 1, :], misc[:, 4, qs])
                V_.tensor_copy(mag, bc(misc[:, 2, qs], 2, NC))
                d()
                V_.memset(mag[:, :, 0:1], 0.0)
                n = 1
                while n < NC:
                    vr, vi = bc(V[:, 0, :], 2, n), bc(V[:, 1, :], 2, n)
                    a0, a1, a2, a3 = (t5[k][:, :, 0:n] for k in range(4))
                    tt(a0, Et[:, 0, :, 0:n], vr, ALU.mult)
                    tt(a1, Et[:, 1, :, 0:n], vi, ALU.mult)
                    tt(a2, Et[:, 0, :, 0:n], vi, ALU.mult)
                    tt(a3, Et[:, 1, :, 0:n], vr, ALU.mult)
                    if 2 * n < NC:
                        tt(V[:, 2, :], V[:, 0, :], V[:, 1, :], ALU.mult)
                        tt(V[:, 3, :], V[:, 1, :], V[:, 1, :], ALU.mult)
                    d()
                    tt(Et[:, 0, :, n:2 * n], a0, a1, ALU.subtract)
                    tt(Et[:, 1, :, n:2 * n], a2, a3, ALU.add)
                    if 2 * n < NC:
                        tt(V[:, 0, :], V[:, 0, :], V[:, 0, :], ALU.mult)
                        ts(V[:, 1, :], V[:, 2, :], 2.0, None, ALU.mult)
                        d()
                        tt(V[:, 0, :], V[:, 0, :], V[:, 3, :], ALU.subtract)
                    d()
                    n *= 2
                V_.memset(hp[:, :, :, 0:1].rearrange("p c q o -> p (c q) o"), 0.0)
                d()

            tables(0)
            for b in range(NB):
                for m in range(ML):
                    ch = ML * b + m
                    dve.wait_ge(S["conv_begun"], ch + 1)
                    for s in range(1, 4):
                        wc = (3 - s) * MR + ch
                        ins = stt(xc[:, m, s:], banks[m][:, 0:T - s], chan[:, wc:wc + 1], xc[:, m, s:], ALU.mult, ALU.add)
                        if s < 3:
                            d()
                    ins.then_inc(S["conv_done"], 1)
                dve.wait_ge(S["RT_put"], 4 * (b + 1))
                dve.wait_ge(S["U_put"], 2 * (b + 1))
                V_.memset(Kp[:, :, 0:(L - 1) * GP], 0.0)
                tt(dI, bc(ident[0:GP, 0:GP], 1, GB), bc(dT[:, b * GB:(b + 1) * GB], 2, GP), ALU.mult)
                for n in range(4):
                    j, h = divmod(n, 2)
                    dve.wait_ge(S["K_put"], 2 * b + j + 1)
                    V_.tensor_copy(Kp.rearrange("p (j q h) x -> p j q h x", q=4, h=2)[:, j, :, h, (L - 1) * GP:],
                                   banks[4 + 2 * h + j][0:GP, :].rearrange("p (q x) -> p q x", q=4))
                d()
                tt(Kp[:, :, (L - 1) * GP:L * GP], Kp[:, :, (L - 1) * GP:L * GP], dI, ALU.add).then_inc(S["K_ready"], 1)
                dve.wait_ge(S["S_put"], b + 1)
                sr, si = (banks[4 + c][:, :].rearrange("p (q n) -> p q n", q=QB) for c in range(2))
                er, ei = Et[:, 0], Et[:, 1]
                a0, a1, a2, a3 = t5
                tt(a0, er, sr, ALU.mult)
                tt(a1, ei, si, ALU.mult)
                tt(a2, er, si, ALU.mult)
                tt(a3, ei, sr, ALU.mult)
                d()
                tt(a0, a0, a1, ALU.add)
                tt(a2, a2, a3, ALU.subtract)
                d()
                flat = [v.rearrange("p q n -> p (q n)") for v in (mag, a0, a1, a2, a3)]
                V_.tensor_tensor_scan(flat[2], flat[0], flat[1], 0.0, ALU.mult, ALU.add)
                V_.tensor_tensor_scan(flat[4], flat[0], flat[3], 0.0, ALU.mult, ALU.add)
                d()
                hr, hi = hp[:, 0, :, 1:NC + 1], hp[:, 1, :, 1:NC + 1]
                tt(a0, er, a1, ALU.mult)
                tt(a2, ei, a3, ALU.mult)
                d()
                tt(hr, a0, a2, ALU.subtract)
                d()
                tt(a0, er, a3, ALU.mult)
                tt(a2, ei, a1, ALU.mult)
                d()
                tt(hi, a0, a2, ALU.add).then_inc(S["h_ready"], 1)
                for m in range(ML):
                    ch = ML * b + m
                    dve.wait_ge(S["square_ready"], ch + 1)
                    stt(th[:, m], rr[:, m], 1.0, th[:, m], ALU.add, ALU.mult).then_inc(S["mult2_ready"], 1)
                for m in range(ML):
                    ch = ML * b + m
                    dve.wait_ge(S["mult_ready"], ch + 1)
                    dve.wait_ge(S["ix_ready"], ch + 1)
                    V_.memset(th[:, m, 0:1], 1.0)
                    d()
                    tt(ii[:, m], ii[:, m], th[:, m], ALU.mult)
                    d()
                    V_.tensor_tensor_scan(rr[:, m], aa[:, m], ii[:, m], 0.0, ALU.mult, ALU.add)
                    d()
                    dve.wait_ge(S["g_kept"], ch + 1)
                    tt(ylru[:, ch], ylru[:, ch], rr[:, m], ALU.mult).then_inc(S["lru_done"], 1)
                if b + 1 < NB:
                    tables(b + 1)
            for m in range(KD):
                s = sg[m % 2]
                dve.wait_ge(S["b_sig"], 3 * m + 3)
                dve.wait_ge(S["b_val"], 5 * m + 4)
                stt(s[3], banks[(5 * m + 3) % 8][:, :], chan[:, 8 * MR + m:8 * MR + m + 1], s[2], ALU.add, ALU.mult)
                dve.wait_ge(S["b_val"], 5 * m + 5)
                tt(s[4], banks[(5 * m + 4) % 8][:, :], s[0], ALU.mult)
                d()
                tt(s[3], s[3], s[1], ALU.mult)
                d()
                tt(merged[:, m], s[3], s[4], ALU.add).then_inc(S["b_done"], 1)

            def norm(v, t, gb, n):
                bs = lnt[:, 0:12].rearrange("p (h x) -> p h x", h=2)
                for h in range(2):
                    V_.bn_stats(bs[:, h, :], v[:, h * 512:(h + 1) * 512])
                d()
                V_.bn_aggr(stats[:, 4 * t:4 * t + 2], lnt[:, 0:12]).then_inc(S["var_ready"], 1)
                dve.wait_ge(S["std_ready"], n)
                V_.reciprocal(stats[:, 4 * t + 3:4 * t + 4], stats[:, 4 * t + 2:4 * t + 3])
                d()
                ts(v, v, stats[:, 4 * t:4 * t + 1], stats[:, 4 * t + 3:4 * t + 4], ALU.subtract, ALU.mult)
                d()
                tt(v, v, lnp[:, gb, :], ALU.mult)
                d()
                return tt(v, v, lnp[:, gb + 1, :], ALU.add)

            dve.wait_ge(S["xtok_loaded"], 16)
            dve.wait_ge(S["lnp_loaded"], 16 * 6)
            for t in range(TT):
                for hf in range(2):
                    n = 2 * t + hf
                    hs = slice(hf * 512, (hf + 1) * 512)
                    dve.wait_ge(S["res_put"], n + 1)
                    stt(x1[:, t, hs], xtok[:, t, hs], ALPHA, banks[n % 4][:, :], ALU.mult, ALU.add).then_inc(S["res_added"], 1)
                d()
                norm(x1[:, t, :], t, 0, t + 1).then_inc(S["x1_ready"], 1)
            for t in range(TT):
                dve.wait_ge(S["x1T_put"], t + 1)
                V_.tensor_copy(x1T[:, 4:8, t * P:(t + 1) * P],
                               banks[5][:, :].rearrange("p (k x) -> p k x", k=4)).then_inc(S["x1T_kept"], 1)
            dve.wait_ge(S["score_ready"], 1)
            dve.wait_ge(S["const_ready"], 2)
            tt(biased, score, bc(rbias, 1, TT), ALU.add)
            d()
            for t in range(TT):
                for g in range(EG):
                    V_.max(gtop[:, t * EG + g, :], biased[:, t, g * 8:(g + 1) * 8])
            d()
            tt(gsum.rearrange("p t g -> p (t g)").unsqueeze(2), gtop[:, :, 0:1], gtop[:, :, 1:2], ALU.add)
            d()
            for t in range(TT):
                mine, other = bc(gsum[:, t, :], 2, EG), bc(gsum[:, t, :], 1, EG)
                tt(pair[:, t], other, mine, ALU.is_gt)
                tt(pair2[:, t], other, mine, ALU.is_equal)
            d()
            tt(pair2, pair2, bc(lt, 1, TT), ALU.mult)
            d()
            tt(pair, pair, pair2, ALU.add)
            d()
            V_.tensor_reduce(gsel, pair, AX, ALU.add)
            d()
            ts(gsel, gsel, TOPG - 0.5, None, ALU.is_lt)
            d()
            gb_ = bc(gsel, 3, 8).rearrange("p t g x -> p (t g) x")
            m8 = lambda v: v.rearrange("p t (g x) -> p (t g) x", g=EG)
            tt(m8(biased), m8(biased), gb_, ALU.mult)
            ts(gsum, gsel, BIG, -BIG, ALU.mult, ALU.add)
            d()
            tt(m8(biased), m8(biased), bc(gsum, 3, 8).rearrange("p t g x -> p (t g) x"), ALU.add)
            d()
            for t in range(TT):
                V_.max(top8[:, t, :], biased[:, t, :])
            d()
            for t in range(TT):
                V_.match_replace(repl[:, t, :], top8[:, t, :], biased[:, t, :], -3 * BIG)
                V_.max_index(idx8[:, t, :].bitcast(u32), top8[:, t, :], biased[:, t, :])
            d()
            ts(mask, repl, -2 * BIG, None, ALU.is_lt)
            V_.tensor_copy(idx8f, idx8.bitcast(u32))
            d()
            dve.sem_inc(S["mask_ready"], 1)

            def ple(t):
                v = tmpd[t % 2]
                for hf in range(2):
                    hs = slice(hf * 512, (hf + 1) * 512)
                    dve.wait_ge(S["ple_put"], 3 * t + hf + 1)
                    tt(v[:, hs], banks[hf][:, :], lnp[:, 4, hs], ALU.add).then_inc(S["pg_biased"], 1)
                dve.wait_ge(S["pg_sig"], t + 1)
                dve.wait_ge(S["ple_put"], 3 * t + 3)
                for hf in range(2):
                    hs = slice(hf * 512, (hf + 1) * 512)
                    tt(v[:, hs], v[:, hs], banks[2 + hf][:, :], ALU.mult)
                d()
                stt(acc[:, t, :], x1[:, t, :], ALPHA, v, ALU.mult, ALU.add).then_inc(S["ple_done"], 1)

            ple(0)
            ple(1)
            dve.wait_ge(S["rank_put"], 1)
            ranks = banks[7][:, 0:TT * E].rearrange("p (t e) -> p t e", t=TT)
            V_.tensor_copy(row, ranks)
            V_.tensor_copy(cnt, banks[7][:, TT * E:(TT + 1) * E])
            d()
            ts(ovc, cnt, P + 0.5, None, ALU.is_gt)
            ts(ovi, cnt, 2 * P + 0.5, None, ALU.is_gt)
            ts(cbase, cnt, 3 * P + 0.5, None, ALU.is_gt)
            ts(repl, row, P - 0.5, None, ALU.is_gt)
            d()
            tt(ovc, ovc, ovi, ALU.add)
            d()
            tt(ovc, ovc, cbase, ALU.add)
            d()
            V_.tensor_tensor_scan(ovi, ones_e, ovc, 0.0, ALU.mult, ALU.add)
            d()
            tt(cbase, ovi, ovc, ALU.subtract)
            V_.tensor_copy(novi.bitcast(i32), ovi[:, E - 1:E])
            tt(texw, bc(ovi[0:1, :], 1, 32), bc(iota_i[0:1, :], 2, E), ALU.is_le)
            d()
            ts(cbase, cbase, float(P), float((E - 1) * P), ALU.mult, ALU.add)
            V_.tensor_reduce(texpf[0:1, :], texw, AX, ALU.add)
            d()
            tt(cbase, cbase, e128, ALU.subtract)
            ts(texpf[0:1, :], texpf[0:1, :], float(E - 1), None, ALU.min)
            d()
            tt(repl, repl, bc(cbase, 1, TT), ALU.mult)
            V_.tensor_copy(texpi[0:1, :].bitcast(i32), texpf[0:1, :])
            tt(row, row, bc(e128, 1, TT), ALU.add)
            d()
            dve.sem_inc(S["texp_ready"], 1)
            tt(row, row, repl, ALU.add)
            for t in range(TT):
                tt(eqt[:, t], bc(iota_e, 1, K), bc(idx8f[:, t, :], 2, E), ALU.is_equal)
            d()
            for t in range(TT):
                tt(eqp[:, t], eqt[:, t], bc(row[:, t, :], 1, K), ALU.mult)
            d()
            V_.tensor_reduce(slotf, eqp, AX, ALU.add)
            d()
            V_.tensor_copy(sloti.bitcast(i32), slotf)
            for t in range(TT):
                tt(eqp[:, t], eqt[:, t], bc(score[:, t, :], 1, K), ALU.mult)
            d()
            dve.sem_inc(S["slot_ready"], 1)
            V_.tensor_reduce(gate, eqp, AX, ALU.add)
            d()
            V_.tensor_reduce(gsc, gate, AX, ALU.add)
            d()
            V_.reciprocal(gsc, gsc)
            d()
            for t in range(TT):
                ts(gate[:, t, :], gate[:, t, :], gsc[:, t:t + 1], SCALE, ALU.mult, ALU.mult)
            d()
            ple(2)
            ple(3)
            for t in range(TT + 1):
                if t < TT:
                    dve.wait_ge(S["sh_silu"], t + 1)
                    if t >= 2:
                        dve.wait_ge(S["sh_hT_put"], t - 1)
                    tt(hdn[t % 2], sil[t % 2], banks[4 + t % 2][:, F:2 * F], ALU.mult).then_inc(S["sh_hid"], 1)
                if t:
                    s = t - 1
                    dve.wait_ge(S["sh_hT_put"], s + 1)
                    V_.tensor_copy(hT[s % 2], banks[0][:, 0:F].rearrange("p (k x) -> p k x", k=2)).then_inc(S["sh_hT"], 1)
                    dve.wait_ge(S["sh_y_put"], s + 1)
                    for hf in range(2):
                        hs = slice(hf * 512, (hf + 1) * 512)
                        ins = tt(acc[:, s, hs], acc[:, s, hs], banks[6 + hf][:, :], ALU.add)
                    ins.then_inc(S["sh_done"], 1)
            dve.wait_ge(S["tokT_put"], 1)
            V_.tensor_copy(idxT.bitcast(i32), banks[1][:, 0:NT]).then_inc(S["idx_ready"], 1)

            def rows_kept(i, u):
                dve.wait_ge(S["xT_e_put"], 4 * i + u + 1)
                V_.tensor_copy(xgT[u % 2][:, 4:8, :], banks[1][:, :].rearrange("p (k x) -> p k x", k=4)).then_inc(S["xT_e_dve"], 1)

            def y_kept(i, u):
                wait(dve, s_ys[u % 2], 32 * i + 16 * (u // 2))
                dve.wait_ge(S["y_e_put"], 4 * i + u + 1)
                V_.tensor_copy(yb[u % 2][:, 512:1024], banks[6][:, :]).then_inc(S["y_e_dve"], 1)

            def expert(i, u, more=True):
                dve.wait_ge(S["silu_e"], 4 * i + u + 1)
                tt(hdn[u % 2], sil[u % 2], banks[2 + u % 2][:, F:2 * F], ALU.mult).then_inc(S["hid_e"], 1)
                if more:
                    rows_kept(i, u + 1)
                if not isinstance(i, int) or u >= 1:
                    y_kept(i, u - 1)
                dve.wait_ge(S["hT_e_put"], 4 * i + u + 1)
                V_.tensor_copy(hT[u % 2], banks[4][:, 0:F].rearrange("p (k x) -> p k x", k=2)).then_inc(S["hT_e_kept"], 1)

            rows_kept(0, 0)
            for u in range(0, 5):
                expert(0, u)
            with dve.Fori(1, E // 4 - 1) as i:
                for u in range(1, 5):
                    expert(i, u)
            for n in range(E - 3, E):
                expert(0, n, more=n + 1 < E)
            y_kept(0, E - 1)
            dve.wait_ge(s_ys[0], 16 * E // 2)
            dve.sem_inc(S["o_y_kept"], 1)
            n_over = dve.value_load(novi[0:1, 0:1].bitcast(i32), min_val=0, max_val=OV)
            with dve.Fori(0, OV) as i:
                with dve.If(i < n_over):
                    dve.wait_ge(S["o_xT_act"], i + 1)
                    V_.tensor_copy(xgT[0][:, 4:8, :], banks[1][:, :].rearrange("p (k x) -> p k x", k=4)).then_inc(S["o_xT_kept"], 1)
                    dve.wait_ge(S["o_silu"], i + 1)
                    tt(hdn[0], sil[0], banks[2][:, F:2 * F], ALU.mult).then_inc(S["o_hid"], 1)
                    dve.wait_ge(S["o_hT_put"], i + 1)
                    V_.tensor_copy(hT[0], banks[4][:, 0:F].rearrange("p (k x) -> p k x", k=2)).then_inc(S["o_hT_kept"], 1)
                    dve.wait_ge(S["o_y_put"], i + 1)
                    V_.tensor_copy(yb[0][:, 0:512], banks[5][:, :])
                    V_.tensor_copy(yb[0][:, 512:1024], banks[6][:, :])
                    d()
                    dve.sem_inc(S["o_y_kept"], 1)
                dve.nop()
            for t in range(TT):
                for k in range(K):
                    n = t * K + k
                    dve.wait_ge(s_yg[k], 16 * (t + 1))
                    stt(acc[:, t, :], yg[k], gate[:, t, k:k + 1], acc[:, t, :], ALU.mult, ALU.add).then_inc(S["acc_added"], 1)
                    d()
                norm(acc[:, t, :], t, 2, TT + t + 1).then_inc(S["out_ready"], 1)


def kernel(**inputs):
    import numpy as np
    import concourse.bacc as bacc
    from concourse.bass_utils import run_bass_kernel_spmd

    nc = bacc.Bacc("TRN2", target_bir_lowering=False, num_devices=1)
    arrays, args = {}, {}
    for name in INPUTS:
        a = np.ascontiguousarray(inputs[name])
        arrays[name + "_in"] = a
        args[name] = nc.dram_tensor(name + "_in", a.shape, mybir.dt.from_np(a.dtype), kind="ExternalInput").ap()
    out = nc.dram_tensor("out_dram", (1, T, D), mybir.dt.float32, kind="ExternalOutput").ap()
    decoder_layer(nc, args, out)
    r = run_bass_kernel_spmd(nc, [arrays], core_ids=[0])
    return r.results[0]["out_dram"]
```

```python
import concourse.bass as bass
from concourse import mybir
from contextlib import ExitStack
import math

P = 128
T = 512
TT = T // P
D = 1024
KD = D // P
D_RNN = 1536
MR = D_RNN // P
NB = 4
ML = MR // NB
CB = ML * P
HD = 96
G = 64
GP = 16
NS = 64
L = 8
NC = T // L
NQ = G // 2
QB = NQ // NB
GB = G // NB
E = 64
EG = 8
TOPG = 4
K = 8
F = 256
ALPHA = 2.0 ** 0.25
EPS = 1e-5
SCALE = 2.5
SL = 96
OV = (T * K - E) // SL
NT = E + OV
LEVELS = (T - 1) // SL
BIG = 1e30
TWO_PI = 2 * math.pi
MAGIC = 12582912.0
C1 = 6.28125
C2 = round((TWO_PI - C1) * 2 ** 21) / 2 ** 21
C3 = TWO_PI - C1 - C2
PI_IN = 3.1415925


INPUTS = ["x", "p", "w_in", "conv_w", "conv_b", "lru_wa", "lru_ba", "lru_wx", "lru_bx", "lru_lambda",
          "w_lru_out", "s5_a_re", "s5_a_im", "s5_b_re", "s5_b_im", "s5_c_re", "s5_c_im", "s5_d",
          "s5_log_dt", "w_glu", "b_glu", "w_out", "ln1_g", "ln1_b", "router_w", "router_bias",
          "moe_w_gate", "moe_w_up", "moe_w_down", "shared_w_gate", "shared_w_up", "shared_w_down",
          "ple_w", "ple_gate_w", "ple_gate_b", "ln2_g", "ln2_b"]


def decoder_layer(nc, A, out):
    f32 = mybir.dt.float32
    i32 = mybir.dt.int32
    u32 = mybir.dt.uint32
    ALU = mybir.AluOpType
    ACT = mybir.ActivationFunctionType
    AX = mybir.AxisListType.X

    ctx = ExitStack()
    with ctx:
        COLS = 52600
        arena = ctx.enter_context(nc.sbuf_tensor("arena", [P, COLS], f32))
        banks = [ctx.enter_context(nc.psum_tensor(f"bank{i}", [P, 512], f32)) for i in range(8)]

        def dram(name, shape, dt=f32):
            return nc.dram_tensor(name, shape, dt, kind="Internal").ap()

        u_dram = dram("u_dram", (T, D))
        k_dram = dram("k_dram", (NB, GB, GP, (2 * L - 1) * GP))
        x1_dram = dram("x1_dram", (T + SL, D))
        acc_dram = dram("acc_dram", (T + SL, D))
        slot_dram = dram("slot_dram", (NT * SL, 2))

        def sem(name):
            return ctx.enter_context(nc.semaphore(name))

        top = [0]

        def at(off, cols, parts=P):
            assert off + cols <= COLS, (off, cols)
            return arena[0:parts, off:off + cols]

        def new(cols, parts=P):
            off = top[0]
            top[0] += cols
            return at(off, cols, parts)

        ident = new(P)
        ones = new(P)
        strict = new(P)
        chan = new(112)
        c_lru = new(2 * MR)
        lnt = new(8 * MR)
        eps_t = new(8)
        xT = new(KD * T).rearrange("p (k t) -> p k t", k=KD)

        base_a = top[0]
        ylru_off = top[0]
        ylru = new(MR * T).rearrange("p (m t) -> p m t", m=MR)
        ysT = new(KD * T).rearrange("p (m t) -> p m t", m=KD)
        wx = new(KD * CB).rearrange("p (k c) -> p k c", k=KD)
        wg = new(KD * CB).rearrange("p (k c) -> p k c", k=KD)
        bd = new(2 * ML * CB).rearrange("p (g k c) -> p g k c", g=2, k=ML)
        lru_off = top[0]
        xc = new(ML * T).rearrange("p (m t) -> p m t", m=ML)
        rr = new(ML * T).rearrange("p (m t) -> p m t", m=ML)
        ii = new(ML * T).rearrange("p (m t) -> p m t", m=ML)
        aa = new(ML * T).rearrange("p (m t) -> p m t", m=ML)
        th = new(ML * T).rearrange("p (m t) -> p m t", m=ML)
        bT = new(2 * GP * NQ).rearrange("p (c j q) -> p c j q", c=2, j=GP)
        cT = new(2 * GP * NQ).rearrange("p (c j q) -> p c j q", c=2, j=GP)
        pw = new((L + 1) * 2 * NQ).rearrange("p (j c q) -> p j c q", j=L + 1, c=2)
        misc = new(5 * NQ).rearrange("p (v q) -> p v q", v=5)
        dT = new(G, GP)
        dI = new(GB * GP, GP).rearrange("p (g j) -> p g j", g=GB)
        qc_off = top[0]
        Q = new(2 * QB * (L + 1) * GP).rearrange("p (c q j o) -> p c q j o", c=2, q=QB, j=L + 1)
        r_off = top[0]
        R = new(2 * QB * P).rearrange("p (c q x) -> p c q x", c=2, q=QB)
        uy_off = top[0]
        U2 = at(uy_off, L * GB * GP, NC).rearrange("p (l x) -> p l x", l=L)
        Y2 = U2
        new(L * GB * GP)
        Kp = at(r_off, GB * (2 * L - 1) * GP, GP).rearrange("p (g x) -> p g x", g=GB)
        rt_off = top[0]
        RT = new(2 * QB * P).rearrange("p (q c x) -> p q c x", q=QB, c=2)
        U2g = at(top[0], GB * P, NC).rearrange("p (g x) -> p g x", g=GB)
        M = new(GB * P).rearrange("p (g x) -> p g x", g=GB)
        U = new(GB * NC).rearrange("p (g c) -> p g c", g=GB)
        Et = new(2 * QB * NC).rearrange("p (c q n) -> p c q n", c=2, q=QB)
        V = new(4 * QB).rearrange("p (c q) -> p c q", c=4)
        hp_off = top[0]
        hp = new(2 * QB * (NC + 1)).rearrange("p (c q n) -> p c q n", c=2, q=QB)
        mag = new(QB * NC).rearrange("p (q n) -> p q n", q=QB)
        tq = QB * (L + 1) * GP
        tmp_off = top[0]
        new(2 * tq)
        tA = at(tmp_off, tq)
        tB = at(tmp_off + tq, tq)
        t5 = [at(tmp_off + n * QB * NC, QB * NC).rearrange("p (q n) -> p q n", q=QB) for n in range(4)]
        wu = at(ylru_off, KD * D).rearrange("p (k c) -> p k c", k=KD)
        xtok0 = at(r_off, TT * D).rearrange("p (t d) -> p t d", t=TT)
        usb = at(rt_off, TT * D).rearrange("p (t d) -> p t d", t=TT)
        braw = at(lru_off, 2 * NS * 2 * GP, NQ).rearrange("p (c x j) -> p c x j", c=2, j=GP)
        craw = [at(o, GP * P, NQ).rearrange("p (j x) -> p j x", j=GP) for o in (lru_off + 4096, ylru_off + 8192)]
        rows = at(tmp_off, P, 112)
        drow = at(tmp_off + P, GP, G)
        s_base = lru_off + 6144
        p_are, p_aim, p_dar, p_ph, p_mg, p_t0, p_t1 = (at(s_base + n * P, P, NQ) for n in range(7))
        pr = at(qc_off, (L + 1) * 2 * P, NQ).rearrange("p (j c x) -> p j c x", j=L + 1, c=2)
        sm = at(tmp_off + 256, 12 * P, NQ).rearrange("p (v x) -> p v x", v=12)
        ldt = at(tmp_off + 256 + 12 * P, 4, NQ)


        pq0, pq1 = (at(o, 4 * P, NQ).rearrange("q (j x) -> q j x", j=4) for o in (hp_off, hp_off + 512))
        mid = ylru_off + MR * T + KD * T
        WB = 4 * KD * 2 * P + MR * 2 * P
        b0, b1 = mid, mid + WB
        wfour = [at(o, 4 * KD * 2 * P).rearrange("p (w k c) -> p w k c", w=4, k=KD) for o in (b0, b1)]
        wlo = [at(o + 4 * KD * 2 * P, MR * 2 * P).rearrange("p (k c) -> p k c", k=MR) for o in (b0, b1)]
        m_off = mid + 2 * WB
        merged = at(m_off, KD * T).rearrange("p (m t) -> p m t", m=KD)
        sg_off = m_off + KD * T
        sg = [[at(sg_off + (5 * n + j) * T, T) for j in range(5)] for n in range(2)]
        tail = sg_off + 10 * T

        x1 = at(ylru_off, TT * D).rearrange("p (t d) -> p t d", t=TT)
        x1T = at(ylru_off + 4096, KD * T).rearrange("p (k t) -> p k t", k=KD)
        plew = at(ylru_off + 8192, 2 * D).rearrange("p (k c) -> p k c", k=2)
        wout = at(b0, KD * D).rearrange("p (k c) -> p k c", k=KD)
        pleg = at(b1, KD * D).rearrange("p (k c) -> p k c", k=KD)
        ptok = at(b1 + 8192, TT * 2 * P).rearrange("p (t c) -> p t c", t=TT)
        pT = at(b1 + 9216, 2 * T).rearrange("p (k t) -> p k t", k=2)
        tmpd = [at(b1 + 10240, D), at(tail + 4096, D)]
        xtok = at(tail, TT * D).rearrange("p (t d) -> p t d", t=TT)
        acc = at(m_off, TT * D).rearrange("p (t d) -> p t d", t=TT)
        lnp = at(sg_off, 5 * D).rearrange("p (v d) -> p v d", v=5)
        wrt = at(tail + 5120, KD * E).rearrange("p (k e) -> p k e", k=KD)
        gu = [at(o, KD * 2 * F).rearrange("p (k w f) -> p k w f", k=KD, w=2)
              for o in (b1, tail, ylru_off + 4096, b0)]
        dn = [at(o, 2 * D).rearrange("p (k c) -> p k c", k=2)
              for o in (b1 + 4096, b0 + 6144, b1 + 6144, b0 + 4096)]
        xg = [at(ylru_off + n * D, D, SL) for n in range(4)]
        xgT = [at(b1 + 8192 + n * KD * SL, KD * SL).rearrange("p (k s) -> p k s", k=KD) for n in range(2)]
        yb = [at(ylru_off + 8192 + n * D, D, SL) for n in range(2)]
        sil = [at(tail + 4096 + n * F, F) for n in range(2)]
        hdn = [at(tail + 4608 + n * F, F) for n in range(2)]
        hT = [at(tail + 5120 + n * F, F).rearrange("p (k s) -> p k s", k=2) for n in range(2)]
        small = b0 + 8192

        def sc(off, cols, parts=P):
            return at(small + off, cols, parts)

        def te(off, n=E):
            return sc(off, TT * n).rearrange("p (t e) -> p t e", t=TT)

        stats = sc(0, 16)
        rbias = sc(16, E)
        iota_e = sc(80, E)
        score, biased, mask, row, repl = (te(144 + 256 * n) for n in range(5))
        gtop = sc(1424, TT * EG * 8).rearrange("p (g x) -> p g x", g=TT * EG)
        gsum = te(1680, EG)
        gsel = te(1712, EG)
        top8, idx8, idx8f, slotf, sloti, gate = (te(1744 + 32 * n, K) for n in range(6))
        cnt, ovc, ovi, e128, cbase, ones_e = (sc(1936 + E * n, E) for n in range(6))
        gsc = sc(2324, TT)
        novi = sc(2328, 1)
        texpf, texpi, iota_i = (sc(2336 + 48 * n, 48) for n in range(3))
        pairs = sc(2480, TT * K * 2).rearrange("p (t k v) -> p t k v", t=TT, k=K)
        lt = sc(2544, EG * EG).rearrange("p (a b) -> p a b", a=EG)
        slotR = sc(2608, SL * 2, NT).rearrange("p (s v) -> p s v", v=2)
        idxT = sc(2800, NT, SL)
        gateT = sc(2906, NT, SL)
        idxcol = sc(3012, 5, SL)
        yzero = at(tail + 4096, D, SL)
        eqt = at(b0 + 6144, TT * K * E).rearrange("p (t k e) -> p t k e", t=TT, k=K)
        eqp = at(tail, TT * K * E).rearrange("p (t k e) -> p t k e", t=TT, k=K)
        pair = at(tail + 2048, TT * EG * EG).rearrange("p (t a b) -> p t a b", t=TT, a=EG)
        pair2 = at(tail + 2304, TT * EG * EG).rearrange("p (t a b) -> p t a b", t=TT, a=EG)
        texw = at(tail + 2560, 24 * E, 1).rearrange("p (i e) -> p i e", i=24)

        s_x = [sem(f"x_tile_loaded{t}") for t in range(TT)]
        names = """ple_val wu2_loaded scaled last_ready rows_added col_seen sc_col lin0_loaded  acc_stored slot_col padded  U2_turned b_val o_xT_act rows_loaded s5_loaded bc_loaded wu_loaded const_ready xT_put xT_act xT_dve rows_put rows_kept
            bc_put bc_kept u_put u_kept u_stored dt_ready dar_ready polar_ready
            powers_ready powers_put powers_kept lru_exp lru_c_ready
            u2_loaded wx_loaded wg_loaded bd_loaded bd_zeroed U_put U_kept xproj_put conv_begun conv_done
            R_ready RT_put RT_kept gproj_put g_kept Q_ready K_put K_ready k_stored M_loaded S_put h_ready
            gates_put gates_kept decay_ready square_ready ix_ready mult2_ready mult_ready lru_done
            Y_put Y_kept yT_put yT_kept
            wb0_loaded wb1_loaded b_sig b_done xtok_loaded wout_loaded lnp_loaded pleg_loaded
            ple_loaded shared_loaded tab_zeroed res_put res_added var_ready std_ready x1_ready x1_stored
            x1T_put x1T_kept pT_put pT_kept router_put score_ready mask_ready rank_put slot_ready
            tok_stored tok_loaded tokT_put idx_ready ple_put pg_biased pg_sig ple_done
            sh_put sh_silu sh_hid sh_hT_put sh_hT sh_y_put sh_done texp_ready 
            xT_e_put xT_e_act xT_e_dve g_e_put silu_e hid_e hT_e_put hT_e_kept y_e_put y_e_act y_e_dve
             o_w o_xT_put o_xT_kept o_g_put o_silu o_hid o_hT_put o_hT_kept o_y_put o_y_kept 
            over_done out_ready out_stored""".split()
        S = {n: sem(n) for n in names}
        s_wgu = [sem(f"expert_in{u}") for u in range(4)]
        s_wdn = [sem(f"expert_down{u}") for u in range(4)]
        s_gath = [sem(f"rows_gathered{u}") for u in range(4)]
        s_acc = [sem(f"tile_reloaded{t}") for t in range(TT)]

        def need(eng, name, v):
            if v > 0:
                eng.wait_ge(S[name], v)

        def wait(eng, s, v):
            if not isinstance(v, int) or v > 0:
                eng.wait_ge(s, v)

        block = ctx.enter_context(nc.Block())

        def bc(ap, axis, n):
            shape = list(ap.shape)
            shape.insert(axis, n)
            return ap.unsqueeze(axis).to_broadcast(shape)

        w_in, w_glu, w_lo, w_out = A["w_in"][0], A["w_glu"][0], A["w_lru_out"][0], A["w_out"][0]
        x_tok = A["x"][0].rearrange("(t p) d -> p t d", p=P)
        w_in_k = w_in.rearrange("(p k) c -> p k c", k=KD)
        w_glu_k = w_glu.rearrange("(k p) c -> p k c", p=P)
        w_lo_k = w_lo.rearrange("(k p) c -> p k c", p=P)
        X_COL, G_COL, U_COL, GA_COL, GB_COL = 0, D_RNN, 2 * D_RNN, 2 * D_RNN + D, 2 * D_RNN + 2 * D
        PIECES = []
        for h in range(CB // HD):
            r0 = h * HD
            while r0 < (h + 1) * HD:
                n = min((h + 1) * HD, (r0 // P + 1) * P) - r0
                PIECES.append((h, r0 - h * HD, n, r0 // P, r0 % P))
                r0 += n
        PAIRS = [(k, m) for m in range(ML) for k in range(ML)
                 if any(t == k and h * HD < (m + 1) * P and (h + 1) * HD > m * P for h, _, _, t, _ in PIECES)]
        LRU_BANKS = [2, 3, 0, 1, 2, 3]
        G_BANKS = [3, 0, 1]

        @block.sync
        def _(sp):
            for t in range(TT):
                sp.dma_start(xtok0[:, t, :], x_tok[:, t, :]).then_inc(s_x[t], 16)
            srcs = [(A["conv_w"][0].rearrange("w (m p) -> (w m) p", p=P), 4 * MR)]
            srcs += [(A[n][0].rearrange("(m p) -> m p", p=P), MR) for n in ("conv_b",)]
            srcs += [(A[n][0].rearrange("h j -> (h j)").rearrange("(m p) -> m p", p=P), MR) for n in ("lru_ba", "lru_bx")]
            srcs += [(A["lru_lambda"][0].rearrange("(m p) -> m p", p=P), MR)]
            srcs += [(A["b_glu"][0].rearrange("(m p) -> m p", p=P), 2 * KD)]
            r0 = 0
            for src, n in srcs:
                sp.dma_start(rows[r0:r0 + n, :], src).then_inc(S["rows_loaded"], 16)
                r0 += n
            sp.dma_start(drow, A["s5_d"][0].rearrange("(g j) -> g j", j=GP)).then_inc(S["rows_loaded"], 16)
            sp.dma_start(p_are, A["s5_a_re"][0].rearrange("(q h) n -> q (h n)", h=2)).then_inc(S["s5_loaded"], 16)
            sp.dma_start(p_aim, A["s5_a_im"][0].rearrange("(q h) n -> q (h n)", h=2)).then_inc(S["s5_loaded"], 16)
            sp.dma_start(ldt[:, 0:2], A["s5_log_dt"][0].rearrange("(q h) -> q h", h=2)).then_inc(S["s5_loaded"], 16)
            sp.dma_start(wu[:, :, 0:512], w_in_k[:, :, U_COL:U_COL + 512]).then_inc(S["wu_loaded"], 16)
            for c, n in enumerate(("s5_b_re", "s5_b_im")):
                sp.dma_start(braw[:, c].rearrange("p x j -> p (x j)"),
                             A[n][0].rearrange("(q h) n j -> q (h n j)", h=2)).then_inc(S["bc_loaded"], 16)
            for c, n in enumerate(("s5_c_re", "s5_c_im")):
                for h in range(2):
                    sp.dma_start(craw[c][:, :, h * NS:(h + 1) * NS],
                                 A[n][0].rearrange("(q h) j n -> h q j n", h=2)[h]).then_inc(S["bc_loaded"], 16)
            sp.dma_start(wu[:, :, 512:1024], w_in_k[:, :, U_COL + 512:U_COL + 1024]).then_inc(S["wu2_loaded"], 16)

            def load_x(b):
                sp.dma_start(wx, w_in_k[:, :, X_COL + b * CB:X_COL + (b + 1) * CB]).then_inc(S["wx_loaded"], 16)

            def load_g(b):
                sp.dma_start(wg, w_in_k[:, :, G_COL + b * CB:G_COL + (b + 1) * CB]).then_inc(S["wg_loaded"], 16)

            def load_bd(b):
                for g, n in enumerate(("lru_wa", "lru_wx")):
                    for h, i0, cnt_, t, p0 in PIECES:
                        sp.dma_start(bd[p0:p0 + cnt_, g, t, h * HD:(h + 1) * HD],
                                     A[n][0, b * (CB // HD) + h, i0:i0 + cnt_, :]).then_inc(S["bd_loaded"], 16)

            def load_u2(b):
                sp.dma_start(U2, u_dram.rearrange("(c l) x -> c l x", l=L)[:, :, b * GB * GP:(b + 1) * GB * GP]
                             ).then_inc(S["u2_loaded"], 16)

            load_x(0)
            load_g(0)
            sp.wait_ge(S["bd_zeroed"], 1)
            load_bd(0)
            sp.wait_ge(S["u_kept"], 2 * TT)
            sp.dma_start(u_dram.rearrange("(t p) d -> p t d", p=P), usb).then_inc(S["u_stored"], 16)
            sp.wait_ge(S["u_stored"], 16)
            sp.wait_ge(S["const_ready"], 1)
            sp.wait_ge(S["xT_put"], 2 * TT)
            load_u2(0)
            for b in range(NB):
                if b + 1 < NB:
                    sp.wait_ge(S["xproj_put"], ML * (b + 1))
                    load_x(b + 1)
                    sp.wait_ge(S["gproj_put"], ML * (b + 1))
                    load_g(b + 1)
                sp.wait_ge(S["K_ready"], b + 1)
                sp.dma_start(k_dram[b].rearrange("g j x -> j g x"), Kp).then_inc(S["k_stored"], 16)
                sp.wait_ge(S["k_stored"], 16 * (b + 1))
                need(sp, "Y_put", 2 * b)
                for l in range(L):
                    sp.dma_start(M[l * GP:(l + 1) * GP],
                                 k_dram[b, :, :, (L - 1 - l) * GP:(L - 1 - l) * GP + L * GP]
                                 .rearrange("g j x -> j g x")).then_inc(S["M_loaded"], 16)
                if b + 1 < NB:
                    sp.wait_ge(S["gates_put"], 2 * ML * (b + 1))
                    load_bd(b + 1)
                    sp.wait_ge(S["yT_put"], 2 * (b + 1))
                    load_u2(b + 1)

            B_SRC = ((w_in_k, GA_COL), (w_in_k, GB_COL), (w_glu_k, D), (w_glu_k, 0))

            def load_b(m, ws, done):
                for w in ws:
                    if w < 4:
                        src, c0 = B_SRC[w]
                        c0 += 2 * P * m
                        sp.dma_start(wfour[m % 2][:, w], src[:, :, c0:c0 + 2 * P]).then_inc(done, 16)
                    else:
                        sp.dma_start(wlo[m % 2], w_lo_k[:, :, 2 * P * m:2 * P * (m + 1)]).then_inc(done, 16)

            sp.wait_ge(S["gproj_put"], MR)
            load_b(0, (0, 1, 2), S["wb0_loaded"])
            sp.wait_ge(S["lru_done"], MR)
            load_b(0, (3, 4), S["lin0_loaded"])
            sp.wait_ge(S["yT_kept"], 2 * NB)
            load_b(1, range(5), S["wb1_loaded"])
            sp.dma_start(xtok, x_tok).then_inc(S["xtok_loaded"], 16)
            for m in range(2, 4):
                sp.wait_ge(S["b_val"], 10 * (m - 1))
                load_b(m, range(5), S[f"wb{m % 2}_loaded"])
            sp.wait_ge(S["b_val"], 30)
            sp.dma_start(wout, w_out.rearrange("(k p) c -> p k c", p=P)).then_inc(S["wout_loaded"], 16)
            sp.dma_start(rbias, A["router_bias"][0].partition_broadcast(P)).then_inc(S["lnp_loaded"], 16)
            sp.wait_ge(S["b_val"], 40)
            sp.dma_start(plew, A["ple_w"][0].rearrange("(p k) c -> p k c", k=2)).then_inc(S["ple_loaded"], 16)
            sp.dma_start(ptok, A["p"][0, 0].rearrange("(t p) c -> p t c", p=P)).then_inc(S["ple_loaded"], 16)
            sp.dma_start(wrt, A["router_w"][0].rearrange("(p k) e -> p k e", k=KD)).then_inc(S["ple_loaded"], 16)
            sp.dma_start(pleg, A["ple_gate_w"][0].rearrange("(p k) c -> p k c", k=KD)).then_inc(S["pleg_loaded"], 16)
            sp.wait_ge(S["b_done"], KD)
            for v, n in enumerate(("ln1_g", "ln1_b", "ln2_g", "ln2_b", "ple_gate_b")):
                sp.dma_start(lnp[:, v, :], A[n][0].partition_broadcast(P)).then_inc(S["lnp_loaded"], 16)
            sp.wait_ge(S["res_put"], 2 * TT)
            for w, n in enumerate(("shared_w_gate", "shared_w_up")):
                sp.dma_start(gu[3][:, :, w, :], A[n][0].rearrange("(p k) f -> p k f", k=KD)).then_inc(S["shared_loaded"], 16)
            sp.dma_start(dn[3], A["shared_w_down"][0].rearrange("(p k) c -> p k c", k=2)).then_inc(S["shared_loaded"], 16)
            for t in range(TT):
                sp.wait_ge(S["x1_ready"], t + 1)
                sp.dma_start(x1_dram[t * P:(t + 1) * P, :], x1[:, t, :]).then_inc(S["x1_stored"], 16)

            w_gate_e = A["moe_w_gate"][0].rearrange("e (p k) f -> e p k f", k=KD)
            w_up_e = A["moe_w_up"][0].rearrange("e (p k) f -> e p k f", k=KD)
            w_down_e = A["moe_w_down"][0].rearrange("e (p k) c -> e p k c", k=2)

            def load_in(e, u, done):
                for w, src in enumerate((w_gate_e, w_up_e)):
                    sp.dma_start(gu[u][:, :, w, :], src[bass.ds(e, 1)].rearrange("o p k f -> p (o k) f")).then_inc(done, 16)

            def load_down(e, u, done):
                sp.dma_start(dn[u], w_down_e[bass.ds(e, 1)].rearrange("o p k c -> p (o k) c")).then_inc(done, 16)

            def load_expert(e, u, in_done, down_done):
                load_in(e, u, in_done)
                load_down(e, u, down_done)

            sp.wait_ge(S["ple_put"], 2 * TT)
            sp.wait_ge(S["ple_val"], TT)
            load_expert(0, 0, s_wgu[0], s_wdn[0])
            sp.wait_ge(S["slot_ready"], 1)
            load_expert(1, 1, s_wgu[1], s_wdn[1])
            sp.wait_ge(S["sh_put"], TT)
            load_expert(2, 2, s_wgu[2], s_wdn[2])
            sp.wait_ge(S["sh_y_put"], TT)
            load_expert(3, 3, s_wgu[3], s_wdn[3])
            sp.wait_ge(S["sh_done"], TT)
            sp.dma_start(acc_dram[0:T, :].rearrange("(t p) d -> p t d", p=P), acc).then_inc(S["acc_stored"], 16)
            with sp.Fori(0, E // 4 - 1) as i:
                for u in range(4):
                    sp.wait_ge(S["g_e_put"], 4 * i + (u + 1))
                    load_in(4 * i + (4 + u), u, s_wgu[u])
                    sp.wait_ge(S["y_e_put"], 4 * i + (u + 1))
                    load_down(4 * i + (4 + u), u, s_wdn[u])
            sp.wait_ge(S["y_e_put"], E)
            sp.wait_ge(S["texp_ready"], 1)
            n_over = sp.value_load(novi[0:1, 0:1].bitcast(i32), min_val=0, max_val=OV)
            with sp.If(n_over > 0):
                with sp.Fori(0, OV) as i:
                    with sp.If(i < n_over):
                        e = sp.value_load(texpi[0:1, bass.ds(i, 1)].bitcast(i32), min_val=0, max_val=E - 1)
                        sp.wait_ge(S["o_y_kept"], 2 * i + 1)
                        load_expert(e, 0, S["o_w"], S["o_w"])
                    sp.nop()
            for t in range(TT):
                if t == 0:
                    sp.wait_ge(S["over_done"], 1)
                sp.dma_start(acc[:, t, :], acc_dram[t * P:(t + 1) * P, :]).then_inc(s_acc[t], 16)
            for t in range(TT):
                if t < TT - 1:
                    sp.wait_ge(S["out_ready"], t + 1)
                else:
                    sp.wait_ge(S["last_ready"], 1)
                sp.dma_start(out[0, t * P:(t + 1) * P, :], acc[:, t, :]).then_inc(S["out_stored"], 16)
            sp.wait_ge(S["out_stored"], 16 * TT)

        @block.gpsimd
        def _(pool):
            nc.gpsimd.memset(ident, 0.0)
            nc.gpsimd.memset(ones, 1.0)
            nc.gpsimd.memset(strict, 1.0)
            nc.gpsimd.memset(eps_t, EPS)
            pool.drain()
            nc.gpsimd.affine_select(out=ident, in_=ident, compare_op=ALU.not_equal, fill=1.0, base=0,
                                    pattern=[[-1, P]], channel_multiplier=1)
            nc.gpsimd.affine_select(out=strict, in_=strict, compare_op=ALU.is_gt, fill=0.0, base=0,
                                    pattern=[[1, P]], channel_multiplier=-1)
            pool.drain()
            pool.sem_inc(S["const_ready"], 1)
            nc.gpsimd.memset(bd.rearrange("p g k c -> p (g k c)"), 0.0).then_inc(S["bd_zeroed"], 1)
            for b in range(NB):
                pool.wait_ge(S["u2_loaded"], 16 * (b + 1))
                if b == 0:
                    pool.wait_ge(S["u_stored"], 16)
                need(pool, "Y_put", 2 * b)
                nc.gpsimd.tensor_copy(U2g.rearrange("c g (l o) -> c l g o", l=L),
                                      U2.rearrange("c l (g o) -> c l g o", g=GB)).then_inc(S["U2_turned"], 1)
                for m in range(ML):
                    pool.wait_ge(S["decay_ready"], ML * b + m + 1)
                    nc.gpsimd.tensor_tensor(rr[:, m], aa[:, m], aa[:, m], ALU.mult).then_inc(S["square_ready"], 1)
                    nc.gpsimd.tensor_tensor(ii[:, m], ii[:, m], xc[:, m], ALU.mult).then_inc(S["ix_ready"], 1)
            pool.wait_ge(S["b_val"], 30)
            nc.gpsimd.memset(ones_e, 1.0)
            nc.gpsimd.iota(iota_e, [[1, E]], base=0, channel_multiplier=0, allow_small_or_imprecise_dtypes=True)
            nc.gpsimd.iota(e128, [[SL, E]], base=0, channel_multiplier=0, allow_small_or_imprecise_dtypes=True)
            nc.gpsimd.iota(pairs[:, :, :, 0], [[P, TT], [0, K]], base=0, channel_multiplier=1,
                           allow_small_or_imprecise_dtypes=True)
            nc.gpsimd.iota(iota_i, [[1, 48]], base=0, channel_multiplier=0, allow_small_or_imprecise_dtypes=True)
            nc.gpsimd.memset(slotR, 0.0)
            nc.gpsimd.memset(yzero, 0.0)
            pool.drain()
            nc.gpsimd.iota(slotR[:, :, 0], [[1, SL]], base=T, channel_multiplier=0, allow_small_or_imprecise_dtypes=True)
            nc.gpsimd.memset(lt.rearrange("p a b -> p (a b)"), 1.0)
            pool.drain()
            nc.gpsimd.affine_select(out=lt, in_=lt, compare_op=ALU.is_gt, fill=0.0, base=0,
                                    pattern=[[1, EG], [-1, EG]], channel_multiplier=0)
            pool.drain()
            nc.gpsimd.dma_start(slot_dram.rearrange("(n s) v -> n (s v)", s=SL), slotR.rearrange("p s v -> p (s v)")
                                ).then_inc(S["tab_zeroed"], 16)
            pool.sem_inc(S["const_ready"], 1)
            pool.wait_ge(S["tab_zeroed"], 16)
            for dst in (x1_dram, acc_dram):
                nc.gpsimd.dma_start(dst[T:T + SL, :], yzero).then_inc(S["padded"], 16)
            pool.wait_ge(S["slot_ready"], 1)
            for t in range(TT):
                for k in range(K):
                    nc.gpsimd.indirect_dma_start(
                        out=slot_dram, out_offset=bass.IndirectOffsetOnAxis(ap=sloti[:, t, k:k + 1].bitcast(u32), axis=0),
                        in_=pairs[:, t, k, :], in_offset=None).then_inc(S["tok_stored"], 16)
            pool.wait_ge(S["tok_stored"], 16 * TT * K)
            nc.gpsimd.dma_start(slotR.rearrange("p s v -> p (s v)"), slot_dram.rearrange("(n s) v -> n (s v)", s=SL)
                                ).then_inc(S["tok_loaded"], 16)

            def gather(e, u, n):
                nc.gpsimd.tensor_copy(idxcol[:, u:u + 1].bitcast(i32), idxT[:, bass.ds(e, 1)].bitcast(i32)).then_inc(S["slot_col"], 1)
                pool.wait_ge(S["slot_col"], n + 1)
                pool.sem_inc(S["col_seen"], 1)
                nc.gpsimd.indirect_dma_start(
                    out=xg[u], out_offset=None, in_=x1_dram,
                    in_offset=bass.IndirectOffsetOnAxis(ap=idxcol[:, u:u + 1].bitcast(u32), axis=0)).then_inc(s_gath[u], 16)

            def add_rows(buf, e, n):
                wait(pool, S["rows_added"], 16 * n)
                pool.sem_inc(S["col_seen"], 1)
                nc.gpsimd.tensor_copy(idxcol[:, 4:5].bitcast(i32), idxT[:, bass.ds(e, 1)].bitcast(i32)).then_inc(S["sc_col"], 1)
                pool.wait_ge(S["sc_col"], n + 1)
                pool.sem_inc(S["col_seen"], 1)
                nc.gpsimd.indirect_dma_start(
                    out=acc_dram, out_offset=bass.IndirectOffsetOnAxis(ap=idxcol[:, 4:5].bitcast(u32), axis=0),
                    in_=yb[buf], in_offset=None, compute_op=ALU.add).then_inc(S["rows_added"], 16)

            pool.wait_ge(S["idx_ready"], 1)
            pool.wait_ge(S["x1_stored"], 16 * TT)
            pool.wait_ge(S["padded"], 32)
            pool.wait_ge(S["ple_done"], TT)
            for u in range(4):
                gather(u, u, u)
            pool.wait_ge(S["acc_stored"], 16)

            def add_expert(i, u):
                pool.wait_ge(S["y_e_act"], 4 * i + u + 1)
                pool.wait_ge(S["y_e_dve"], 4 * i + u + 1)
                add_rows(u % 2, 4 * i + u, 4 * i + u)

            for u in range(4):
                pool.wait_ge(S["xT_e_put"], u + 1)
                gather(4 + u, u, 4 + u)
                add_expert(0, u)
            with pool.Fori(1, E // 4 - 1) as i:
                for u in range(4):
                    pool.wait_ge(S["xT_e_put"], 4 * i + (u + 1))
                    gather(4 * i + (4 + u), u, 4 * i + (4 + u))
                    add_expert(i, u)
            for u in range(E - 4, E):
                add_expert(0, u)
            n_over = pool.value_load(novi[0:1, 0:1].bitcast(i32), min_val=0, max_val=OV)
            with pool.If(n_over > 0):
                with pool.Fori(0, OV) as i:
                    with pool.If(i < n_over):
                        gather(i + E, 0, i + E)
                        pool.wait_ge(S["o_y_kept"], 2 * i + 2)
                        add_rows(0, i + E, i + E)
                        pool.wait_ge(S["rows_added"], 16 * i + 16 * (E + 1))
                        pool.sem_inc(S["o_y_kept"], 1)
                    pool.nop()
            pool.wait_ge(S["rows_added"], 16 * E)
            pool.sem_inc(S["over_done"], 1)
            for t in range(TT - 1):
                pool.wait_ge(S["scaled"], t + 1)
                nc.gpsimd.tensor_tensor(acc[:, t, :], acc[:, t, :], lnp[:, 3, :], ALU.add).then_inc(S["out_ready"], 1)

        mm = nc.tensor.matmul

        @block.tensor
        def _(pe):
            def tp(dst, src, n):
                return nc.tensor.transpose(dst, src, ident[0:n, 0:n])

            pe.wait_ge(S["const_ready"], 1)
            for t in range(TT):
                pe.wait_ge(s_x[t], 16)
                xv = xtok0[:, t, :].rearrange("p (d k) -> p k d", k=KD)
                for h in range(2):
                    for k in range(4):
                        last = tp(banks[2 * t + h][:, k * P:(k + 1) * P], xv[:, 4 * h + k, :], P)
                    last.then_inc(S["xT_put"], 1)
            pe.wait_ge(S["rows_loaded"], 16 * 7)
            pe.wait_ge(S["xT_act"], 1)
            tp(banks[0][:, 0:112], rows, 112)
            tp(banks[0][0:GP, P:P + G], drow, G).then_inc(S["rows_put"], 1)
            pe.wait_ge(S["wu_loaded"], 16)
            pe.wait_ge(S["xT_act"], TT)
            pe.wait_ge(S["xT_dve"], TT)

            def u_proj(n):
                hf, t = divmod(n, TT)
                if n == 3:
                    pe.wait_ge(S["rows_kept"], 1)
                if n == 4:
                    pe.wait_ge(S["bc_kept"], 4)
                    pe.wait_ge(S["wu2_loaded"], 16)
                for k in range(KD):
                    last = mm(banks[(5 + n) % 8][:, :], xT[:, k, t * P:(t + 1) * P], wu[:, k, hf * 512:(hf + 1) * 512],
                              start=(k == 0), stop=(k == KD - 1))
                last.then_inc(S["u_put"], 1)

            u_proj(0)
            pe.wait_ge(S["bc_loaded"], 16 * 6)
            for c in range(4):
                for j in range(GP):
                    src = braw[:, c, :, j] if c < 2 else craw[c - 2][:, j, :]
                    last = tp(banks[1 + c][:, j * NQ:(j + 1) * NQ], src, NQ)
                last.then_inc(S["bc_put"], 1)
            for n in range(1, 2 * TT):
                u_proj(n)
            pe.wait_ge(S["powers_ready"], 1)
            pe.wait_ge(S["u_kept"], 2)
            for j in range(1, L + 1):
                for c in range(2):
                    n = 2 * (j - 1) + c
                    tp(banks[5][:, n * NQ:(n + 1) * NQ], pr[:, j, c, :], NQ)
            for n, v in enumerate((8, 10, 7, 3, 2)):
                last = tp(banks[6][:, n * NQ:(n + 1) * NQ], sm[:, v, :], NQ)
            last.then_inc(S["powers_put"], 1)

            for b in range(NB):
                if b == 0:
                    pe.wait_ge(S["u_kept"], 2 * TT)
                    pe.wait_ge(S["powers_kept"], 1)
                pe.wait_ge(S["wx_loaded"], 16 * (b + 1))
                need(pe, "gates_kept", 6 * b)
                for m in range(ML):
                    for k in range(KD):
                        last = mm(banks[m][:, :], wx[:, k, m * P:(m + 1) * P], xT[:, k, :], start=(k == 0), stop=(k == KD - 1))
                    last.then_inc(S["xproj_put"], 1)
                pe.wait_ge(S["U2_turned"], b + 1)
                need(pe, "yT_kept", 2 * b)
                for g in range(GB):
                    last = tp(banks[4 + g // 8][:, (g % 8) * NC:(g % 8 + 1) * NC], U2g[:, g, :], NC)
                    if g % 8 == 7:
                        last.then_inc(S["U_put"], 1)
                pe.wait_ge(S["R_ready"], b + 1)
                pe.wait_ge(S["U_kept"], 2 * (b + 1))
                need(pe, "Y_kept", 4 * b)
                for n in range(2 * QB):
                    q, c = divmod(n, 2)
                    last = tp(banks[4 + n // 4][:, (n % 4) * P:(n % 4 + 1) * P], R[:, c, q, :], P)
                    if n % 4 == 3:
                        last.then_inc(S["RT_put"], 1)
                pe.wait_ge(S["wg_loaded"], 16 * (b + 1))

                def g_proj(m):
                    if m:
                        pe.wait_ge(S["conv_done"], ML * b + m)
                    for k in range(KD):
                        last = mm(banks[G_BANKS[m]][:, :], wg[:, k, m * P:(m + 1) * P], xT[:, k, :],
                                  start=(k == 0), stop=(k == KD - 1))
                    last.then_inc(S["gproj_put"], 1)

                g_proj(0)
                pe.wait_ge(S["Q_ready"], b + 1)
                for g in range(GB):
                    q, h = divmod(g, 2)
                    hs = slice(h * NS, (h + 1) * NS)
                    if g == 0:
                        pe.wait_ge(S["RT_kept"], 4 * (b + 1))
                    for c in range(2):
                        last = mm(banks[4 + 2 * h + q // 4][0:GP, (q % 4) * P:(q % 4 + 1) * P], bT[hs, c, :, b * QB + q],
                                  Q[hs, c, q, 0:L, :], start=(c == 0), stop=(c == 1))
                    if g % 8 == 7:
                        last.then_inc(S["K_put"], 1)
                g_proj(1)
                pe.wait_ge(S["K_ready"], b + 1)
                for c in range(2):
                    for q in range(QB):
                        for h in range(2):
                            last = mm(banks[4 + c][h * NS:(h + 1) * NS, q * NC:(q + 1) * NC],
                                      RT[:, q, c, h * NS:(h + 1) * NS], U[:, 2 * q + h, :], start=True, stop=True)
                last.then_inc(S["S_put"], 1)
                g_proj(2)
                pe.wait_ge(S["bd_loaded"], 16 * 2 * len(PIECES) * (b + 1))
                pe.wait_ge(S["conv_done"], ML * (b + 1))
                for n in range(2 * ML):
                    g, m = divmod(n, ML)
                    if n in (1, 2, 3):
                        pe.wait_ge(S["g_kept"], ML * b + n)
                    if n > 3:
                        pe.wait_ge(S["gates_kept"], 6 * b + n - 3)
                    ks = [k for k, mt in PAIRS if mt == m]
                    for k in ks:
                        last = mm(banks[LRU_BANKS[n]][:, :], bd[:, g, k, m * P:(m + 1) * P], xc[:, k, :],
                                  start=(k == ks[0]), stop=(k == ks[-1]))
                    last.then_inc(S["gates_put"], 1)
                pe.wait_ge(S["h_ready"], b + 1)
                pe.wait_ge(S["M_loaded"], 16 * L * (b + 1))
                for g in range(GB):
                    q, h = divmod(g, 2)
                    hs = slice(h * NS, (h + 1) * NS)
                    dst = banks[4 + 2 * h + q // 4][0:NC, (q % 4) * P:(q % 4 + 1) * P]
                    mm(dst, U[:, g, :], M[:, g, :], start=True, stop=False)
                    mm(dst, hp[hs, 0, q, 0:NC], Q[hs, 0, q, 1:L + 1, :], start=False, stop=False)
                    last = mm(dst, hp[hs, 1, q, 0:NC], Q[hs, 1, q, 1:L + 1, :], start=False, stop=True)
                    if g % 8 == 7:
                        last.then_inc(S["Y_put"], 1)
                pe.wait_ge(S["Y_kept"], 4 * (b + 1))
                for s in range(2):
                    for l in range(L):
                        last = tp(banks[4 + s][:, l * NC:(l + 1) * NC], Y2[:, l, s * P:(s + 1) * P], NC)
                    last.then_inc(S["yT_put"], 1)

            for m in range(KD):
                if m == 0:
                    pe.wait_ge(S["gates_kept"], 6 * NB)
                if m % 2 == 0:
                    if m == 0:
                        pe.wait_ge(S["wb0_loaded"], 48)
                    elif m == 4:
                        pe.wait_ge(S["wb0_loaded"], 48 + 80)
                    else:
                        pe.wait_ge(S["wb1_loaded"], 80 * (m // 4 + 1))
                n = m // 2 % 2
                cs = slice((m % 2) * P, (m % 2 + 1) * P)
                for j, w in enumerate((0, 1, 2, 3, 4)):
                    v = 5 * m + j
                    if m == 0 and j == 3:
                        pe.wait_ge(S["lin0_loaded"], 32)
                        pe.wait_ge(S["lru_done"], MR)
                    if m == 0 and j == 2:
                        pe.wait_ge(S["yT_kept"], 2 * NB)
                    if v >= 8:
                        pv = v - 8
                        pm, pj = divmod(pv, 5)
                        if pj < 3:
                            pe.wait_ge(S["b_sig"], 3 * pm + pj + 1)
                        else:
                            pe.wait_ge(S["b_done"], pm + 1)
                    nk = MR if w == 4 else KD
                    for k in range(nk):
                        lhs = wlo[n][:, k, cs] if w == 4 else wfour[n][:, w, k, cs]
                        rhs = ylru[:, k, :] if w == 4 else (xT[:, k, :] if w < 2 else ysT[:, k, :])
                        last = mm(banks[v % 8][:, :], lhs, rhs, start=(k == 0), stop=(k == nk - 1))
                    last.then_inc(S["b_val"], 1)
            def x1_turn(t):
                pe.wait_ge(S["x1_ready"], t + 1)
                if t:
                    pe.wait_ge(S["x1T_kept"], 2 * t)
                xv = x1[:, t, :].rearrange("p (d k) -> p k d", k=KD)
                for h in range(2):
                    for k in range(4):
                        last = tp(banks[4 + h][:, k * P:(k + 1) * P], xv[:, 4 * h + k, :], P)
                last.then_inc(S["x1T_put"], 1)

            pe.wait_ge(S["wout_loaded"], 16)
            pe.wait_ge(S["b_done"], KD)
            for n in range(2 * TT):
                t, hf = divmod(n, 2)
                if n >= 4:
                    pe.wait_ge(S["res_added"], n - 3)
                for k in range(KD):
                    last = mm(banks[n % 4][:, :], merged[:, k, t * P:(t + 1) * P], wout[:, k, hf * 512:(hf + 1) * 512],
                              start=(k == 0), stop=(k == KD - 1))
                last.then_inc(S["res_put"], 1)
                if hf and t:
                    x1_turn(t - 1)
            pe.wait_ge(S["ple_loaded"], 48)
            for c in range(2):
                for t in range(TT):
                    last = tp(banks[6 + c][:, t * P:(t + 1) * P], ptok[:, t, :].rearrange("p (d k) -> p k d", k=2)[:, c, :], P)
            last.then_inc(S["pT_put"], 1)

            def ple_gate(t):
                for hf in range(2):
                    if t:
                        pe.wait_ge(S["pg_biased"], 2 * (t - 1) + hf + 1)
                    else:
                        pe.wait_ge(S["res_added"], 2 * TT)
                    for k in range(KD):
                        last = mm(banks[hf][:, :], x1T[:, k, t * P:(t + 1) * P], pleg[:, k, hf * 512:(hf + 1) * 512],
                                  start=(k == 0), stop=(k == KD - 1))
                    last.then_inc(S["ple_put"], 1)

            def ple_value(t):
                if t:
                    pe.wait_ge(S["ple_done"], t)
                else:
                    pe.wait_ge(S["res_added"], 2 * TT)
                    pe.wait_ge(S["pT_kept"], 2)
                for hf in range(2):
                    for k in range(2):
                        last = mm(banks[2 + hf][:, :], pT[:, k, t * P:(t + 1) * P], plew[:, k, hf * 512:(hf + 1) * 512],
                                  start=(k == 0), stop=(k == 1))
                last.then_inc(S["ple_val"], 1)

            def sh_in(t):
                if t >= 2:
                    pe.wait_ge(S["sh_hid"], t - 1)
                for k in range(KD):
                    last = mm(banks[4 + t % 2][:, :], x1T[:, k, t * P:(t + 1) * P], gu[3][:, k, :, :],
                              start=(k == 0), stop=(k == KD - 1))
                last.then_inc(S["sh_put"], 1)

            ple_value(0)
            x1_turn(TT - 1)
            pe.wait_ge(S["x1T_kept"], 2 * TT)
            for t in range(TT):
                for k in range(KD):
                    last = mm(banks[6][:, t * E:(t + 1) * E], x1T[:, k, t * P:(t + 1) * P], wrt[:, k, :],
                              start=(k == 0), stop=(k == KD - 1))
            last.then_inc(S["router_put"], 1)

            pe.wait_ge(S["pleg_loaded"], 16)
            ple_gate(0)
            ple_gate(1)
            ple_value(1)
            pe.wait_ge(S["mask_ready"], 1)
            for t in range(TT):
                for s in range(t + 1):
                    mm(banks[7][:, t * E:(t + 1) * E], strict if s == t else ones, mask[:, s, :], start=(s == 0), stop=(s == t))
            for s in range(TT):
                last = mm(banks[7][:, TT * E:(TT + 1) * E], ones, mask[:, s, :], start=(s == 0), stop=(s == TT - 1))
            last.then_inc(S["rank_put"], 1)
            pe.wait_ge(S["shared_loaded"], 48)
            sh_in(0)
            for t in (2, 3):
                ple_gate(t)
                ple_value(t)

            def sh_out(t):
                pe.wait_ge(S["sh_hid"], t + 1)
                if t == 0:
                    pe.wait_ge(S["ple_done"], TT)
                else:
                    pe.wait_ge(S["sh_hT"], t)
                hv = hdn[t % 2].rearrange("p (d k) -> p k d", k=2)
                for k in range(2):
                    last = tp(banks[0][:, k * P:(k + 1) * P], hv[:, k, :], P)
                last.then_inc(S["sh_hT_put"], 1)
                pe.wait_ge(S["sh_hT"], t + 1)
                pe.wait_ge(S["slot_ready"], 1)
                if t:
                    pe.wait_ge(S["sh_done"], t)
                for hf in range(2):
                    for k in range(2):
                        last = mm(banks[6 + hf][:, :], hT[t % 2][:, k, :], dn[3][:, k, hf * 512:(hf + 1) * 512],
                                  start=(k == 0), stop=(k == 1))
                last.then_inc(S["sh_y_put"], 1)

            for t in range(TT):
                if t + 1 < TT:
                    sh_in(t + 1)
                if t == TT - 1:
                    pe.wait_ge(S["tok_loaded"], 16)
                    for v in range(2):
                        last = tp(banks[1][0:SL, v * P:v * P + NT], slotR[:, :, v], NT)
                    last.then_inc(S["tokT_put"], 1)
                sh_out(t)

            def x_turn(i, u):
                pe.wait_ge(s_gath[u % 4], 16 * i + 16 * (u // 4 + 1))
                wait(pe, S["xT_e_act"], 4 * i + u)
                wait(pe, S["xT_e_dve"], 4 * i + u)
                xv = xg[u % 4].rearrange("p (d k) -> p k d", k=KD)
                for h in range(2):
                    for k in range(4):
                        last = tp(banks[h][:, k * SL:(k + 1) * SL], xv[:, 4 * h + k, :], SL)
                last.then_inc(S["xT_e_put"], 1)

            def gate_up(i, u):
                pe.wait_ge(s_wgu[u % 4], 32 * i + 32 * (u // 4 + 1))
                pe.wait_ge(S["xT_e_act"], 4 * i + u + 1)
                pe.wait_ge(S["xT_e_dve"], 4 * i + u + 1)
                for k in range(KD):
                    last = mm(banks[2 + u % 2][0:SL, :], xgT[u % 2][:, k, :], gu[u % 4][:, k, :, :],
                              start=(k == 0), stop=(k == KD - 1))
                last.then_inc(S["g_e_put"], 1)

            def hid_turn(i, u):
                pe.wait_ge(S["hid_e"], 4 * i + u + 1)
                hv = hdn[u % 2][0:SL, :].rearrange("p (d k) -> p k d", k=2)
                for k in range(2):
                    last = tp(banks[4][:, k * SL:(k + 1) * SL], hv[:, k, :], SL)
                last.then_inc(S["hT_e_put"], 1)

            def down(i, u):
                pe.wait_ge(s_wdn[u % 4], 16 * i + 16 * (u // 4 + 1))
                pe.wait_ge(S["hT_e_kept"], 4 * i + u + 1)
                wait(pe, S["y_e_act"], 4 * i + u)
                wait(pe, S["y_e_dve"], 4 * i + u)
                for hf in range(2):
                    for k in range(2):
                        last = mm(banks[5 + hf][0:SL, :], hT[u % 2][:, k, 0:SL], dn[u % 4][:, k, hf * 512:(hf + 1) * 512],
                                  start=(k == 0), stop=(k == 1))
                last.then_inc(S["y_e_put"], 1)

            def expert(i, u, more=True):
                gate_up(i, u)
                if more:
                    x_turn(i, u + 1)
                if not isinstance(i, int) or u:
                    down(i, u - 1)
                hid_turn(i, u)

            pe.wait_ge(S["idx_ready"], 1)
            pe.wait_ge(S["sh_done"], TT)
            x_turn(0, 0)
            for u in range(0, 5):
                expert(0, u)
            with pe.Fori(1, E // 4 - 1) as i:
                for u in range(1, 5):
                    expert(i, u)
            for n in range(E - 3, E):
                expert(0, n, more=n + 1 < E)
            down(0, E - 1)
            pe.wait_ge(S["y_e_act"], E)
            pe.wait_ge(S["y_e_dve"], E)
            pe.wait_ge(S["texp_ready"], 1)
            n_over = pe.value_load(novi[0:1, 0:1].bitcast(i32), min_val=0, max_val=OV)
            with pe.If(n_over > 0):
                with pe.Fori(0, OV) as i:
                    with pe.If(i < n_over):
                        pe.wait_ge(s_gath[0], 16 * i + 16 * (E // 4 + 1))
                        xv = xg[0].rearrange("p (d k) -> p k d", k=KD)
                        for h in range(2):
                            for k in range(4):
                                last = tp(banks[h][:, k * SL:(k + 1) * SL], xv[:, 4 * h + k, :], SL)
                        last.then_inc(S["o_xT_put"], 1)
                        pe.wait_ge(S["o_xT_kept"], i + 1)
                        pe.wait_ge(S["o_w"], 48 * i + 48)
                        for k in range(KD):
                            last = mm(banks[2][0:SL, :], xgT[0][:, k, :], gu[0][:, k, :, :], start=(k == 0), stop=(k == KD - 1))
                        last.then_inc(S["o_g_put"], 1)
                        pe.wait_ge(S["o_hid"], i + 1)
                        hv = hdn[0][0:SL, :].rearrange("p (d k) -> p k d", k=2)
                        for k in range(2):
                            last = tp(banks[4][:, k * SL:(k + 1) * SL], hv[:, k, :], SL)
                        last.then_inc(S["o_hT_put"], 1)
                        pe.wait_ge(S["o_hT_kept"], i + 1)
                        for hf in range(2):
                            for k in range(2):
                                last = mm(banks[5 + hf][0:SL, :], hT[0][:, k, 0:SL], dn[0][:, k, hf * 512:(hf + 1) * 512],
                                          start=(k == 0), stop=(k == 1))
                        last.then_inc(S["o_y_put"], 1)
                    pe.nop()

        @block.scalar
        def _(act):
            def f(out_, in_, func, **kw):
                return nc.scalar.activation(out_, in_, func, **kw)

            for t in range(TT):
                act.wait_ge(S["xT_put"], 2 * t + 1)
                f(xT[:, 0:4, t * P:(t + 1) * P], banks[2 * t][:, :].rearrange("p (k x) -> p k x", k=4),
                  ACT.Copy).then_inc(S["xT_act"], 1)
            act.wait_ge(S["s5_loaded"], 48)
            f(ldt[:, 2:4], ldt[:, 0:2], ACT.Exp).then_inc(S["dt_ready"], 1)
            act.wait_ge(S["dar_ready"], 1)
            f(p_mg, p_dar, ACT.Exp)
            f(sm[:, 7, :], p_dar, ACT.Exp, scale=float(L)).then_inc(S["polar_ready"], 1)
            act.wait_ge(S["dar_ready"], 2)
            f(sm[:, 2, :], p_t1, ACT.Sin)
            f(sm[:, 3, :], sm[:, 1, :], ACT.Sin).then_inc(S["polar_ready"], 1)
            act.wait_ge(S["rows_kept"], 1)
            f(lnt[:, MR:2 * MR], lnt[:, 0:MR], ACT.Exp, scale=-1.0).then_inc(S["lru_exp"], 1)
            for c in (1, 3):
                act.wait_ge(S["bc_put"], c + 1)
                f((bT if c < 2 else cT)[:, 1].rearrange("p j q -> p (j q)"), banks[1 + c][:, :], ACT.Copy).then_inc(S["bc_kept"], 1)
            for n in range(2 * TT):
                hf, t = divmod(n, TT)
                act.wait_ge(S["u_put"], n + 1)
                f(usb[:, t, hf * 512:(hf + 1) * 512], banks[(5 + n) % 8][:, :], ACT.Copy).then_inc(S["u_kept"], 1)
            act.wait_ge(S["lru_c_ready"], 1)
            for b in range(NB):
                for m in range(ML):
                    ch = ML * b + m
                    act.wait_ge(S["xproj_put"], ML * b + m + 1)
                    need(act, "lru_done", ML * b)
                    f(xc[:, m, :], banks[m][:, :], ACT.Identity, scale=chan[:, 3 * MR + ch:3 * MR + ch + 1],
                      bias=chan[:, 4 * MR + ch:4 * MR + ch + 1]).then_inc(S["conv_begun"], 1)
                for s in range(2):
                    act.wait_ge(S["U_put"], 2 * b + s + 1)
                    f(U[:, 8 * s:8 * s + 8, :].rearrange("p g c -> p (g c)"), banks[4 + s][:, :], ACT.Copy).then_inc(S["U_kept"], 1)
                if b == 0:
                    act.wait_ge(S["u_stored"], 16)
                for j in range(4):
                    act.wait_ge(S["RT_put"], 4 * b + j + 1)
                    f(RT[:, 2 * j:2 * j + 2].rearrange("p q c x -> p (q c x)"), banks[4 + j][:, :], ACT.Copy).then_inc(S["RT_kept"], 1)
                for m in range(ML):
                    act.wait_ge(S["gproj_put"], ML * b + m + 1)
                    f(ylru[:, ML * b + m, :], banks[G_BANKS[m]][:, :], ACT.Gelu_apprx_tanh).then_inc(S["g_kept"], 1)
                for n in range(2 * ML):
                    g, m = divmod(n, ML)
                    ch = (5 + g) * MR + ML * b + m
                    act.wait_ge(S["gates_put"], 6 * b + n + 1)
                    f((rr, ii)[g][:, m, :], banks[LRU_BANKS[n]][:, :], ACT.Sigmoid, bias=chan[:, ch:ch + 1]).then_inc(S["gates_kept"], 1)
                act.drain()
                for m in range(ML):
                    ch = ML * b + m
                    f(aa[:, m, :], rr[:, m, :], ACT.Exp, scale=c_lru[:, ch:ch + 1])
                    f(th[:, m, :], rr[:, m, :], ACT.Tanh, scale=c_lru[:, MR + ch:MR + ch + 1]).then_inc(S["decay_ready"], 1)
                for m in range(ML):
                    act.wait_ge(S["mult2_ready"], ML * b + m + 1)
                    f(th[:, m, :], th[:, m, :], ACT.Sqrt).then_inc(S["mult_ready"], 1)
                act.wait_ge(S["k_stored"], 16 * (b + 1))
                for n in range(4):
                    j, h = divmod(n, 2)
                    act.wait_ge(S["Y_put"], 2 * b + j + 1)
                    f(Y2.rearrange("c l (j q h o) -> c j h q l o", j=2, q=4, h=2)[:, j, h],
                      banks[4 + 2 * h + j][0:NC, :].rearrange("c (q l o) -> c q l o", q=4, l=L),
                      ACT.Gelu_apprx_tanh).then_inc(S["Y_kept"], 1)
                for s in range(2):
                    act.wait_ge(S["yT_put"], 2 * b + s + 1)
                    f(ysT[:, 2 * b + s, :].rearrange("p (c l) -> p l c", l=L),
                      banks[4 + s][:, :].rearrange("p (l c) -> p l c", l=L), ACT.Copy).then_inc(S["yT_kept"], 1)
            for m in range(KD):
                need(act, "b_done", m - 1)
                for j in range(3):
                    act.wait_ge(S["b_val"], 5 * m + j + 1)
                    kw = {"bias": chan[:, 8 * MR + KD + m:8 * MR + KD + m + 1]} if j == 2 else {}
                    f(sg[m % 2][j], banks[(5 * m + j) % 8][:, :], ACT.Sigmoid, **kw).then_inc(S["b_sig"], 1)
            def x1_kept(t, halves):
                act.wait_ge(S["x1T_put"], t + 1)
                for h in halves:
                    f(x1T[:, 4 * h:4 * h + 4, t * P:(t + 1) * P], banks[4 + h][:, :].rearrange("p (k x) -> p k x", k=4),
                      ACT.Copy).then_inc(S["x1T_kept"], 1)

            for t in range(TT):
                act.wait_ge(S["var_ready"], t + 1)
                f(stats[:, 4 * t + 2:4 * t + 3], stats[:, 4 * t + 1:4 * t + 2], ACT.Sqrt, bias=eps_t[:, 0:1]).then_inc(S["std_ready"], 1)
                if t:
                    x1_kept(t - 1, (0, 1))
            act.wait_ge(S["pT_put"], 1)
            for c in range(2):
                f(pT[:, c, :], banks[6 + c][:, :], ACT.Copy).then_inc(S["pT_kept"], 1)
            x1_kept(TT - 1, (0,))
            act.wait_ge(S["router_put"], 1)
            f(score.rearrange("p t e -> p (t e)"), banks[6][:, 0:TT * E], ACT.Sigmoid).then_inc(S["score_ready"], 1)
            for t in range(TT):
                act.wait_ge(S["pg_biased"], 2 * t + 2)
                f(tmpd[t % 2], tmpd[t % 2], ACT.Sigmoid).then_inc(S["pg_sig"], 1)
            act.wait_ge(S["ple_done"], TT)
            for t in range(TT):
                act.wait_ge(S["sh_put"], t + 1)
                need(act, "sh_hid", t - 1)
                f(sil[t % 2], banks[4 + t % 2][:, 0:F], ACT.Silu).then_inc(S["sh_silu"], 1)
            def rows_kept(i, u):
                act.wait_ge(S["xT_e_put"], 4 * i + u + 1)
                f(xgT[u % 2][:, 0:4, :], banks[0][:, 0:4 * SL].rearrange("p (k x) -> p k x", k=4), ACT.Copy).then_inc(S["xT_e_act"], 1)

            def y_kept(i, u):
                wait(act, S["rows_added"], 64 * i + 16 * (u - 1))
                act.wait_ge(S["y_e_put"], 4 * i + u + 1)
                f(yb[u % 2][:, 0:512], banks[5][0:SL, :], ACT.Copy).then_inc(S["y_e_act"], 1)

            def expert(i, u, more=True):
                act.wait_ge(S["g_e_put"], 4 * i + u + 1)
                wait(act, S["hid_e"], 4 * i + u - 1)
                f(sil[u % 2][0:SL, :], banks[2 + u % 2][0:SL, 0:F], ACT.Silu).then_inc(S["silu_e"], 1)
                if more:
                    rows_kept(i, u + 1)
                if not isinstance(i, int) or u >= 1:
                    y_kept(i, u - 1)

            rows_kept(0, 0)
            for u in range(0, 5):
                expert(0, u)
            with act.Fori(1, E // 4 - 1) as i:
                for u in range(1, 5):
                    expert(i, u)
            for n in range(E - 3, E):
                expert(0, n, more=n + 1 < E)
            y_kept(0, E - 1)
            act.wait_ge(S["texp_ready"], 1)
            n_over = act.value_load(novi[0:1, 0:1].bitcast(i32), min_val=0, max_val=OV)
            with act.If(n_over > 0):
                with act.Fori(0, OV) as i:
                    with act.If(i < n_over):
                        act.wait_ge(S["o_xT_put"], i + 1)
                        f(xgT[0][:, 0:4, :], banks[0][:, 0:4 * SL].rearrange("p (k x) -> p k x", k=4), ACT.Copy).then_inc(S["o_xT_act"], 1)
                        act.wait_ge(S["o_g_put"], i + 1)
                        f(sil[0][0:SL, :], banks[2][0:SL, 0:F], ACT.Silu).then_inc(S["o_silu"], 1)
                    act.nop()
            for t in range(TT):
                act.wait_ge(S["var_ready"], TT + t + 1)
                f(stats[:, 4 * t + 2:4 * t + 3], stats[:, 4 * t + 1:4 * t + 2], ACT.Sqrt, bias=eps_t[:, 0:1]).then_inc(S["std_ready"], 1)

        @block.vector
        def _(dve):
            V_ = nc.vector

            def d():
                dve.drain()

            def tt(out_, a, b_, op):
                return V_.tensor_tensor(out_, a, b_, op)

            def ts(out_, a, s1, s2, op0, op1=ALU.bypass):
                return V_.tensor_scalar(out_, a, s1, s2, op0, op1)

            def stt(out_, a, s, b_, op0, op1):
                return V_.scalar_tensor_tensor(out_, a, s, b_, op0, op1)

            for t in range(TT):
                dve.wait_ge(S["xT_put"], 2 * t + 2)
                V_.tensor_copy(xT[:, 4:8, t * P:(t + 1) * P],
                               banks[2 * t + 1][:, :].rearrange("p (k x) -> p k x", k=4)).then_inc(S["xT_dve"], 1)
            dve.wait_ge(S["dt_ready"], 1)
            for h in range(2):
                hs = slice(h * NS, (h + 1) * NS)
                ts(p_dar[:, hs], p_are[:, hs], ldt[:, 2 + h:3 + h], None, ALU.mult)
                ts(p_ph[:, hs], p_aim[:, hs], ldt[:, 2 + h:3 + h], None, ALU.mult)
            d()
            dve.sem_inc(S["dar_ready"], 1)
            ts(p_t0, p_ph, 1.0 / TWO_PI, MAGIC, ALU.mult, ALU.add)
            d()
            ts(p_t0, p_t0, -MAGIC, None, ALU.add)
            d()
            stt(p_t1, p_t0, -C1, p_ph, ALU.mult, ALU.add)
            d()
            stt(p_t1, p_t0, -C2, p_t1, ALU.mult, ALU.add)
            d()
            stt(p_t1, p_t0, -C3, p_t1, ALU.mult, ALU.add)
            d()
            ts(p_t1, p_t1, PI_IN, -PI_IN, ALU.min, ALU.max)
            d()
            stt(sm[:, 1, :], p_t1, -1.0, p_t1, ALU.mult, ALU.max)
            d()
            ts(sm[:, 1, :], sm[:, 1, :], -1.0, math.pi / 2, ALU.mult, ALU.add).then_inc(S["dar_ready"], 1)
            dve.wait_ge(S["rows_put"], 1)
            V_.tensor_copy(chan, banks[0][:, 0:112])
            V_.tensor_copy(dT, banks[0][0:GP, P:P + G])
            d()
            lam = chan[:, 7 * MR:8 * MR]
            stt(lnt[:, 0:MR], lam, -1.0, lam, ALU.mult, ALU.max)
            d()
            dve.sem_inc(S["rows_kept"], 1)
            ex, w1, w2, w3, w4 = (lnt[:, n * MR:(n + 1) * MR] for n in (1, 2, 3, 4, 5))
            dve.wait_ge(S["lru_exp"], 1)
            ts(w1, ex, 2.0, None, ALU.add)
            d()
            V_.reciprocal(w2, w1)
            d()
            tt(w1, ex, w2, ALU.mult)
            d()
            tt(w2, w1, w1, ALU.mult)
            V_.memset(w3, 1.0 / 17)
            d()
            for n in range(15, 0, -2):
                tt(w3, w3, w2, ALU.mult)
                d()
                ts(w3, w3, 1.0 / n, None, ALU.add)
                d()
            stt(w3, w3, 2.0, w1, ALU.mult, ALU.mult)
            ts(w4, lam, -1.0, 0.0, ALU.mult, ALU.max)
            d()
            tt(w3, w3, w4, ALU.add)
            d()
            ts(c_lru[:, 0:MR], w3, -8.0, None, ALU.mult)
            ts(c_lru[:, MR:2 * MR], w3, 8.0, None, ALU.mult).then_inc(S["lru_c_ready"], 1)
            for c in (0, 2):
                dve.wait_ge(S["bc_put"], c + 1)
                V_.tensor_copy((bT if c < 2 else cT)[:, 0].rearrange("p j q -> p (j q)"), banks[1 + c][:, :]).then_inc(S["bc_kept"], 1)
            dve.wait_ge(S["bc_kept"], 4)
            dve.wait_ge(S["polar_ready"], 2)
            sin, cos = sm[:, 2, :], sm[:, 3, :]
            tt(pr[:, 1, 0, :], p_mg, cos, ALU.mult)
            tt(pr[:, 1, 1, :], p_mg, sin, ALU.mult)
            tt(sm[:, 5, :], p_are, p_are, ALU.mult)
            tt(sm[:, 6, :], p_aim, p_aim, ALU.mult)
            d()
            ts(sm[:, 4, :], pr[:, 1, 0, :], -1.0, None, ALU.add)
            tt(sm[:, 5, :], sm[:, 5, :], sm[:, 6, :], ALU.add)
            d()
            V_.reciprocal(sm[:, 6, :], sm[:, 5, :])
            tt(sm[:, 8, :], sm[:, 4, :], p_are, ALU.mult)
            tt(sm[:, 9, :], pr[:, 1, 1, :], p_aim, ALU.mult)
            tt(sm[:, 10, :], pr[:, 1, 1, :], p_are, ALU.mult)
            tt(sm[:, 11, :], sm[:, 4, :], p_aim, ALU.mult)
            d()
            tt(sm[:, 8, :], sm[:, 8, :], sm[:, 9, :], ALU.add)
            tt(sm[:, 10, :], sm[:, 10, :], sm[:, 11, :], ALU.subtract)
            d()
            tt(sm[:, 8, :], sm[:, 8, :], sm[:, 6, :], ALU.mult)
            tt(sm[:, 10, :], sm[:, 10, :], sm[:, 6, :], ALU.mult)
            for _ in range(3):
                tt(sm[:, 0, :], cos, cos, ALU.mult)
                tt(sm[:, 1, :], sin, sin, ALU.mult)
                tt(sm[:, 4, :], cos, sin, ALU.mult)
                d()
                tt(cos, sm[:, 0, :], sm[:, 1, :], ALU.subtract)
                ts(sin, sm[:, 4, :], 2.0, None, ALU.mult)
                d()
            for n in (1, 2, 4):
                src, one = pr[:, 1:n + 1], pr[:, n]
                x, y = (tA[0:NQ, k * 512:k * 512 + n * P].rearrange("q (j x) -> q j x", j=n) for k in range(2))
                cr, ci = bc(one[:, 0, :], 1, n), bc(one[:, 1, :], 1, n)
                dst = pr[:, n + 1:2 * n + 1]
                for c, (f0, f1, op) in enumerate(((cr, ci, ALU.subtract), (ci, cr, ALU.add))):
                    tt(pq0[:, 0:n], src[:, :, 0, :], f0, ALU.mult)
                    tt(pq1[:, 0:n], src[:, :, 1, :], f1, ALU.mult)
                    d()
                    tt(dst[:, :, c, :], pq0[:, 0:n], pq1[:, 0:n], op)
                    d()
            dve.sem_inc(S["powers_ready"], 1)
            dve.wait_ge(S["powers_put"], 1)
            V_.tensor_copy(pw[:, 1:L + 1].rearrange("p j c q -> p (j c q)"), banks[5][:, :])
            V_.tensor_copy(misc.rearrange("p v q -> p (v q)"), banks[6][:, 0:5 * NQ])
            V_.memset(pw[:, 0, 0, :], 1.0)
            V_.memset(pw[:, 0, 1, :], 0.0)
            d()
            dve.sem_inc(S["powers_kept"], 1)
            zr, zi = bc(misc[:, 0, :], 1, GP), bc(misc[:, 1, :], 1, GP)
            w = [at(tmp_off + n * 512, 512).rearrange("p (j q) -> p j q", j=GP) for n in range(4)]
            tt(w[0], bT[:, 0], zr, ALU.mult)
            tt(w[1], bT[:, 1], zi, ALU.mult)
            tt(w[2], bT[:, 1], zr, ALU.mult)
            tt(w[3], bT[:, 0], zi, ALU.mult)
            d()
            tt(bT[:, 0], w[0], w[1], ALU.subtract)
            tt(bT[:, 1], w[2], w[3], ALU.add)
            d()

            def tables(b):
                qs = slice(b * QB, (b + 1) * QB)
                need(dve, "k_stored", 16 * b)
                if b == 0:
                    dve.wait_ge(S["xT_put"], 2 * TT)
                x, y = (tm.rearrange("p (q j o) -> p q j o", q=QB, j=L + 1) for tm in (tA, tB))
                x8, y8 = (at(o, QB * P).rearrange("p (q l o) -> p q l o", q=QB, l=L) for o in (tmp_off, tmp_off + tq))
                Rv = R.rearrange("p c q (l o) -> p c q l o", l=L)
                bb = [bT[:, c, :, qs].rearrange("p o q -> p q o") for c in range(2)]
                for c, (c0, c1, op) in enumerate(((0, 1, ALU.subtract), (1, 0, ALU.add))):
                    for l in range(L):
                        pv = [bc(pw[:, L - 1 - l, k, qs], 2, GP) for k in range(2)]
                        tt(x8[:, :, l, :], bb[0], pv[c0], ALU.mult)
                        tt(y8[:, :, l, :], bb[1], pv[c1], ALU.mult)
                    d()
                    ins = tt(Rv[:, c], x8, y8, op)
                    d()
                ins = None
                dve.sem_inc(S["R_ready"], 1)
                need(dve, "Y_put", 2 * b)
                cc = [cT[:, c, :, qs].rearrange("p o q -> p q o") for c in range(2)]
                for c in range(2):
                    for j in range(L + 1):
                        pv = [bc(pw[:, j, k, qs], 2, GP) for k in range(2)]
                        tt(x[:, :, j, :], cc[0], pv[c], ALU.mult)
                        tt(y[:, :, j, :], cc[1], pv[1 - c], ALU.mult)
                    d()
                    if c == 0:
                        tt(Q[:, 0], x, y, ALU.subtract)
                    else:
                        stt(Q[:, 1].rearrange("p q j o -> p (q j o)"), tA, -1.0, tB, ALU.mult, ALU.subtract)
                    d()
                dve.sem_inc(S["Q_ready"], 1)
                V_.memset(Et[:, 0, :, 0:1], 1.0)
                V_.memset(Et[:, 1, :, 0:1], 0.0)
                V_.tensor_copy(V[:, 0, :], misc[:, 3, qs])
                V_.tensor_copy(V[:, 1, :], misc[:, 4, qs])
                V_.tensor_copy(mag, bc(misc[:, 2, qs], 2, NC))
                d()
                V_.memset(mag[:, :, 0:1], 0.0)
                n = 1
                while n < NC:
                    vr, vi = bc(V[:, 0, :], 2, n), bc(V[:, 1, :], 2, n)
                    a0, a1, a2, a3 = (t5[k][:, :, 0:n] for k in range(4))
                    tt(a0, Et[:, 0, :, 0:n], vr, ALU.mult)
                    tt(a1, Et[:, 1, :, 0:n], vi, ALU.mult)
                    tt(a2, Et[:, 0, :, 0:n], vi, ALU.mult)
                    tt(a3, Et[:, 1, :, 0:n], vr, ALU.mult)
                    if 2 * n < NC:
                        tt(V[:, 2, :], V[:, 0, :], V[:, 1, :], ALU.mult)
                        tt(V[:, 3, :], V[:, 1, :], V[:, 1, :], ALU.mult)
                    d()
                    tt(Et[:, 0, :, n:2 * n], a0, a1, ALU.subtract)
                    tt(Et[:, 1, :, n:2 * n], a2, a3, ALU.add)
                    if 2 * n < NC:
                        tt(V[:, 0, :], V[:, 0, :], V[:, 0, :], ALU.mult)
                        ts(V[:, 1, :], V[:, 2, :], 2.0, None, ALU.mult)
                        d()
                        tt(V[:, 0, :], V[:, 0, :], V[:, 3, :], ALU.subtract)
                    d()
                    n *= 2
                V_.memset(hp[:, :, :, 0:1].rearrange("p c q o -> p (c q) o"), 0.0)
                d()

            tables(0)
            for b in range(NB):
                for m in range(ML):
                    ch = ML * b + m
                    dve.wait_ge(S["conv_begun"], ch + 1)
                    for s in range(1, 4):
                        wc = (3 - s) * MR + ch
                        ins = stt(xc[:, m, s:], banks[m][:, 0:T - s], chan[:, wc:wc + 1], xc[:, m, s:], ALU.mult, ALU.add)
                        if s < 3:
                            d()
                    ins.then_inc(S["conv_done"], 1)
                dve.wait_ge(S["RT_put"], 4 * (b + 1))
                dve.wait_ge(S["U_put"], 2 * (b + 1))
                V_.memset(Kp[:, :, 0:(L - 1) * GP], 0.0)
                tt(dI, bc(ident[0:GP, 0:GP], 1, GB), bc(dT[:, b * GB:(b + 1) * GB], 2, GP), ALU.mult)
                for n in range(4):
                    j, h = divmod(n, 2)
                    dve.wait_ge(S["K_put"], 2 * b + j + 1)
                    V_.tensor_copy(Kp.rearrange("p (j q h) x -> p j q h x", q=4, h=2)[:, j, :, h, (L - 1) * GP:],
                                   banks[4 + 2 * h + j][0:GP, :].rearrange("p (q x) -> p q x", q=4))
                d()
                tt(Kp[:, :, (L - 1) * GP:L * GP], Kp[:, :, (L - 1) * GP:L * GP], dI, ALU.add).then_inc(S["K_ready"], 1)
                dve.wait_ge(S["S_put"], b + 1)
                sr, si = (banks[4 + c][:, :].rearrange("p (q n) -> p q n", q=QB) for c in range(2))
                er, ei = Et[:, 0], Et[:, 1]
                a0, a1, a2, a3 = t5
                tt(a0, er, sr, ALU.mult)
                tt(a1, ei, si, ALU.mult)
                tt(a2, er, si, ALU.mult)
                tt(a3, ei, sr, ALU.mult)
                d()
                tt(a0, a0, a1, ALU.add)
                tt(a2, a2, a3, ALU.subtract)
                d()
                flat = [v.rearrange("p q n -> p (q n)") for v in (mag, a0, a1, a2, a3)]
                V_.tensor_tensor_scan(flat[2], flat[0], flat[1], 0.0, ALU.mult, ALU.add)
                V_.tensor_tensor_scan(flat[4], flat[0], flat[3], 0.0, ALU.mult, ALU.add)
                d()
                hr, hi = hp[:, 0, :, 1:NC + 1], hp[:, 1, :, 1:NC + 1]
                tt(a0, er, a1, ALU.mult)
                tt(a2, ei, a3, ALU.mult)
                d()
                tt(hr, a0, a2, ALU.subtract)
                d()
                tt(a0, er, a3, ALU.mult)
                tt(a2, ei, a1, ALU.mult)
                d()
                tt(hi, a0, a2, ALU.add).then_inc(S["h_ready"], 1)
                for m in range(ML):
                    ch = ML * b + m
                    dve.wait_ge(S["square_ready"], ch + 1)
                    stt(th[:, m], rr[:, m], 1.0, th[:, m], ALU.add, ALU.mult).then_inc(S["mult2_ready"], 1)
                for m in range(ML):
                    ch = ML * b + m
                    dve.wait_ge(S["mult_ready"], ch + 1)
                    dve.wait_ge(S["ix_ready"], ch + 1)
                    V_.memset(th[:, m, 0:1], 1.0)
                    d()
                    tt(ii[:, m], ii[:, m], th[:, m], ALU.mult)
                    d()
                    V_.tensor_tensor_scan(rr[:, m], aa[:, m], ii[:, m], 0.0, ALU.mult, ALU.add)
                    d()
                    dve.wait_ge(S["g_kept"], ch + 1)
                    tt(ylru[:, ch], ylru[:, ch], rr[:, m], ALU.mult).then_inc(S["lru_done"], 1)
                if b + 1 < NB:
                    tables(b + 1)
            for m in range(KD):
                s = sg[m % 2]
                dve.wait_ge(S["b_sig"], 3 * m + 3)
                dve.wait_ge(S["b_val"], 5 * m + 4)
                stt(s[3], banks[(5 * m + 3) % 8][:, :], chan[:, 8 * MR + m:8 * MR + m + 1], s[2], ALU.add, ALU.mult)
                dve.wait_ge(S["b_val"], 5 * m + 5)
                tt(s[4], banks[(5 * m + 4) % 8][:, :], s[0], ALU.mult)
                d()
                tt(s[3], s[3], s[1], ALU.mult)
                d()
                tt(merged[:, m], s[3], s[4], ALU.add).then_inc(S["b_done"], 1)

            def moments(v, t):
                bs = lnt[:, 12 * t:12 * t + 12]
                for h in range(2):
                    V_.bn_stats(bs[:, 6 * h:6 * h + 6], v[:, h * 512:(h + 1) * 512])
                d()
                V_.bn_aggr(stats[:, 4 * t:4 * t + 2], bs).then_inc(S["var_ready"], 1)

            def scale(v, t, gb, n):
                dve.wait_ge(S["std_ready"], n)
                V_.reciprocal(stats[:, 4 * t + 3:4 * t + 4], stats[:, 4 * t + 2:4 * t + 3])
                d()
                ts(v, v, stats[:, 4 * t:4 * t + 1], stats[:, 4 * t + 3:4 * t + 4], ALU.subtract, ALU.mult)
                d()
                return tt(v, v, lnp[:, gb, :], ALU.mult)

            dve.wait_ge(S["xtok_loaded"], 16)
            dve.wait_ge(S["lnp_loaded"], 16 * 6)
            for t in range(TT):
                for hf in range(2):
                    n = 2 * t + hf
                    hs = slice(hf * 512, (hf + 1) * 512)
                    dve.wait_ge(S["res_put"], n + 1)
                    stt(x1[:, t, hs], xtok[:, t, hs], ALPHA, banks[n % 4][:, :], ALU.mult, ALU.add).then_inc(S["res_added"], 1)
                d()
                moments(x1[:, t, :], t)
                scale(x1[:, t, :], t, 0, t + 1)
                d()
                tt(x1[:, t, :], x1[:, t, :], lnp[:, 1, :], ALU.add).then_inc(S["x1_ready"], 1)
            dve.wait_ge(S["x1T_put"], TT)
            V_.tensor_copy(x1T[:, 4:8, (TT - 1) * P:T], banks[5][:, :].rearrange("p (k x) -> p k x", k=4)).then_inc(S["x1T_kept"], 1)
            dve.wait_ge(S["score_ready"], 1)
            dve.wait_ge(S["const_ready"], 2)
            tt(biased, score, bc(rbias, 1, TT), ALU.add)
            d()
            for t in range(TT):
                for g in range(EG):
                    V_.max(gtop[:, t * EG + g, :], biased[:, t, g * 8:(g + 1) * 8])
            d()
            tt(gsum.rearrange("p t g -> p (t g)").unsqueeze(2), gtop[:, :, 0:1], gtop[:, :, 1:2], ALU.add)
            d()
            for t in range(TT):
                mine, other = bc(gsum[:, t, :], 2, EG), bc(gsum[:, t, :], 1, EG)
                tt(pair[:, t], other, mine, ALU.is_gt)
                tt(pair2[:, t], other, mine, ALU.is_equal)
            d()
            tt(pair2, pair2, bc(lt, 1, TT), ALU.mult)
            d()
            tt(pair, pair, pair2, ALU.add)
            d()
            V_.tensor_reduce(gsel, pair, AX, ALU.add)
            d()
            ts(gsel, gsel, TOPG - 0.5, None, ALU.is_lt)
            d()
            gb_ = bc(gsel, 3, 8).rearrange("p t g x -> p (t g) x")
            m8 = lambda v: v.rearrange("p t (g x) -> p (t g) x", g=EG)
            tt(m8(biased), m8(biased), gb_, ALU.mult)
            ts(gsum, gsel, BIG, -BIG, ALU.mult, ALU.add)
            d()
            tt(m8(biased), m8(biased), bc(gsum, 3, 8).rearrange("p t g x -> p (t g) x"), ALU.add)
            d()
            for t in range(TT):
                V_.max(top8[:, t, :], biased[:, t, :])
            d()
            for t in range(TT):
                V_.match_replace(repl[:, t, :], top8[:, t, :], biased[:, t, :], -3 * BIG)
                V_.max_index(idx8[:, t, :].bitcast(u32), top8[:, t, :], biased[:, t, :])
            d()
            ts(mask, repl, -2 * BIG, None, ALU.is_lt)
            V_.tensor_copy(idx8f, idx8.bitcast(u32))
            d()
            dve.sem_inc(S["mask_ready"], 1)

            def ple(t):
                v = tmpd[t % 2]
                for hf in range(2):
                    hs = slice(hf * 512, (hf + 1) * 512)
                    dve.wait_ge(S["ple_put"], 2 * t + hf + 1)
                    tt(v[:, hs], banks[hf][:, :], lnp[:, 4, hs], ALU.add).then_inc(S["pg_biased"], 1)
                dve.wait_ge(S["pg_sig"], t + 1)
                dve.wait_ge(S["ple_val"], t + 1)
                for hf in range(2):
                    hs = slice(hf * 512, (hf + 1) * 512)
                    tt(v[:, hs], v[:, hs], banks[2 + hf][:, :], ALU.mult)
                d()
                stt(acc[:, t, :], x1[:, t, :], ALPHA, v, ALU.mult, ALU.add).then_inc(S["ple_done"], 1)

            dve.wait_ge(S["padded"], 32)
            ple(0)
            ple(1)
            dve.wait_ge(S["rank_put"], 1)
            ranks = banks[7][:, 0:TT * E].rearrange("p (t e) -> p t e", t=TT)
            V_.tensor_copy(row, ranks)
            V_.tensor_copy(cnt, banks[7][:, TT * E:(TT + 1) * E])
            d()
            ts(ovc, cnt, SL + 0.5, None, ALU.is_gt)
            ts(repl, row, SL - 0.5, None, ALU.is_gt)
            d()
            for n in range(2, LEVELS + 1):
                ts(cbase, cnt, n * SL + 0.5, None, ALU.is_gt)
                d()
                tt(ovc, ovc, cbase, ALU.add)
                d()
            V_.tensor_tensor_scan(ovi, ones_e, ovc, 0.0, ALU.mult, ALU.add)
            d()
            tt(cbase, ovi, ovc, ALU.subtract)
            V_.tensor_copy(novi.bitcast(i32), ovi[:, E - 1:E])
            for h in range(2):
                tt(texw, bc(ovi[0:1, :], 1, 24), bc(iota_i[0:1, 24 * h:24 * h + 24], 2, E), ALU.is_le)
                d()
                V_.tensor_reduce(texpf[0:1, 24 * h:24 * h + 24], texw, AX, ALU.add)
                d()
            ts(cbase, cbase, float(SL), float((E - 1) * SL), ALU.mult, ALU.add)
            d()
            tt(cbase, cbase, e128, ALU.subtract)
            ts(texpf[0:1, :], texpf[0:1, :], float(E - 1), None, ALU.min)
            d()
            tt(repl, repl, bc(cbase, 1, TT), ALU.mult)
            V_.tensor_copy(texpi[0:1, :].bitcast(i32), texpf[0:1, :])
            tt(row, row, bc(e128, 1, TT), ALU.add)
            d()
            dve.sem_inc(S["texp_ready"], 1)
            tt(row, row, repl, ALU.add)
            for t in range(TT):
                tt(eqt[:, t], bc(iota_e, 1, K), bc(idx8f[:, t, :], 2, E), ALU.is_equal)
            d()
            for t in range(TT):
                tt(eqp[:, t], eqt[:, t], bc(row[:, t, :], 1, K), ALU.mult)
            d()
            V_.tensor_reduce(slotf, eqp, AX, ALU.add)
            d()
            V_.tensor_copy(sloti.bitcast(i32), slotf)
            for t in range(TT):
                tt(eqp[:, t], eqt[:, t], bc(score[:, t, :], 1, K), ALU.mult)
            d()
            V_.tensor_reduce(gate, eqp, AX, ALU.add)
            d()
            V_.tensor_reduce(gsc, gate, AX, ALU.add)
            d()
            V_.reciprocal(gsc, gsc)
            d()
            for t in range(TT):
                ts(pairs[:, t, :, 1], gate[:, t, :], gsc[:, t:t + 1], SCALE, ALU.mult, ALU.mult)
            d()
            dve.sem_inc(S["slot_ready"], 1)
            ple(2)
            ple(3)
            def tables_kept():
                dve.wait_ge(S["tokT_put"], 1)
                V_.tensor_copy(gateT, banks[1][0:SL, P:P + NT])
                V_.tensor_copy(idxT.bitcast(i32), banks[1][0:SL, 0:NT])
                d()
                dve.sem_inc(S["idx_ready"], 1)

            for t in range(TT + 1):
                if t < TT:
                    dve.wait_ge(S["sh_silu"], t + 1)
                    if t >= 2:
                        dve.wait_ge(S["sh_hT_put"], t - 1)
                    tt(hdn[t % 2], sil[t % 2], banks[4 + t % 2][:, F:2 * F], ALU.mult).then_inc(S["sh_hid"], 1)
                if t:
                    s = t - 1
                    if s == TT - 1:
                        tables_kept()
                    dve.wait_ge(S["sh_hT_put"], s + 1)
                    V_.tensor_copy(hT[s % 2], banks[0][:, 0:F].rearrange("p (k x) -> p k x", k=2)).then_inc(S["sh_hT"], 1)
                    dve.wait_ge(S["sh_y_put"], s + 1)
                    for hf in range(2):
                        hs = slice(hf * 512, (hf + 1) * 512)
                        ins = tt(acc[:, s, hs], acc[:, s, hs], banks[6 + hf][:, :], ALU.add)
                    ins.then_inc(S["sh_done"], 1)
            def rows_kept(i, u):
                dve.wait_ge(S["xT_e_put"], 4 * i + u + 1)
                V_.tensor_copy(xgT[u % 2][:, 4:8, :], banks[1][:, 0:4 * SL].rearrange("p (k x) -> p k x", k=4)).then_inc(S["xT_e_dve"], 1)

            def y_kept(i, u):
                wait(dve, S["rows_added"], 64 * i + 16 * (u - 1))
                dve.wait_ge(S["y_e_put"], 4 * i + u + 1)
                V_.tensor_copy(yb[u % 2][:, 512:1024], banks[6][0:SL, :]).then_inc(S["y_e_dve"], 1)

            def expert(i, u, more=True):
                dve.wait_ge(S["silu_e"], 4 * i + u + 1)
                stt(hdn[u % 2][0:SL, :], sil[u % 2][0:SL, :], gateT[:, bass.ds(4 * i + u, 1)],
                    banks[2 + u % 2][0:SL, F:2 * F], ALU.mult, ALU.mult).then_inc(S["hid_e"], 1)
                if more:
                    rows_kept(i, u + 1)
                if not isinstance(i, int) or u >= 1:
                    y_kept(i, u - 1)
                dve.wait_ge(S["hT_e_put"], 4 * i + u + 1)
                V_.tensor_copy(hT[u % 2][:, :, 0:SL], banks[4][:, 0:2 * SL].rearrange("p (k x) -> p k x", k=2)).then_inc(S["hT_e_kept"], 1)

            rows_kept(0, 0)
            for u in range(0, 5):
                expert(0, u)
            with dve.Fori(1, E // 4 - 1) as i:
                for u in range(1, 5):
                    expert(i, u)
            for n in range(E - 3, E):
                expert(0, n, more=n + 1 < E)
            y_kept(0, E - 1)
            dve.wait_ge(S["rows_added"], 16 * E)
            dve.sem_inc(S["o_y_kept"], 1)
            n_over = dve.value_load(novi[0:1, 0:1].bitcast(i32), min_val=0, max_val=OV)
            with dve.If(n_over > 0):
                with dve.Fori(0, OV) as i:
                    with dve.If(i < n_over):
                        dve.wait_ge(S["o_xT_act"], i + 1)
                        V_.tensor_copy(xgT[0][:, 4:8, :], banks[1][:, 0:4 * SL].rearrange("p (k x) -> p k x", k=4)).then_inc(S["o_xT_kept"], 1)
                        dve.wait_ge(S["o_silu"], i + 1)
                        stt(hdn[0][0:SL, :], sil[0][0:SL, :], gateT[:, bass.ds(i + E, 1)], banks[2][0:SL, F:2 * F],
                            ALU.mult, ALU.mult).then_inc(S["o_hid"], 1)
                        dve.wait_ge(S["o_hT_put"], i + 1)
                        V_.tensor_copy(hT[0][:, :, 0:SL], banks[4][:, 0:2 * SL].rearrange("p (k x) -> p k x", k=2)).then_inc(S["o_hT_kept"], 1)
                        dve.wait_ge(S["o_y_put"], i + 1)
                        V_.tensor_copy(yb[0][:, 0:512], banks[5][0:SL, :])
                        V_.tensor_copy(yb[0][:, 512:1024], banks[6][0:SL, :])
                        d()
                        dve.sem_inc(S["o_y_kept"], 1)
                    dve.nop()
            for t in range(TT + 1):
                if t < TT:
                    dve.wait_ge(s_acc[t], 16)
                    moments(acc[:, t, :], t)
                if t:
                    scale(acc[:, t - 1, :], t - 1, 2, TT + t).then_inc(S["scaled"], 1)
            d()
            tt(acc[:, TT - 1, :], acc[:, TT - 1, :], lnp[:, 3, :], ALU.add).then_inc(S["last_ready"], 1)


def kernel(**inputs):
    import numpy as np
    import concourse.bacc as bacc
    from concourse.bass_utils import run_bass_kernel_spmd

    nc = bacc.Bacc("TRN2", target_bir_lowering=False, num_devices=1)
    arrays, args = {}, {}
    for name in INPUTS:
        a = np.ascontiguousarray(inputs[name])
        arrays[name + "_in"] = a
        args[name] = nc.dram_tensor(name + "_in", a.shape, mybir.dt.from_np(a.dtype), kind="ExternalInput").ap()
    out = nc.dram_tensor("out_dram", (1, T, D), mybir.dt.float32, kind="ExternalOutput").ap()
    decoder_layer(nc, args, out)
    r = run_bass_kernel_spmd(nc, [arrays], core_ids=[0])
    return r.results[0]["out_dram"]
```

```python
import concourse.bass as bass
from concourse import mybir
from contextlib import ExitStack
import math

P = 128
T = 512
TT = T // P
D = 1024
KD = D // P
D_RNN = 1536
MR = D_RNN // P
NB = 4
ML = MR // NB
CB = ML * P
HD = 96
G = 64
GP = 16
NS = 64
L = 8
NC = T // L
NQ = G // 2
QB = NQ // NB
GB = G // NB
E = 64
EG = 8
TOPG = 4
K = 8
F = 256
ALPHA = 2.0 ** 0.25
EPS = 1e-5
SCALE = 2.5
SL = 96
OV = (T * K - E) // SL
NT = E + OV
LEVELS = (T - 1) // SL
BIG = 1e30
TWO_PI = 2 * math.pi
MAGIC = 12582912.0
C1 = 6.28125
C2 = round((TWO_PI - C1) * 2 ** 21) / 2 ** 21
C3 = TWO_PI - C1 - C2
PI_IN = 3.1415925


INPUTS = ["x", "p", "w_in", "conv_w", "conv_b", "lru_wa", "lru_ba", "lru_wx", "lru_bx", "lru_lambda",
          "w_lru_out", "s5_a_re", "s5_a_im", "s5_b_re", "s5_b_im", "s5_c_re", "s5_c_im", "s5_d",
          "s5_log_dt", "w_glu", "b_glu", "w_out", "ln1_g", "ln1_b", "router_w", "router_bias",
          "moe_w_gate", "moe_w_up", "moe_w_down", "shared_w_gate", "shared_w_up", "shared_w_down",
          "ple_w", "ple_gate_w", "ple_gate_b", "ln2_g", "ln2_b"]


def decoder_layer(nc, A, out):
    f32 = mybir.dt.float32
    f32r = mybir.dt.float32r
    i32 = mybir.dt.int32
    u32 = mybir.dt.uint32
    ALU = mybir.AluOpType
    ACT = mybir.ActivationFunctionType
    AX = mybir.AxisListType.X

    ctx = ExitStack()
    with ctx:
        COLS = 53200
        arena = ctx.enter_context(nc.sbuf_tensor("arena", [P, COLS], f32))
        arena_at = nc.sbuf_base - 4 * COLS
        banks = [ctx.enter_context(nc.psum_tensor(f"bank{i}", [P, 512], f32)) for i in range(8)]

        def dram(name, shape, dt=f32):
            return nc.dram_tensor(name, shape, dt, kind="Internal").ap()

        u_dram = dram("u_dram", (T, D))
        k_dram = dram("k_dram", (NB, GB, GP, (2 * L - 1) * GP))
        x1_dram = dram("x1_dram", (T + SL, D))
        acc_dram = dram("acc_dram", (T + SL, D))
        slot_dram = dram("slot_dram", (NT * SL, 2))

        def sem(name):
            return ctx.enter_context(nc.semaphore(name))

        top = [0]

        def at(off, cols, rows_=P):
            assert off + cols <= COLS, (off, cols)
            return arena[0:rows_, off:off + cols]

        def new(cols, rows_=P):
            off = top[0]
            top[0] += cols
            return at(off, cols, rows_)

        def part(name, off, n, width):
            assert off % 8 == 0 and off + n * width <= COLS
            t = nc.alloc_sbuf_tensor_at(name, (P, n * width), f32r, offset=arena_at + 4 * off)
            return t[:, :].rearrange("p (k t) -> p k t", k=n)

        def tile_parts(name, offs):
            return [part(f"{name}{k}", o, 1, T)[:, 0] for k, o in enumerate(offs)]

        ident = new(P)
        ones = new(P)
        strict = new(P)
        chan = new(112)
        c_lru = new(2 * MR)
        lnt = new(8 * MR)
        eps_t = new(8)
        x_off = top[0]
        xT = new(KD * T).rearrange("p (k t) -> p k t", k=KD)
        late = top[0]
        xH = tile_parts("x_high", [late + k * T for k in range(KD)])
        xL = tile_parts("x_low", [x_off + k * T for k in range(KD)])
        new(KD * T)

        ylru_off = top[0]
        ylru = new(MR * T).rearrange("p (m t) -> p m t", m=MR)
        ys_off = top[0]
        ysT = new(KD * T).rearrange("p (m t) -> p m t", m=KD)
        mid = top[0]
        wa_at = [mid + m * 2 * KD * P for m in range(ML)]
        new(ML * 2 * KD * P)
        wa = [at(o, KD * P).rearrange("p (k c) -> p k c", k=KD) for o in wa_at]
        wa_lo = [part(f"wa_low{n}", o, KD, P) for n, o in enumerate(wa_at)]
        wa_hi = [part(f"wa_high{n}", o + KD * P, KD, P) for n, o in enumerate(wa_at)]
        bd = new(2 * ML * CB).rearrange("p (g k c) -> p g k c", g=2, k=ML)
        lru_off = top[0]
        xc = new(ML * T).rearrange("p (m t) -> p m t", m=ML)
        rr = new(ML * T).rearrange("p (m t) -> p m t", m=ML)
        ii = new(ML * T).rearrange("p (m t) -> p m t", m=ML)
        aa = new(ML * T).rearrange("p (m t) -> p m t", m=ML)
        s5_off = top[0]
        bT = new(2 * GP * NQ).rearrange("p (c j q) -> p c j q", c=2, j=GP)
        cT = new(2 * GP * NQ).rearrange("p (c j q) -> p c j q", c=2, j=GP)
        pw = new((L + 1) * 2 * NQ).rearrange("p (j c q) -> p j c q", j=L + 1, c=2)
        misc = new(5 * NQ).rearrange("p (v q) -> p v q", v=5)
        dT = new(G, GP)
        dI = new(GB * GP, GP).rearrange("p (g j) -> p g j", g=GB)
        qc_off = top[0]
        Q = new(2 * QB * (L + 1) * GP).rearrange("p (c q j o) -> p c q j o", c=2, q=QB, j=L + 1)
        r_off = top[0]
        R = new(2 * QB * P).rearrange("p (c q x) -> p c q x", c=2, q=QB)
        uy_off = top[0]
        U2 = at(uy_off, L * GB * GP, NC).rearrange("p (l x) -> p l x", l=L)
        Y2 = U2
        new(L * GB * GP)
        Kp = at(r_off, GB * (2 * L - 1) * GP, GP).rearrange("p (g x) -> p g x", g=GB)
        rt_off = top[0]
        RT = new(2 * QB * P).rearrange("p (q c x) -> p q c x", q=QB, c=2)
        U2g = at(top[0], GB * P, NC).rearrange("p (g x) -> p g x", g=GB)
        M = new(GB * P).rearrange("p (g x) -> p g x", g=GB)
        u_off = top[0]
        U = new(GB * NC).rearrange("p (g c) -> p g c", g=GB)
        Et = new(2 * QB * NC).rearrange("p (c q n) -> p c q n", c=2, q=QB)
        V = new(4 * QB).rearrange("p (c q) -> p c q", c=4)
        hp_off = top[0]
        hp = new(2 * QB * (NC + 1)).rearrange("p (c q n) -> p c q n", c=2, q=QB)
        mag = new(QB * NC).rearrange("p (q n) -> p q n", q=QB)
        tq = QB * (L + 1) * GP
        tmp_off = top[0]
        new(2 * tq)
        tA = at(tmp_off, tq)
        tB = at(tmp_off + tq, tq)
        t5 = [at(tmp_off + n * QB * NC, QB * NC).rearrange("p (q n) -> p q n", q=QB) for n in range(4)]
        wu = at(ylru_off, KD * D).rearrange("p (k c) -> p k c", k=KD)
        xtok0 = at(r_off, TT * D).rearrange("p (t d) -> p t d", t=TT)
        usb = at(rt_off, TT * D).rearrange("p (t d) -> p t d", t=TT)
        braw = at(lru_off, 2 * NS * 2 * GP, NQ).rearrange("p (c x j) -> p c x j", c=2, j=GP)
        craw = [at(o, GP * P, NQ).rearrange("p (j x) -> p j x", j=GP) for o in (lru_off + 4096, ylru_off + 8192)]
        rows = at(tmp_off, P, 112)
        drow = at(tmp_off + P, GP, G)
        s_base = u_off
        p_are, p_aim, p_dar, p_ph, p_mg, p_t0, p_t1 = (at(s_base + n * P, P, NQ) for n in range(7))
        pr = at(qc_off, (L + 1) * 2 * P, NQ).rearrange("p (j c x) -> p j c x", j=L + 1, c=2)
        sm = at(tmp_off + 256, 12 * P, NQ).rearrange("p (v x) -> p v x", v=12)
        ldt = at(tmp_off + 256 + 12 * P, 4, NQ)


        pq0, pq1 = (at(o, 4 * P, NQ).rearrange("q (j x) -> q j x", j=4) for o in (hp_off, hp_off + 512))
        PB = 2 * MR * P
        WB = 4 * KD * 2 * P + MR * 2 * P
        b0 = late + (MR + KD) * T
        b1 = b0 + WB
        m_off = b0 + 2 * WB
        merged = at(m_off, KD * T).rearrange("p (m t) -> p m t", m=KD)
        sg_off = m_off + KD * T
        sg = [[at(sg_off + (5 * n + j) * T, T) for j in range(5)] for n in range(2)]
        tail = sg_off + 10 * T
        wb_at = [mid, mid + PB, tail, tail + PB]
        wb = [at(o, MR * P).rearrange("p (k c) -> p k c", k=MR) for o in wb_at]
        wb_lo = [part(f"wb_low{n}", o, MR, P) for n, o in enumerate(wb_at)]
        wb_hi = [part(f"wb_high{n}", o + MR * P, MR, P) for n, o in enumerate(wb_at)]
        lH_off = mid + 2 * PB
        lH = tile_parts("lru_high", [lH_off + k * T for k in range(MR)])
        lL = tile_parts("lru_low", [ylru_off + k * T for k in range(MR)])
        yH = tile_parts("s5_high", [s5_off + k * T for k in range(KD - 1)] + [lH_off + MR * T])
        yL = tile_parts("s5_low", [ys_off + k * T for k in range(KD)])

        x1 = at(tail, TT * D).rearrange("p (t d) -> p t d", t=TT)
        x1T = at(late + 4096, KD * T).rearrange("p (k t) -> p k t", k=KD)
        plew = at(late + 8192, 2 * D).rearrange("p (k c) -> p k c", k=2)
        wout = at(x_off, KD * D).rearrange("p (k c) -> p k c", k=KD)
        pleg = at(b1, KD * D).rearrange("p (k c) -> p k c", k=KD)
        ptok = at(b1 + 8192, TT * 2 * P).rearrange("p (t c) -> p t c", t=TT)
        pT = at(b1 + 9216, 2 * T).rearrange("p (k t) -> p k t", k=2)
        tmpd = [at(b1 + 10240, D), at(tail + 4096, D)]
        acc = at(m_off, TT * D).rearrange("p (t d) -> p t d", t=TT)
        lnp = at(sg_off, 5 * D).rearrange("p (v d) -> p v d", v=5)
        wrt = at(tail + 5120, KD * E).rearrange("p (k e) -> p k e", k=KD)
        gu = [at(o, KD * 2 * F).rearrange("p (k w f) -> p k w f", k=KD, w=2)
              for o in (b1, tail, late + 4096, b0)]
        dn = [at(o, 2 * D).rearrange("p (k c) -> p k c", k=2)
              for o in (b1 + 4096, b0 + 6144, b1 + 6144, b0 + 4096)]
        xg = [at(late + n * D, D, SL) for n in range(4)]
        xgT = [at(b1 + 8192 + n * KD * SL, KD * SL).rearrange("p (k s) -> p k s", k=KD) for n in range(2)]
        yb = [at(late + 8192 + n * D, D, SL) for n in range(2)]
        sil = [at(tail + 4096 + n * F, F) for n in range(2)]
        hdn = [at(tail + 4608 + n * F, F) for n in range(2)]
        hT = [at(tail + 5120 + n * F, F).rearrange("p (k s) -> p k s", k=2) for n in range(2)]
        small = b0 + 8192

        def sc(off, cols, parts=P):
            return at(small + off, cols, parts)

        def te(off, n=E):
            return sc(off, TT * n).rearrange("p (t e) -> p t e", t=TT)

        stats = sc(0, 16)
        rbias = sc(16, E)
        iota_e = sc(80, E)
        score, biased, mask, row, repl = (te(144 + 256 * n) for n in range(5))
        gtop = sc(1424, TT * EG * 8).rearrange("p (g x) -> p g x", g=TT * EG)
        gsum = te(1680, EG)
        gsel = te(1712, EG)
        top8, idx8, idx8f, slotf, sloti, gate = (te(1744 + 32 * n, K) for n in range(6))
        cnt, ovc, ovi, e128, cbase, ones_e = (sc(1936 + E * n, E) for n in range(6))
        gsc = sc(2324, TT)
        novi = sc(2328, 1)
        texpf, texpi, iota_i = (sc(2336 + 48 * n, 48) for n in range(3))
        pairs = sc(2480, TT * K * 2).rearrange("p (t k v) -> p t k v", t=TT, k=K)
        lt = sc(2544, EG * EG).rearrange("p (a b) -> p a b", a=EG)
        slotR = sc(2608, SL * 2, NT).rearrange("p (s v) -> p s v", v=2)
        idxT = sc(2800, NT, SL)
        gateT = sc(2906, NT, SL)
        idxcol = sc(3012, 5, SL)
        yzero = at(tail + 4096, D, SL)
        eqt = at(b0 + 6144, TT * K * E).rearrange("p (t k e) -> p t k e", t=TT, k=K)
        eqp = at(x_off, TT * K * E).rearrange("p (t k e) -> p t k e", t=TT, k=K)
        pair = at(x_off + 2048, TT * EG * EG).rearrange("p (t a b) -> p t a b", t=TT, a=EG)
        pair2 = at(x_off + 2304, TT * EG * EG).rearrange("p (t a b) -> p t a b", t=TT, a=EG)
        texw = at(x_off + 2560, 24 * E, 1).rearrange("p (i e) -> p i e", i=24)

        s_x = [sem(f"x_tile_loaded{t}") for t in range(TT)]
        names = """ple_val wu2_loaded scaled last_ready rows_added col_seen sc_col acc_stored slot_col padded U2_turned
            b_val o_xT_act rows_loaded s5_loaded bc_loaded wu_loaded const_ready xT_put xT_act
            xT_dve rows_put rows_kept bc_put bc_kept u_put u_kept u_stored dar_ready polar_ready
            powers_ready powers_put powers_kept lru_c_ready high_ready low_ready w_high w_split
            K_kept u2_loaded bd_loaded bd_zeroed U_put U_kept xproj_put conv_begun conv_done R_ready
            RT_put RT_kept gproj_put g_kept Q_ready K_put K_ready k_stored M_loaded S_put h_ready
            gates_put gates_kept decay_ready square_ready ix_ready mult2_ready mult_ready lru_done
            Y_put Y_kept yT_put yT_kept b_sig b_done wout_loaded lnp_loaded pleg_loaded ple_loaded
            shared_loaded tab_zeroed res_put res_added var_ready std_ready x1_ready x1_stored
            x1T_put x1T_kept pT_put pT_kept router_put score_ready mask_ready slot_ready tok_stored
            tok_loaded tokT_put idx_ready ple_put pg_biased pg_sig ple_done sh_put sh_silu sh_hid
            sh_hT_put sh_hT sh_y_put sh_done texp_ready xT_e_put xT_e_act xT_e_dve g_e_put silu_e
            hid_e hT_e_put hT_e_kept y_e_put y_e_act y_e_dve o_w o_xT_put o_xT_kept o_g_put o_silu
            o_hid o_hT_put o_hT_kept o_y_put o_y_kept over_done out_ready out_stored""".split()
        S = {n: sem(n) for n in names}
        s_w = [sem(f"weights_loaded{n}") for n in range(4)]
        s_wgu = [sem(f"expert_in{u}") for u in range(4)]
        s_wdn = [sem(f"expert_down{u}") for u in range(4)]
        s_gath = [sem(f"rows_gathered{u}") for u in range(4)]
        s_acc = [sem(f"tile_reloaded{t}") for t in range(TT)]

        def need(eng, name, v):
            if v > 0:
                eng.wait_ge(S[name], v)

        def wait(eng, s, v):
            if not isinstance(v, int) or v > 0:
                eng.wait_ge(s, v)

        block = ctx.enter_context(nc.Block())

        def bc(ap, axis, n):
            shape = list(ap.shape)
            shape.insert(axis, n)
            return ap.unsqueeze(axis).to_broadcast(shape)

        w_in, w_glu, w_lo, w_out = A["w_in"][0], A["w_glu"][0], A["w_lru_out"][0], A["w_out"][0]
        x_tok = A["x"][0].rearrange("(t p) d -> p t d", p=P)
        w_in_k = w_in.rearrange("(p k) c -> p k c", k=KD)
        w_glu_k = w_glu.rearrange("(k p) c -> p k c", p=P)
        w_lo_k = w_lo.rearrange("(k p) c -> p k c", p=P)
        X_COL, G_COL, U_COL, GA_COL, GB_COL = 0, D_RNN, 2 * D_RNN, 2 * D_RNN + D, 2 * D_RNN + 2 * D
        PIECES = []
        for h in range(CB // HD):
            r0 = h * HD
            while r0 < (h + 1) * HD:
                n = min((h + 1) * HD, (r0 // P + 1) * P) - r0
                PIECES.append((h, r0 - h * HD, n, r0 // P, r0 % P))
                r0 += n
        PAIRS = [(k, m) for m in range(ML) for k in range(ML)
                 if any(t == k and h * HD < (m + 1) * P and (h + 1) * HD > m * P for h, _, _, t, _ in PIECES)]
        LRU_BANKS = [2, 3, 0, 1, 2, 3]
        G_BANKS = [3, 0, 1]

        @block.sync
        def _(sp):
            for t in range(TT):
                sp.dma_start(xtok0[:, t, :], x_tok[:, t, :]).then_inc(s_x[t], 16)
            srcs = [(A["conv_w"][0].rearrange("w (m p) -> (w m) p", p=P), 4 * MR)]
            srcs += [(A[n][0].rearrange("(m p) -> m p", p=P), MR) for n in ("conv_b",)]
            srcs += [(A[n][0].rearrange("h j -> (h j)").rearrange("(m p) -> m p", p=P), MR) for n in ("lru_ba", "lru_bx")]
            srcs += [(A["lru_lambda"][0].rearrange("(m p) -> m p", p=P), MR)]
            srcs += [(A["b_glu"][0].rearrange("(m p) -> m p", p=P), 2 * KD)]
            r0 = 0
            for src, n in srcs:
                sp.dma_start(rows[r0:r0 + n, :], src).then_inc(S["rows_loaded"], 16)
                r0 += n
            sp.dma_start(drow, A["s5_d"][0].rearrange("(g j) -> g j", j=GP)).then_inc(S["rows_loaded"], 16)
            sp.dma_start(p_are, A["s5_a_re"][0].rearrange("(q h) n -> q (h n)", h=2)).then_inc(S["s5_loaded"], 16)
            sp.dma_start(p_aim, A["s5_a_im"][0].rearrange("(q h) n -> q (h n)", h=2)).then_inc(S["s5_loaded"], 16)
            sp.dma_start(ldt[:, 0:2], A["s5_log_dt"][0].rearrange("(q h) -> q h", h=2)).then_inc(S["s5_loaded"], 16)
            sp.dma_start(wu[:, :, 0:512], w_in_k[:, :, U_COL:U_COL + 512]).then_inc(S["wu_loaded"], 16)
            for c, n in enumerate(("s5_b_re", "s5_b_im")):
                sp.dma_start(braw[:, c].rearrange("p x j -> p (x j)"),
                             A[n][0].rearrange("(q h) n j -> q (h n j)", h=2)).then_inc(S["bc_loaded"], 16)
            for c, n in enumerate(("s5_c_re", "s5_c_im")):
                for h in range(2):
                    sp.dma_start(craw[c][:, :, h * NS:(h + 1) * NS],
                                 A[n][0].rearrange("(q h) j n -> h q j n", h=2)[h]).then_inc(S["bc_loaded"], 16)
            sp.dma_start(wu[:, :, 512:1024], w_in_k[:, :, U_COL + 512:U_COL + 1024]).then_inc(S["wu2_loaded"], 16)

            def load_a(col, b, m):
                c0 = col + b * CB + m * P
                sp.dma_start(wa[m], w_in_k[:, :, c0:c0 + P]).then_inc(s_w[m], 16)

            def load_bd(b):
                for g, n in enumerate(("lru_wa", "lru_wx")):
                    for h, i0, cnt_, t, p0 in PIECES:
                        sp.dma_start(bd[p0:p0 + cnt_, g, t, h * HD:(h + 1) * HD],
                                     A[n][0, b * (CB // HD) + h, i0:i0 + cnt_, :]).then_inc(S["bd_loaded"], 16)

            def load_u2(b):
                sp.dma_start(U2, u_dram.rearrange("(c l) x -> c l x", l=L)[:, :, b * GB * GP:(b + 1) * GB * GP]
                             ).then_inc(S["u2_loaded"], 16)

            for m in range(ML):
                load_a(X_COL, 0, m)
            sp.wait_ge(S["bd_zeroed"], 1)
            load_bd(0)
            sp.wait_ge(S["u_kept"], 2 * TT)
            sp.dma_start(u_dram.rearrange("(t p) d -> p t d", p=P), usb).then_inc(S["u_stored"], 16)
            sp.wait_ge(S["u_stored"], 16)
            sp.wait_ge(S["const_ready"], 1)
            sp.wait_ge(S["xT_put"], 2 * TT)
            load_u2(0)
            for b in range(NB):
                for m in range(ML):
                    sp.wait_ge(S["xproj_put"], ML * b + m + 1)
                    load_a(G_COL, b, m)
                if b + 1 < NB:
                    sp.wait_ge(S["gproj_put"], ML * b + 1)
                    load_a(X_COL, b + 1, 0)
                sp.wait_ge(S["K_ready"], b + 1)
                sp.dma_start(k_dram[b].rearrange("g j x -> j g x"), Kp).then_inc(S["k_stored"], 16)
                sp.wait_ge(S["k_stored"], 16 * (b + 1))
                need(sp, "Y_put", 2 * b)
                for l in range(L):
                    sp.dma_start(M[l * GP:(l + 1) * GP],
                                 k_dram[b, :, :, (L - 1 - l) * GP:(L - 1 - l) * GP + L * GP]
                                 .rearrange("g j x -> j g x")).then_inc(S["M_loaded"], 16)
                if b + 1 < NB:
                    for m in range(1, ML):
                        sp.wait_ge(S["gproj_put"], ML * b + m + 1)
                        load_a(X_COL, b + 1, m)
                    sp.wait_ge(S["gates_put"], 2 * ML * (b + 1))
                    load_bd(b + 1)
                    sp.wait_ge(S["yT_put"], 2 * (b + 1))
                    load_u2(b + 1)

            B_SRC = ((w_in_k, GA_COL), (w_in_k, GB_COL), (w_glu_k, D), (w_glu_k, 0))

            for n in range(5 * KD):
                m, w = divmod(n, 5)
                if n == 0:
                    sp.wait_ge(S["gproj_put"], MR)
                elif n == 2:
                    sp.wait_ge(S["h_ready"], NB)
                    sp.wait_ge(S["Y_put"], 2 * NB)
                elif n >= 4:
                    sp.wait_ge(S["b_val"], n - 3)
                if w < 4:
                    src, c0 = B_SRC[w]
                    sp.dma_start(wb[n % 4][:, 0:KD], src[:, :, c0 + P * m:c0 + P * (m + 1)]).then_inc(s_w[n % 4], 16)
                else:
                    sp.dma_start(wb[n % 4], w_lo_k[:, :, P * m:P * (m + 1)]).then_inc(s_w[n % 4], 16)
            sp.wait_ge(S["b_val"], 5 * KD - 3)
            sp.dma_start(wout, w_out.rearrange("(k p) c -> p k c", p=P)).then_inc(S["wout_loaded"], 16)
            sp.wait_ge(S["b_val"], 5 * KD)
            for t in range(TT):
                sp.dma_start(x1[:, t, :], x_tok[:, t, :]).then_inc(s_x[t], 16)
            sp.dma_start(rbias, A["router_bias"][0].partition_broadcast(P)).then_inc(S["lnp_loaded"], 16)
            sp.wait_ge(S["b_done"], KD)
            for v, n in enumerate(("ln1_g", "ln1_b", "ln2_g", "ln2_b", "ple_gate_b")):
                sp.dma_start(lnp[:, v, :], A[n][0].partition_broadcast(P)).then_inc(S["lnp_loaded"], 16)
            sp.dma_start(plew, A["ple_w"][0].rearrange("(p k) c -> p k c", k=2)).then_inc(S["ple_loaded"], 16)
            sp.dma_start(ptok, A["p"][0, 0].rearrange("(t p) c -> p t c", p=P)).then_inc(S["ple_loaded"], 16)
            sp.dma_start(wrt, A["router_w"][0].rearrange("(p k) e -> p k e", k=KD)).then_inc(S["ple_loaded"], 16)
            sp.dma_start(pleg, A["ple_gate_w"][0].rearrange("(p k) c -> p k c", k=KD)).then_inc(S["pleg_loaded"], 16)
            for w, n in enumerate(("shared_w_gate", "shared_w_up")):
                sp.dma_start(gu[3][:, :, w, :], A[n][0].rearrange("(p k) f -> p k f", k=KD)).then_inc(S["shared_loaded"], 16)
            sp.dma_start(dn[3], A["shared_w_down"][0].rearrange("(p k) c -> p k c", k=2)).then_inc(S["shared_loaded"], 16)
            for t in range(TT):
                sp.wait_ge(S["x1_ready"], t + 1)
                sp.dma_start(x1_dram[t * P:(t + 1) * P, :], x1[:, t, :]).then_inc(S["x1_stored"], 16)

            w_gate_e = A["moe_w_gate"][0].rearrange("e (p k) f -> e p k f", k=KD)
            w_up_e = A["moe_w_up"][0].rearrange("e (p k) f -> e p k f", k=KD)
            w_down_e = A["moe_w_down"][0].rearrange("e (p k) c -> e p k c", k=2)

            def load_in(e, u, done):
                for w, src in enumerate((w_gate_e, w_up_e)):
                    sp.dma_start(gu[u][:, :, w, :], src[bass.ds(e, 1)].rearrange("o p k f -> p (o k) f")).then_inc(done, 16)

            def load_down(e, u, done):
                sp.dma_start(dn[u], w_down_e[bass.ds(e, 1)].rearrange("o p k c -> p (o k) c")).then_inc(done, 16)

            def load_expert(e, u, in_done, down_done):
                load_in(e, u, in_done)
                load_down(e, u, down_done)

            sp.wait_ge(S["ple_put"], 2 * TT)
            sp.wait_ge(S["ple_val"], TT)
            load_expert(0, 0, s_wgu[0], s_wdn[0])
            sp.wait_ge(S["slot_ready"], 1)
            sp.wait_ge(S["ple_done"], TT)
            sp.wait_ge(S["x1_stored"], 16 * TT)
            load_expert(1, 1, s_wgu[1], s_wdn[1])
            sp.wait_ge(S["sh_put"], TT)
            load_expert(2, 2, s_wgu[2], s_wdn[2])
            sp.wait_ge(S["sh_y_put"], TT)
            load_expert(3, 3, s_wgu[3], s_wdn[3])
            sp.wait_ge(S["sh_done"], TT)
            sp.dma_start(acc_dram[0:T, :].rearrange("(t p) d -> p t d", p=P), acc).then_inc(S["acc_stored"], 16)
            with sp.Fori(0, E // 4 - 1) as i:
                for u in range(4):
                    sp.wait_ge(S["g_e_put"], 4 * i + (u + 1))
                    load_in(4 * i + (4 + u), u, s_wgu[u])
                    sp.wait_ge(S["y_e_put"], 4 * i + (u + 1))
                    load_down(4 * i + (4 + u), u, s_wdn[u])
            sp.wait_ge(S["y_e_put"], E)
            sp.wait_ge(S["texp_ready"], 1)
            n_over = sp.value_load(novi[0:1, 0:1].bitcast(i32), min_val=0, max_val=OV)
            with sp.If(n_over > 0):
                with sp.Fori(0, OV) as i:
                    with sp.If(i < n_over):
                        e = sp.value_load(texpi[0:1, bass.ds(i, 1)].bitcast(i32), min_val=0, max_val=E - 1)
                        sp.wait_ge(S["o_y_kept"], 2 * i + 1)
                        load_expert(e, 0, S["o_w"], S["o_w"])
                    sp.nop()
            for t in range(TT):
                if t == 0:
                    sp.wait_ge(S["over_done"], 1)
                sp.dma_start(acc[:, t, :], acc_dram[t * P:(t + 1) * P, :]).then_inc(s_acc[t], 16)
            for t in range(TT):
                if t < TT - 1:
                    sp.wait_ge(S["out_ready"], t + 1)
                else:
                    sp.wait_ge(S["last_ready"], 1)
                sp.dma_start(out[0, t * P:(t + 1) * P, :], acc[:, t, :]).then_inc(S["out_stored"], 16)
            sp.wait_ge(S["out_stored"], 16 * TT)

        @block.gpsimd
        def _(pool):
            nc.gpsimd.memset(ident, 0.0)
            nc.gpsimd.memset(ones, 1.0)
            nc.gpsimd.memset(strict, 1.0)
            nc.gpsimd.memset(eps_t, EPS)
            pool.drain()
            nc.gpsimd.affine_select(out=ident, in_=ident, compare_op=ALU.not_equal, fill=1.0, base=0,
                                    pattern=[[-1, P]], channel_multiplier=1)
            nc.gpsimd.affine_select(out=strict, in_=strict, compare_op=ALU.is_gt, fill=0.0, base=0,
                                    pattern=[[1, P]], channel_multiplier=-1)
            pool.drain()
            pool.sem_inc(S["const_ready"], 1)
            nc.gpsimd.memset(bd.rearrange("p g k c -> p (g k c)"), 0.0).then_inc(S["bd_zeroed"], 1)

            def low_part(w, lo, hi, n):
                pool.wait_ge(S["w_high"], n + 1)
                nc.gpsimd.tensor_tensor(lo, w, hi.bitcast(f32), ALU.subtract).then_inc(S["w_split"], 1)

            def low_b(n):
                nk = MR if n % 5 == 4 else KD
                low_part(wb[n % 4][:, 0:nk], wb_lo[n % 4][:, 0:nk], wb_hi[n % 4][:, 0:nk], 2 * MR + n)

            for m in range(ML):
                low_part(wa[m], wa_lo[m], wa_hi[m], m)
            for b in range(NB):
                low_part(wa[0], wa_lo[0], wa_hi[0], ML * (2 * b + 1))
                pool.wait_ge(S["u2_loaded"], 16 * (b + 1))
                if b == 0:
                    pool.wait_ge(S["u_stored"], 16)
                need(pool, "Y_put", 2 * b)
                nc.gpsimd.tensor_copy(U2g.rearrange("c g (l o) -> c l g o", l=L),
                                      U2.rearrange("c l (g o) -> c l g o", g=GB)).then_inc(S["U2_turned"], 1)
                for m in range(1, ML):
                    low_part(wa[m], wa_lo[m], wa_hi[m], ML * (2 * b + 1) + m)
                pool.wait_ge(S["RT_put"], 4 * (b + 1))
                pool.wait_ge(S["U_put"], 2 * (b + 1))
                need(pool, "K_ready", b)
                nc.gpsimd.memset(Kp[:, :, 0:(L - 1) * GP], 0.0)
                nc.gpsimd.tensor_tensor(dI, bc(ident[0:GP, 0:GP], 1, GB), bc(dT[:, b * GB:(b + 1) * GB], 2, GP), ALU.mult)
                pool.drain()
                pool.sem_inc(S["K_kept"], 1)
                if b + 1 < NB:
                    low_part(wa[0], wa_lo[0], wa_hi[0], ML * (2 * b + 2))
                else:
                    low_b(0)
                for m in range(ML):
                    pool.wait_ge(S["decay_ready"], ML * b + m + 1)
                    nc.gpsimd.tensor_tensor(ii[:, m], ii[:, m], xc[:, m], ALU.mult).then_inc(S["ix_ready"], 1)
                    pool.drain()
                    nc.gpsimd.tensor_tensor(xc[:, m], aa[:, m], aa[:, m], ALU.mult).then_inc(S["square_ready"], 1)
                if b + 1 < NB:
                    for m in range(1, ML):
                        low_part(wa[m], wa_lo[m], wa_hi[m], ML * (2 * b + 2) + m)
            for n in range(1, 5 * KD):
                low_b(n)
            pool.wait_ge(S["b_val"], 5 * KD)
            nc.gpsimd.memset(ones_e, 1.0)
            nc.gpsimd.iota(iota_e, [[1, E]], base=0, channel_multiplier=0, allow_small_or_imprecise_dtypes=True)
            nc.gpsimd.iota(e128, [[SL, E]], base=0, channel_multiplier=0, allow_small_or_imprecise_dtypes=True)
            nc.gpsimd.iota(pairs[:, :, :, 0], [[P, TT], [0, K]], base=0, channel_multiplier=1,
                           allow_small_or_imprecise_dtypes=True)
            nc.gpsimd.iota(iota_i, [[1, 48]], base=0, channel_multiplier=0, allow_small_or_imprecise_dtypes=True)
            nc.gpsimd.memset(slotR, 0.0)
            nc.gpsimd.memset(yzero, 0.0)
            pool.drain()
            nc.gpsimd.iota(slotR[:, :, 0], [[1, SL]], base=T, channel_multiplier=0, allow_small_or_imprecise_dtypes=True)
            nc.gpsimd.memset(lt.rearrange("p a b -> p (a b)"), 1.0)
            pool.drain()
            nc.gpsimd.affine_select(out=lt, in_=lt, compare_op=ALU.is_gt, fill=0.0, base=0,
                                    pattern=[[1, EG], [-1, EG]], channel_multiplier=0)
            pool.drain()
            nc.gpsimd.dma_start(slot_dram.rearrange("(n s) v -> n (s v)", s=SL), slotR.rearrange("p s v -> p (s v)")
                                ).then_inc(S["tab_zeroed"], 16)
            pool.sem_inc(S["const_ready"], 1)
            pool.wait_ge(S["tab_zeroed"], 16)
            for dst in (x1_dram, acc_dram):
                nc.gpsimd.dma_start(dst[T:T + SL, :], yzero).then_inc(S["padded"], 16)
            pool.wait_ge(S["slot_ready"], 1)
            for t in range(TT):
                for k in range(K):
                    nc.gpsimd.indirect_dma_start(
                        out=slot_dram, out_offset=bass.IndirectOffsetOnAxis(ap=sloti[:, t, k:k + 1].bitcast(u32), axis=0),
                        in_=pairs[:, t, k, :], in_offset=None).then_inc(S["tok_stored"], 16)
            pool.wait_ge(S["tok_stored"], 16 * TT * K)
            nc.gpsimd.dma_start(slotR.rearrange("p s v -> p (s v)"), slot_dram.rearrange("(n s) v -> n (s v)", s=SL)
                                ).then_inc(S["tok_loaded"], 16)

            def gather(e, u, n):
                nc.gpsimd.tensor_copy(idxcol[:, u:u + 1].bitcast(i32), idxT[:, bass.ds(e, 1)].bitcast(i32)).then_inc(S["slot_col"], 1)
                pool.wait_ge(S["slot_col"], n + 1)
                pool.sem_inc(S["col_seen"], 1)
                nc.gpsimd.indirect_dma_start(
                    out=xg[u], out_offset=None, in_=x1_dram,
                    in_offset=bass.IndirectOffsetOnAxis(ap=idxcol[:, u:u + 1].bitcast(u32), axis=0)).then_inc(s_gath[u], 16)

            def add_rows(buf, e, n):
                wait(pool, S["rows_added"], 16 * n)
                pool.sem_inc(S["col_seen"], 1)
                nc.gpsimd.tensor_copy(idxcol[:, 4:5].bitcast(i32), idxT[:, bass.ds(e, 1)].bitcast(i32)).then_inc(S["sc_col"], 1)
                pool.wait_ge(S["sc_col"], n + 1)
                pool.sem_inc(S["col_seen"], 1)
                nc.gpsimd.indirect_dma_start(
                    out=acc_dram, out_offset=bass.IndirectOffsetOnAxis(ap=idxcol[:, 4:5].bitcast(u32), axis=0),
                    in_=yb[buf], in_offset=None, compute_op=ALU.add).then_inc(S["rows_added"], 16)

            pool.wait_ge(S["idx_ready"], 1)
            pool.wait_ge(S["x1_stored"], 16 * TT)
            pool.wait_ge(S["padded"], 32)
            for u in range(4):
                gather(u, u, u)
            pool.wait_ge(S["acc_stored"], 16)

            def add_expert(i, u):
                pool.wait_ge(S["y_e_act"], 4 * i + u + 1)
                pool.wait_ge(S["y_e_dve"], 4 * i + u + 1)
                add_rows(u % 2, 4 * i + u, 4 * i + u)

            for u in range(4):
                pool.wait_ge(S["xT_e_put"], u + 1)
                gather(4 + u, u, 4 + u)
                add_expert(0, u)
            with pool.Fori(1, E // 4 - 1) as i:
                for u in range(4):
                    pool.wait_ge(S["xT_e_put"], 4 * i + (u + 1))
                    gather(4 * i + (4 + u), u, 4 * i + (4 + u))
                    add_expert(i, u)
            for u in range(E - 4, E):
                add_expert(0, u)
            n_over = pool.value_load(novi[0:1, 0:1].bitcast(i32), min_val=0, max_val=OV)
            with pool.If(n_over > 0):
                with pool.Fori(0, OV) as i:
                    with pool.If(i < n_over):
                        gather(i + E, 0, i + E)
                        pool.wait_ge(S["o_y_kept"], 2 * i + 2)
                        add_rows(0, i + E, i + E)
                        pool.wait_ge(S["rows_added"], 16 * i + 16 * (E + 1))
                        pool.sem_inc(S["o_y_kept"], 1)
                    pool.nop()
            pool.wait_ge(S["rows_added"], 16 * E)
            pool.sem_inc(S["over_done"], 1)
            for t in range(TT - 1):
                pool.wait_ge(S["scaled"], t + 1)
                nc.gpsimd.tensor_tensor(acc[:, t, :], acc[:, t, :], lnp[:, 3, :], ALU.add).then_inc(S["out_ready"], 1)

        mm = nc.tensor.matmul

        def mm3(dst, w_hi, w_lo, v_hi, v_lo, start, stop):
            mm(dst, w_hi, v_hi, start=start, stop=False)
            mm(dst, w_hi, v_lo, start=False, stop=False)
            return mm(dst, w_lo, v_hi, start=False, stop=stop)

        @block.tensor
        def _(pe):
            def tp(dst, src, n):
                return nc.tensor.transpose(dst, src, ident[0:n, 0:n])

            pe.wait_ge(S["const_ready"], 1)
            for t in range(TT):
                pe.wait_ge(s_x[t], 16)
                xv = xtok0[:, t, :].rearrange("p (d k) -> p k d", k=KD)
                for h in range(2):
                    for k in range(4):
                        last = tp(banks[2 * t + h][:, k * P:(k + 1) * P], xv[:, 4 * h + k, :], P)
                    last.then_inc(S["xT_put"], 1)
            pe.wait_ge(S["rows_loaded"], 16 * 7)
            pe.wait_ge(S["xT_act"], 1)
            tp(banks[0][:, 0:112], rows, 112)
            tp(banks[0][0:GP, P:P + G], drow, G).then_inc(S["rows_put"], 1)
            pe.wait_ge(S["wu_loaded"], 16)
            pe.wait_ge(S["xT_act"], TT)
            pe.wait_ge(S["xT_dve"], TT)

            def u_proj(n):
                hf, t = divmod(n, TT)
                if n == 3:
                    pe.wait_ge(S["rows_kept"], 1)
                if n == 4:
                    pe.wait_ge(S["bc_kept"], 4)
                    pe.wait_ge(S["wu2_loaded"], 16)
                for k in range(KD):
                    last = mm(banks[(5 + n) % 8][:, :], xT[:, k, t * P:(t + 1) * P], wu[:, k, hf * 512:(hf + 1) * 512],
                              start=(k == 0), stop=(k == KD - 1))
                last.then_inc(S["u_put"], 1)

            u_proj(0)
            pe.wait_ge(S["bc_loaded"], 16 * 6)
            for c in range(4):
                for j in range(GP):
                    src = braw[:, c, :, j] if c < 2 else craw[c - 2][:, j, :]
                    last = tp(banks[1 + c][:, j * NQ:(j + 1) * NQ], src, NQ)
                last.then_inc(S["bc_put"], 1)
            for n in range(1, 2 * TT):
                u_proj(n)
            pe.wait_ge(S["powers_ready"], 1)
            pe.wait_ge(S["u_kept"], 2)
            for j in range(1, L + 1):
                for c in range(2):
                    n = 2 * (j - 1) + c
                    tp(banks[5][:, n * NQ:(n + 1) * NQ], pr[:, j, c, :], NQ)
            for n, v in enumerate((8, 10, 7, 3, 2)):
                last = tp(banks[6][:, n * NQ:(n + 1) * NQ], sm[:, v, :], NQ)
            last.then_inc(S["powers_put"], 1)

            def x_proj(b, m):
                pe.wait_ge(S["w_split"], 2 * ML * b + m + 1)
                for k in range(KD):
                    if b == 0 and m == 0:
                        pe.wait_ge(S["low_ready"], k + 1)
                    last = mm3(banks[m][:, :], wa_hi[m][:, k], wa_lo[m][:, k], xH[k], xL[k], k == 0, k == KD - 1)
                last.then_inc(S["xproj_put"], 1)

            def b_product(v):
                m, j = divmod(v, 5)
                pe.wait_ge(S["w_split"], 2 * MR + v + 1)
                if v == 0:
                    pe.wait_ge(S["gates_kept"], 6 * NB)
                if v == 2:
                    pe.wait_ge(S["yT_kept"], 2 * NB)
                if v >= 8:
                    pm, pj = divmod(v - 8, 5)
                    if pj < 3:
                        pe.wait_ge(S["b_sig"], 3 * pm + pj + 1)
                    else:
                        pe.wait_ge(S["b_done"], pm + 1)
                hi, lo = wb_hi[v % 4], wb_lo[v % 4]
                nk = MR if j == 4 else KD
                for k in range(nk):
                    if m == 0 and j in (2, 4):
                        pe.wait_ge(S["low_ready"], (KD if j == 2 else 2 * KD) + k + 1)
                    vh, vl = (xH[k], xL[k]) if j < 2 else (lH[k], lL[k]) if j == 4 else (yH[k], yL[k])
                    last = mm3(banks[v % 8][:, :], hi[:, k], lo[:, k], vh, vl, k == 0, k == nk - 1)
                last.then_inc(S["b_val"], 1)

            pe.wait_ge(S["u_kept"], 2 * TT)
            x_proj(0, 0)
            for b in range(NB):
                for m in range(1, ML):
                    x_proj(b, m)
                def g_proj(m):
                    if m:
                        pe.wait_ge(S["conv_done"], ML * b + m)
                    pe.wait_ge(S["w_split"], 2 * ML * b + ML + m + 1)
                    for k in range(KD):
                        last = mm3(banks[G_BANKS[m]][:, :], wa_hi[m][:, k], wa_lo[m][:, k], xH[k], xL[k],
                                   k == 0, k == KD - 1)
                    last.then_inc(S["gproj_put"], 1)

                g_proj(0)
                pe.wait_ge(S["U2_turned"], b + 1)
                if b == 0:
                    pe.wait_ge(S["powers_kept"], 1)
                need(pe, "yT_kept", 2 * b)
                for g in range(GB):
                    last = tp(banks[4 + g // 8][:, (g % 8) * NC:(g % 8 + 1) * NC], U2g[:, g, :], NC)
                    if g % 8 == 7:
                        last.then_inc(S["U_put"], 1)
                pe.wait_ge(S["R_ready"], b + 1)
                pe.wait_ge(S["U_kept"], 2 * (b + 1))
                need(pe, "Y_kept", 4 * b)
                for n in range(2 * QB):
                    q, c = divmod(n, 2)
                    last = tp(banks[4 + n // 4][:, (n % 4) * P:(n % 4 + 1) * P], R[:, c, q, :], P)
                    if n % 4 == 3:
                        last.then_inc(S["RT_put"], 1)
                pe.wait_ge(S["Q_ready"], b + 1)
                for g in range(GB):
                    q, h = divmod(g, 2)
                    hs = slice(h * NS, (h + 1) * NS)
                    if g == 0:
                        pe.wait_ge(S["RT_kept"], 4 * (b + 1))
                    for c in range(2):
                        last = mm(banks[4 + 2 * h + q // 4][0:GP, (q % 4) * P:(q % 4 + 1) * P], bT[hs, c, :, b * QB + q],
                                  Q[hs, c, q, 0:L, :], start=(c == 0), stop=(c == 1))
                    if g % 8 == 7:
                        last.then_inc(S["K_put"], 1)
                g_proj(1)
                pe.wait_ge(S["K_ready"], b + 1)
                for c in range(2):
                    for q in range(QB):
                        for h in range(2):
                            last = mm(banks[4 + c][h * NS:(h + 1) * NS, q * NC:(q + 1) * NC],
                                      RT[:, q, c, h * NS:(h + 1) * NS], U[:, 2 * q + h, :], start=True, stop=True)
                last.then_inc(S["S_put"], 1)
                g_proj(2)
                pe.wait_ge(S["bd_loaded"], 16 * 2 * len(PIECES) * (b + 1))
                pe.wait_ge(S["conv_done"], ML * (b + 1))
                for n in range(2 * ML):
                    g, m = divmod(n, ML)
                    if n in (1, 2, 3):
                        pe.wait_ge(S["g_kept"], ML * b + n)
                    if n > 3:
                        pe.wait_ge(S["gates_kept"], 6 * b + n - 3)
                    ks = [k for k, mt in PAIRS if mt == m]
                    for k in ks:
                        last = mm(banks[LRU_BANKS[n]][:, :], bd[:, g, k, m * P:(m + 1) * P], xc[:, k, :],
                                  start=(k == ks[0]), stop=(k == ks[-1]))
                    last.then_inc(S["gates_put"], 1)
                pe.wait_ge(S["h_ready"], b + 1)
                pe.wait_ge(S["M_loaded"], 16 * L * (b + 1))
                for g in range(GB):
                    q, h = divmod(g, 2)
                    hs = slice(h * NS, (h + 1) * NS)
                    dst = banks[4 + 2 * h + q // 4][0:NC, (q % 4) * P:(q % 4 + 1) * P]
                    mm(dst, U[:, g, :], M[:, g, :], start=True, stop=False)
                    mm(dst, hp[hs, 0, q, 0:NC], Q[hs, 0, q, 1:L + 1, :], start=False, stop=False)
                    last = mm(dst, hp[hs, 1, q, 0:NC], Q[hs, 1, q, 1:L + 1, :], start=False, stop=True)
                    if g % 8 == 7:
                        last.then_inc(S["Y_put"], 1)
                if b + 1 < NB:
                    pe.wait_ge(S["gates_kept"], 6 * (b + 1))
                    x_proj(b + 1, 0)
                else:
                    b_product(0)
                pe.wait_ge(S["Y_kept"], 4 * (b + 1))
                for s in range(2):
                    for l in range(L):
                        last = tp(banks[4 + s][:, l * NC:(l + 1) * NC], Y2[:, l, s * P:(s + 1) * P], NC)
                    last.then_inc(S["yT_put"], 1)

            for v in range(1, 5 * KD):
                b_product(v)
            def x1_turn(t):
                pe.wait_ge(S["x1_ready"], t + 1)
                if t:
                    pe.wait_ge(S["x1T_kept"], 2 * t)
                xv = x1[:, t, :].rearrange("p (d k) -> p k d", k=KD)
                for h in range(2):
                    for k in range(4):
                        last = tp(banks[4 + h][:, k * P:(k + 1) * P], xv[:, 4 * h + k, :], P)
                last.then_inc(S["x1T_put"], 1)

            def p_turn():
                pe.wait_ge(S["ple_loaded"], 48)
                for c in range(2):
                    for t in range(TT):
                        last = tp(banks[6 + c][:, t * P:(t + 1) * P],
                                  ptok[:, t, :].rearrange("p (d k) -> p k d", k=2)[:, c, :], P)
                last.then_inc(S["pT_put"], 1)

            pe.wait_ge(S["wout_loaded"], 16)
            pe.wait_ge(S["b_done"], KD - 1)
            for n in range(2 * TT):
                t, hf = divmod(n, 2)
                if n >= 4:
                    pe.wait_ge(S["res_added"], n - 3)
                for k in range(KD):
                    if n == 0 and k == KD - 1:
                        pe.wait_ge(S["b_done"], KD)
                    last = mm(banks[n % 4][:, :], merged[:, k, t * P:(t + 1) * P], wout[:, k, hf * 512:(hf + 1) * 512],
                              start=(k == 0), stop=(k == KD - 1))
                last.then_inc(S["res_put"], 1)
                if hf and t == 2:
                    p_turn()
                if hf and t:
                    x1_turn(t - 1)
            def ple_gate(t):
                for hf in range(2):
                    if t:
                        pe.wait_ge(S["pg_biased"], 2 * (t - 1) + hf + 1)
                    else:
                        pe.wait_ge(S["res_added"], 2 * TT)
                    for k in range(KD):
                        last = mm(banks[hf][:, :], x1T[:, k, t * P:(t + 1) * P], pleg[:, k, hf * 512:(hf + 1) * 512],
                                  start=(k == 0), stop=(k == KD - 1))
                    last.then_inc(S["ple_put"], 1)

            def ple_value(t):
                if t:
                    pe.wait_ge(S["ple_done"], t)
                else:
                    pe.wait_ge(S["res_added"], 2 * TT)
                    pe.wait_ge(S["pT_kept"], 2)
                for hf in range(2):
                    for k in range(2):
                        last = mm(banks[2 + hf][:, :], pT[:, k, t * P:(t + 1) * P], plew[:, k, hf * 512:(hf + 1) * 512],
                                  start=(k == 0), stop=(k == 1))
                last.then_inc(S["ple_val"], 1)

            def sh_in(t):
                if t >= 2:
                    pe.wait_ge(S["sh_hid"], t - 1)
                for k in range(KD):
                    last = mm(banks[4 + t % 2][:, :], x1T[:, k, t * P:(t + 1) * P], gu[3][:, k, :, :],
                              start=(k == 0), stop=(k == KD - 1))
                last.then_inc(S["sh_put"], 1)

            def route(t):
                pe.wait_ge(S["pT_kept"], 2)
                pe.wait_ge(S["x1T_kept"], 2 * t + 2)
                for k in range(KD):
                    last = mm(banks[6][:, t * E:(t + 1) * E], x1T[:, k, t * P:(t + 1) * P], wrt[:, k, :],
                              start=(k == 0), stop=(k == KD - 1))
                return last

            ple_value(0)
            route(0)
            route(1)
            x1_turn(TT - 1)
            route(2)
            route(3).then_inc(S["router_put"], 1)
            pe.wait_ge(S["pleg_loaded"], 16)
            ple_gate(0)
            ple_gate(1)
            ple_value(1)
            pe.wait_ge(S["mask_ready"], 1)
            for t in range(TT):
                for s in range(t + 1):
                    mm(banks[7][:, t * E:(t + 1) * E], strict if s == t else ones, mask[:, s, :], start=(s == 0), stop=(s == t))
            for s in range(TT):
                last = mm(banks[7][:, TT * E:(TT + 1) * E], ones, mask[:, s, :], start=(s == 0), stop=(s == TT - 1))
            last.then_inc(S["router_put"], 1)
            pe.wait_ge(S["shared_loaded"], 48)
            sh_in(0)
            for t in (2, 3):
                ple_gate(t)
                ple_value(t)

            def sh_out(t):
                pe.wait_ge(S["sh_hid"], t + 1)
                if t == 0:
                    pe.wait_ge(S["ple_done"], TT)
                else:
                    pe.wait_ge(S["sh_hT"], t)
                hv = hdn[t % 2].rearrange("p (d k) -> p k d", k=2)
                for k in range(2):
                    last = tp(banks[0][:, k * P:(k + 1) * P], hv[:, k, :], P)
                last.then_inc(S["sh_hT_put"], 1)
                pe.wait_ge(S["sh_hT"], t + 1)
                pe.wait_ge(S["slot_ready"], 1)
                if t:
                    pe.wait_ge(S["sh_done"], t)
                for hf in range(2):
                    for k in range(2):
                        last = mm(banks[6 + hf][:, :], hT[t % 2][:, k, :], dn[3][:, k, hf * 512:(hf + 1) * 512],
                                  start=(k == 0), stop=(k == 1))
                last.then_inc(S["sh_y_put"], 1)

            for t in range(TT):
                if t + 1 < TT:
                    sh_in(t + 1)
                if t == TT - 1:
                    pe.wait_ge(S["tok_loaded"], 16)
                    for v in range(2):
                        last = tp(banks[1][0:SL, v * P:v * P + NT], slotR[:, :, v], NT)
                    last.then_inc(S["tokT_put"], 1)
                sh_out(t)

            def x_turn(i, u):
                pe.wait_ge(s_gath[u % 4], 16 * i + 16 * (u // 4 + 1))
                wait(pe, S["xT_e_act"], 4 * i + u)
                wait(pe, S["xT_e_dve"], 4 * i + u)
                xv = xg[u % 4].rearrange("p (d k) -> p k d", k=KD)
                for h in range(2):
                    for k in range(4):
                        last = tp(banks[h][:, k * SL:(k + 1) * SL], xv[:, 4 * h + k, :], SL)
                last.then_inc(S["xT_e_put"], 1)

            def gate_up(i, u):
                pe.wait_ge(s_wgu[u % 4], 32 * i + 32 * (u // 4 + 1))
                pe.wait_ge(S["xT_e_act"], 4 * i + u + 1)
                pe.wait_ge(S["xT_e_dve"], 4 * i + u + 1)
                for k in range(KD):
                    last = mm(banks[2 + u % 2][0:SL, :], xgT[u % 2][:, k, :], gu[u % 4][:, k, :, :],
                              start=(k == 0), stop=(k == KD - 1))
                last.then_inc(S["g_e_put"], 1)

            def hid_turn(i, u):
                pe.wait_ge(S["hid_e"], 4 * i + u + 1)
                hv = hdn[u % 2][0:SL, :].rearrange("p (d k) -> p k d", k=2)
                for k in range(2):
                    last = tp(banks[4][:, k * SL:(k + 1) * SL], hv[:, k, :], SL)
                last.then_inc(S["hT_e_put"], 1)

            def down(i, u):
                pe.wait_ge(s_wdn[u % 4], 16 * i + 16 * (u // 4 + 1))
                pe.wait_ge(S["hT_e_kept"], 4 * i + u + 1)
                wait(pe, S["y_e_act"], 4 * i + u)
                wait(pe, S["y_e_dve"], 4 * i + u)
                for hf in range(2):
                    for k in range(2):
                        last = mm(banks[5 + hf][0:SL, :], hT[u % 2][:, k, 0:SL], dn[u % 4][:, k, hf * 512:(hf + 1) * 512],
                                  start=(k == 0), stop=(k == 1))
                last.then_inc(S["y_e_put"], 1)

            def expert(i, u, more=True):
                gate_up(i, u)
                if more:
                    x_turn(i, u + 1)
                if not isinstance(i, int) or u:
                    down(i, u - 1)
                hid_turn(i, u)

            pe.wait_ge(S["idx_ready"], 1)
            pe.wait_ge(S["sh_done"], TT)
            x_turn(0, 0)
            for u in range(0, 5):
                expert(0, u)
            with pe.Fori(1, E // 4 - 1) as i:
                for u in range(1, 5):
                    expert(i, u)
            for n in range(E - 3, E):
                expert(0, n, more=n + 1 < E)
            down(0, E - 1)
            pe.wait_ge(S["y_e_act"], E)
            pe.wait_ge(S["y_e_dve"], E)
            pe.wait_ge(S["texp_ready"], 1)
            n_over = pe.value_load(novi[0:1, 0:1].bitcast(i32), min_val=0, max_val=OV)
            with pe.If(n_over > 0):
                with pe.Fori(0, OV) as i:
                    with pe.If(i < n_over):
                        pe.wait_ge(s_gath[0], 16 * i + 16 * (E // 4 + 1))
                        xv = xg[0].rearrange("p (d k) -> p k d", k=KD)
                        for h in range(2):
                            for k in range(4):
                                last = tp(banks[h][:, k * SL:(k + 1) * SL], xv[:, 4 * h + k, :], SL)
                        last.then_inc(S["o_xT_put"], 1)
                        pe.wait_ge(S["o_xT_kept"], i + 1)
                        pe.wait_ge(S["o_w"], 48 * i + 48)
                        for k in range(KD):
                            last = mm(banks[2][0:SL, :], xgT[0][:, k, :], gu[0][:, k, :, :], start=(k == 0), stop=(k == KD - 1))
                        last.then_inc(S["o_g_put"], 1)
                        pe.wait_ge(S["o_hid"], i + 1)
                        hv = hdn[0][0:SL, :].rearrange("p (d k) -> p k d", k=2)
                        for k in range(2):
                            last = tp(banks[4][:, k * SL:(k + 1) * SL], hv[:, k, :], SL)
                        last.then_inc(S["o_hT_put"], 1)
                        pe.wait_ge(S["o_hT_kept"], i + 1)
                        for hf in range(2):
                            for k in range(2):
                                last = mm(banks[5 + hf][0:SL, :], hT[0][:, k, 0:SL], dn[0][:, k, hf * 512:(hf + 1) * 512],
                                          start=(k == 0), stop=(k == 1))
                        last.then_inc(S["o_y_put"], 1)
                    pe.nop()

        @block.scalar
        def _(act):
            def f(out_, in_, func, **kw):
                return nc.scalar.activation(out_, in_, func, **kw)

            for t in range(TT):
                act.wait_ge(S["xT_put"], 2 * t + 1)
                f(xT[:, 0:4, t * P:(t + 1) * P], banks[2 * t][:, :].rearrange("p (k x) -> p k x", k=4),
                  ACT.Copy).then_inc(S["xT_act"], 1)
            act.wait_ge(S["s5_loaded"], 48)
            f(ldt[:, 2:4], ldt[:, 0:2], ACT.Exp).then_inc(S["polar_ready"], 1)
            act.wait_ge(S["dar_ready"], 1)
            f(p_mg, p_dar, ACT.Exp)
            f(sm[:, 7, :], p_dar, ACT.Exp, scale=float(L)).then_inc(S["polar_ready"], 1)
            act.wait_ge(S["dar_ready"], 2)
            f(sm[:, 2, :], p_t1, ACT.Sin)
            f(sm[:, 3, :], sm[:, 1, :], ACT.Sin).then_inc(S["polar_ready"], 1)
            act.wait_ge(S["rows_kept"], 1)
            f(lnt[:, MR:2 * MR], lnt[:, 0:MR], ACT.Exp, scale=-1.0).then_inc(S["polar_ready"], 1)
            for c in (1, 3):
                act.wait_ge(S["bc_put"], c + 1)
                f((bT if c < 2 else cT)[:, 1].rearrange("p j q -> p (j q)"), banks[1 + c][:, :], ACT.Copy).then_inc(S["bc_kept"], 1)

            def high_a(m, n):
                act.wait_ge(s_w[m], 16 * (n + 1))
                f(wa_hi[m], wa[m], ACT.Copy).then_inc(S["w_high"], 1)

            def high_b(n):
                before = 32 * NB if n % 4 < ML else 0
                nk = MR if n % 5 == 4 else KD
                act.wait_ge(s_w[n % 4], before + 16 * (n // 4 + 1))
                f(wb_hi[n % 4][:, 0:nk], wb[n % 4][:, 0:nk], ACT.Copy).then_inc(S["w_high"], 1)

            for m in range(ML):
                high_a(m, 0)
            act.wait_ge(S["xT_dve"], TT)
            for k in range(KD):
                f(xH[k], xT[:, k], ACT.Copy).then_inc(S["high_ready"], 1)
            for n in range(2 * TT):
                hf, t = divmod(n, TT)
                act.wait_ge(S["u_put"], n + 1)
                f(usb[:, t, hf * 512:(hf + 1) * 512], banks[(5 + n) % 8][:, :], ACT.Copy).then_inc(S["u_kept"], 1)
            act.wait_ge(S["lru_c_ready"], 1)
            for b in range(NB):
                for m in range(ML):
                    if m == 2:
                        high_a(0, 2 * b + 1)
                    ch = ML * b + m
                    act.wait_ge(S["xproj_put"], ML * b + m + 1)
                    need(act, "lru_done", ML * b)
                    f(xc[:, m, :], banks[m][:, :], ACT.Identity, scale=chan[:, 3 * MR + ch:3 * MR + ch + 1],
                      bias=chan[:, 4 * MR + ch:4 * MR + ch + 1]).then_inc(S["conv_begun"], 1)
                for s in range(2):
                    act.wait_ge(S["U_put"], 2 * b + s + 1)
                    f(U[:, 8 * s:8 * s + 8, :].rearrange("p g c -> p (g c)"), banks[4 + s][:, :], ACT.Copy).then_inc(S["U_kept"], 1)
                if b == 0:
                    act.wait_ge(S["u_stored"], 16)
                for j in range(4):
                    act.wait_ge(S["RT_put"], 4 * b + j + 1)
                    f(RT[:, 2 * j:2 * j + 2].rearrange("p q c x -> p (q c x)"), banks[4 + j][:, :], ACT.Copy).then_inc(S["RT_kept"], 1)
                high_a(1, 2 * b + 1)
                high_a(2, 2 * b + 1)
                for m in range(ML):
                    act.wait_ge(S["gproj_put"], ML * b + m + 1)
                    f(ylru[:, ML * b + m, :], banks[G_BANKS[m]][:, :], ACT.Gelu_apprx_tanh).then_inc(S["g_kept"], 1)
                    for n in range(4 if m == 0 else 0):
                        j, h = divmod(n, 2)
                        act.wait_ge(S["K_put"], 2 * b + j + 1)
                        f(Kp.rearrange("p (j q h) x -> p j q h x", q=4, h=2)[:, j, :, h, (L - 1) * GP:],
                          banks[4 + 2 * h + j][0:GP, :].rearrange("p (q x) -> p q x", q=4), ACT.Copy).then_inc(S["K_kept"], 1)
                if b + 1 < NB:
                    high_a(0, 2 * b + 2)
                for n in range(2 * ML):
                    g, m = divmod(n, ML)
                    ch = (5 + g) * MR + ML * b + m
                    act.wait_ge(S["gates_put"], 6 * b + n + 1)
                    f((rr, ii)[g][:, m, :], banks[LRU_BANKS[n]][:, :], ACT.Sigmoid, bias=chan[:, ch:ch + 1]).then_inc(S["gates_kept"], 1)
                    if n == 3 and b + 1 == NB:
                        high_b(0)
                if b + 1 < NB:
                    high_a(1, 2 * b + 2)
                    high_a(2, 2 * b + 2)
                else:
                    high_b(1)
                act.drain()
                for m in range(ML):
                    ch = ML * b + m
                    f(aa[:, m, :], rr[:, m, :], ACT.Exp, scale=c_lru[:, ch:ch + 1])
                    act.drain()
                    f(rr[:, m, :], rr[:, m, :], ACT.Tanh, scale=c_lru[:, MR + ch:MR + ch + 1]).then_inc(S["decay_ready"], 1)
                for m in range(ML):
                    act.wait_ge(S["mult2_ready"], ML * b + m + 1)
                    f(rr[:, m, :], rr[:, m, :], ACT.Sqrt).then_inc(S["mult_ready"], 1)
                act.wait_ge(S["k_stored"], 16 * (b + 1))
                for n in range(4):
                    j, h = divmod(n, 2)
                    act.wait_ge(S["Y_put"], 2 * b + j + 1)
                    f(Y2.rearrange("c l (j q h o) -> c j h q l o", j=2, q=4, h=2)[:, j, h],
                      banks[4 + 2 * h + j][0:NC, :].rearrange("c (q l o) -> c q l o", q=4, l=L),
                      ACT.Gelu_apprx_tanh).then_inc(S["Y_kept"], 1)
                for s in range(2):
                    act.wait_ge(S["yT_put"], 2 * b + s + 1)
                    f(ysT[:, 2 * b + s, :].rearrange("p (c l) -> p l c", l=L),
                      banks[4 + s][:, :].rearrange("p (l c) -> p l c", l=L), ACT.Copy).then_inc(S["yT_kept"], 1)
            act.drain()
            for k in range(KD):
                if k == KD - 1:
                    act.wait_ge(S["lru_done"], MR)
                f(yH[k], ysT[:, k], ACT.Copy).then_inc(S["high_ready"], 1)
                if k == 0:
                    high_b(2)
            high_b(3)
            for k in range(MR):
                f(lH[k], ylru[:, k], ACT.Copy).then_inc(S["high_ready"], 1)
                if k == 3:
                    high_b(4)
            for n in range(5 * KD):
                m, j = divmod(n, 5)
                if j == 0:
                    need(act, "b_done", m - 1)
                if j < 3:
                    act.wait_ge(S["b_val"], n + 1)
                    kw = {"bias": chan[:, 8 * MR + KD + m:8 * MR + KD + m + 1]} if j == 2 else {}
                    f(sg[m % 2][j], banks[n % 8][:, :], ACT.Sigmoid, **kw).then_inc(S["b_sig"], 1)
                if 0 < n < 5 * KD - 4:
                    high_b(n + 4)
            def x1_kept(t, halves):
                act.wait_ge(S["x1T_put"], t + 1)
                for h in halves:
                    f(x1T[:, 4 * h:4 * h + 4, t * P:(t + 1) * P], banks[4 + h][:, :].rearrange("p (k x) -> p k x", k=4),
                      ACT.Copy).then_inc(S["x1T_kept"], 1)

            for t in range(TT):
                act.wait_ge(S["var_ready"], t + 1)
                f(stats[:, 4 * t + 2:4 * t + 3], stats[:, 4 * t + 1:4 * t + 2], ACT.Sqrt, bias=eps_t[:, 0:1]).then_inc(S["std_ready"], 1)
                if t == 2:
                    act.wait_ge(S["pT_put"], 1)
                    for c in range(2):
                        f(pT[:, c, :], banks[6 + c][:, :], ACT.Copy).then_inc(S["pT_kept"], 1)
                if t:
                    x1_kept(t - 1, (0, 1))
            x1_kept(TT - 1, (0,))
            act.wait_ge(S["router_put"], 1)
            f(score.rearrange("p t e -> p (t e)"), banks[6][:, 0:TT * E], ACT.Sigmoid).then_inc(S["score_ready"], 1)
            for t in range(TT):
                act.wait_ge(S["pg_biased"], 2 * t + 2)
                f(tmpd[t % 2], tmpd[t % 2], ACT.Sigmoid).then_inc(S["pg_sig"], 1)
            act.wait_ge(S["ple_done"], TT)
            for t in range(TT):
                act.wait_ge(S["sh_put"], t + 1)
                need(act, "sh_hid", t - 1)
                f(sil[t % 2], banks[4 + t % 2][:, 0:F], ACT.Silu).then_inc(S["sh_silu"], 1)
            def rows_kept(i, u):
                act.wait_ge(S["xT_e_put"], 4 * i + u + 1)
                f(xgT[u % 2][:, 0:4, :], banks[0][:, 0:4 * SL].rearrange("p (k x) -> p k x", k=4), ACT.Copy).then_inc(S["xT_e_act"], 1)

            def y_kept(i, u):
                wait(act, S["rows_added"], 64 * i + 16 * (u - 1))
                act.wait_ge(S["y_e_put"], 4 * i + u + 1)
                f(yb[u % 2][:, 0:512], banks[5][0:SL, :], ACT.Copy).then_inc(S["y_e_act"], 1)

            def expert(i, u, more=True):
                act.wait_ge(S["g_e_put"], 4 * i + u + 1)
                wait(act, S["hid_e"], 4 * i + u - 1)
                f(sil[u % 2][0:SL, :], banks[2 + u % 2][0:SL, 0:F], ACT.Silu).then_inc(S["silu_e"], 1)
                if more:
                    rows_kept(i, u + 1)
                if not isinstance(i, int) or u >= 1:
                    y_kept(i, u - 1)

            rows_kept(0, 0)
            for u in range(0, 5):
                expert(0, u)
            with act.Fori(1, E // 4 - 1) as i:
                for u in range(1, 5):
                    expert(i, u)
            for n in range(E - 3, E):
                expert(0, n, more=n + 1 < E)
            y_kept(0, E - 1)
            act.wait_ge(S["texp_ready"], 1)
            n_over = act.value_load(novi[0:1, 0:1].bitcast(i32), min_val=0, max_val=OV)
            with act.If(n_over > 0):
                with act.Fori(0, OV) as i:
                    with act.If(i < n_over):
                        act.wait_ge(S["o_xT_put"], i + 1)
                        f(xgT[0][:, 0:4, :], banks[0][:, 0:4 * SL].rearrange("p (k x) -> p k x", k=4), ACT.Copy).then_inc(S["o_xT_act"], 1)
                        act.wait_ge(S["o_g_put"], i + 1)
                        f(sil[0][0:SL, :], banks[2][0:SL, 0:F], ACT.Silu).then_inc(S["o_silu"], 1)
                    act.nop()
            for t in range(TT):
                act.wait_ge(S["var_ready"], TT + t + 1)
                f(stats[:, 4 * t + 2:4 * t + 3], stats[:, 4 * t + 1:4 * t + 2], ACT.Sqrt, bias=eps_t[:, 0:1]).then_inc(S["std_ready"], 1)

        @block.vector
        def _(dve):
            V_ = nc.vector

            def d():
                dve.drain()

            def tt(out_, a, b_, op):
                return V_.tensor_tensor(out_, a, b_, op)

            def ts(out_, a, s1, s2, op0, op1=ALU.bypass):
                return V_.tensor_scalar(out_, a, s1, s2, op0, op1)

            def stt(out_, a, s, b_, op0, op1):
                return V_.scalar_tensor_tensor(out_, a, s, b_, op0, op1)

            for t in range(TT):
                dve.wait_ge(S["xT_put"], 2 * t + 2)
                V_.tensor_copy(xT[:, 4:8, t * P:(t + 1) * P],
                               banks[2 * t + 1][:, :].rearrange("p (k x) -> p k x", k=4)).then_inc(S["xT_dve"], 1)
            dve.wait_ge(S["polar_ready"], 1)
            for h in range(2):
                hs = slice(h * NS, (h + 1) * NS)
                ts(p_dar[:, hs], p_are[:, hs], ldt[:, 2 + h:3 + h], None, ALU.mult)
                ts(p_ph[:, hs], p_aim[:, hs], ldt[:, 2 + h:3 + h], None, ALU.mult)
            d()
            dve.sem_inc(S["dar_ready"], 1)
            ts(p_t0, p_ph, 1.0 / TWO_PI, MAGIC, ALU.mult, ALU.add)
            d()
            ts(p_t0, p_t0, -MAGIC, None, ALU.add)
            d()
            stt(p_t1, p_t0, -C1, p_ph, ALU.mult, ALU.add)
            d()
            stt(p_t1, p_t0, -C2, p_t1, ALU.mult, ALU.add)
            d()
            stt(p_t1, p_t0, -C3, p_t1, ALU.mult, ALU.add)
            d()
            ts(p_t1, p_t1, PI_IN, -PI_IN, ALU.min, ALU.max)
            d()
            stt(sm[:, 1, :], p_t1, -1.0, p_t1, ALU.mult, ALU.max)
            d()
            ts(sm[:, 1, :], sm[:, 1, :], -1.0, math.pi / 2, ALU.mult, ALU.add).then_inc(S["dar_ready"], 1)
            dve.wait_ge(S["rows_put"], 1)
            V_.tensor_copy(chan, banks[0][:, 0:112])
            V_.tensor_copy(dT, banks[0][0:GP, P:P + G])
            d()
            lam = chan[:, 7 * MR:8 * MR]
            stt(lnt[:, 0:MR], lam, -1.0, lam, ALU.mult, ALU.max)
            d()
            dve.sem_inc(S["rows_kept"], 1)
            ex, w1, w2, w3, w4 = (lnt[:, n * MR:(n + 1) * MR] for n in (1, 2, 3, 4, 5))
            dve.wait_ge(S["polar_ready"], 4)
            ts(w1, ex, 2.0, None, ALU.add)
            d()
            V_.reciprocal(w2, w1)
            d()
            tt(w1, ex, w2, ALU.mult)
            d()
            tt(w2, w1, w1, ALU.mult)
            V_.memset(w3, 1.0 / 17)
            d()
            for n in range(15, 0, -2):
                tt(w3, w3, w2, ALU.mult)
                d()
                ts(w3, w3, 1.0 / n, None, ALU.add)
                d()
            stt(w3, w3, 2.0, w1, ALU.mult, ALU.mult)
            ts(w4, lam, -1.0, 0.0, ALU.mult, ALU.max)
            d()
            tt(w3, w3, w4, ALU.add)
            d()
            ts(c_lru[:, 0:MR], w3, -8.0, None, ALU.mult)
            ts(c_lru[:, MR:2 * MR], w3, 8.0, None, ALU.mult).then_inc(S["lru_c_ready"], 1)
            for c in (0, 2):
                dve.wait_ge(S["bc_put"], c + 1)
                V_.tensor_copy((bT if c < 2 else cT)[:, 0].rearrange("p j q -> p (j q)"), banks[1 + c][:, :]).then_inc(S["bc_kept"], 1)
            dve.wait_ge(S["bc_kept"], 4)
            dve.wait_ge(S["polar_ready"], 3)
            sin, cos = sm[:, 2, :], sm[:, 3, :]
            tt(pr[:, 1, 0, :], p_mg, cos, ALU.mult)
            tt(pr[:, 1, 1, :], p_mg, sin, ALU.mult)
            tt(sm[:, 5, :], p_are, p_are, ALU.mult)
            tt(sm[:, 6, :], p_aim, p_aim, ALU.mult)
            d()
            ts(sm[:, 4, :], pr[:, 1, 0, :], -1.0, None, ALU.add)
            tt(sm[:, 5, :], sm[:, 5, :], sm[:, 6, :], ALU.add)
            d()
            V_.reciprocal(sm[:, 6, :], sm[:, 5, :])
            tt(sm[:, 8, :], sm[:, 4, :], p_are, ALU.mult)
            tt(sm[:, 9, :], pr[:, 1, 1, :], p_aim, ALU.mult)
            tt(sm[:, 10, :], pr[:, 1, 1, :], p_are, ALU.mult)
            tt(sm[:, 11, :], sm[:, 4, :], p_aim, ALU.mult)
            d()
            tt(sm[:, 8, :], sm[:, 8, :], sm[:, 9, :], ALU.add)
            tt(sm[:, 10, :], sm[:, 10, :], sm[:, 11, :], ALU.subtract)
            d()
            tt(sm[:, 8, :], sm[:, 8, :], sm[:, 6, :], ALU.mult)
            tt(sm[:, 10, :], sm[:, 10, :], sm[:, 6, :], ALU.mult)
            for _ in range(3):
                tt(sm[:, 0, :], cos, cos, ALU.mult)
                tt(sm[:, 1, :], sin, sin, ALU.mult)
                tt(sm[:, 4, :], cos, sin, ALU.mult)
                d()
                tt(cos, sm[:, 0, :], sm[:, 1, :], ALU.subtract)
                ts(sin, sm[:, 4, :], 2.0, None, ALU.mult)
                d()
            for n in (1, 2, 4):
                src, one = pr[:, 1:n + 1], pr[:, n]
                x, y = (tA[0:NQ, k * 512:k * 512 + n * P].rearrange("q (j x) -> q j x", j=n) for k in range(2))
                cr, ci = bc(one[:, 0, :], 1, n), bc(one[:, 1, :], 1, n)
                dst = pr[:, n + 1:2 * n + 1]
                for c, (f0, f1, op) in enumerate(((cr, ci, ALU.subtract), (ci, cr, ALU.add))):
                    tt(pq0[:, 0:n], src[:, :, 0, :], f0, ALU.mult)
                    tt(pq1[:, 0:n], src[:, :, 1, :], f1, ALU.mult)
                    d()
                    tt(dst[:, :, c, :], pq0[:, 0:n], pq1[:, 0:n], op)
                    d()
            dve.sem_inc(S["powers_ready"], 1)

            def low(dst, v, hi, n):
                dve.wait_ge(S["high_ready"], n + 1)
                tt(dst, v, hi.bitcast(f32), ALU.subtract).then_inc(S["low_ready"], 1)

            dve.wait_ge(S["u_put"], 2 * TT)
            for k in range(KD):
                low(xL[k], xT[:, k], xH[k], k)
            dve.wait_ge(S["powers_put"], 1)
            V_.tensor_copy(pw[:, 1:L + 1].rearrange("p j c q -> p (j c q)"), banks[5][:, :])
            V_.tensor_copy(misc.rearrange("p v q -> p (v q)"), banks[6][:, 0:5 * NQ])
            V_.memset(pw[:, 0, 0, :], 1.0)
            V_.memset(pw[:, 0, 1, :], 0.0)
            d()
            dve.sem_inc(S["powers_kept"], 1)
            zr, zi = bc(misc[:, 0, :], 1, GP), bc(misc[:, 1, :], 1, GP)
            w = [at(tmp_off + n * 512, 512).rearrange("p (j q) -> p j q", j=GP) for n in range(4)]
            tt(w[0], bT[:, 0], zr, ALU.mult)
            tt(w[1], bT[:, 1], zi, ALU.mult)
            tt(w[2], bT[:, 1], zr, ALU.mult)
            tt(w[3], bT[:, 0], zi, ALU.mult)
            d()
            tt(bT[:, 0], w[0], w[1], ALU.subtract)
            tt(bT[:, 1], w[2], w[3], ALU.add)
            d()

            def tables(b):
                qs = slice(b * QB, (b + 1) * QB)
                need(dve, "k_stored", 16 * b)
                if b == 0:
                    dve.wait_ge(S["xT_put"], 2 * TT)
                x, y = (tm.rearrange("p (q j o) -> p q j o", q=QB, j=L + 1) for tm in (tA, tB))
                x8, y8 = (at(o, QB * P).rearrange("p (q l o) -> p q l o", q=QB, l=L) for o in (tmp_off, tmp_off + tq))
                Rv = R.rearrange("p c q (l o) -> p c q l o", l=L)
                bb = [bT[:, c, :, qs].rearrange("p o q -> p q o") for c in range(2)]
                for c, (c0, c1, op) in enumerate(((0, 1, ALU.subtract), (1, 0, ALU.add))):
                    for l in range(L):
                        pv = [bc(pw[:, L - 1 - l, k, qs], 2, GP) for k in range(2)]
                        tt(x8[:, :, l, :], bb[0], pv[c0], ALU.mult)
                        tt(y8[:, :, l, :], bb[1], pv[c1], ALU.mult)
                    d()
                    ins = tt(Rv[:, c], x8, y8, op)
                    d()
                dve.sem_inc(S["R_ready"], 1)
                need(dve, "Y_put", 2 * b)
                cc = [cT[:, c, :, qs].rearrange("p o q -> p q o") for c in range(2)]
                for c in range(2):
                    for j in range(L + 1):
                        pv = [bc(pw[:, j, k, qs], 2, GP) for k in range(2)]
                        tt(x[:, :, j, :], cc[0], pv[c], ALU.mult)
                        tt(y[:, :, j, :], cc[1], pv[1 - c], ALU.mult)
                    d()
                    if c == 0:
                        tt(Q[:, 0], x, y, ALU.subtract)
                    else:
                        stt(Q[:, 1].rearrange("p q j o -> p (q j o)"), tA, -1.0, tB, ALU.mult, ALU.subtract)
                    d()
                dve.sem_inc(S["Q_ready"], 1)

            def turns(b):
                qs = slice(b * QB, (b + 1) * QB)
                V_.memset(Et[:, 0, :, 0:1], 1.0)
                V_.memset(Et[:, 1, :, 0:1], 0.0)
                V_.tensor_copy(V[:, 0, :], misc[:, 3, qs])
                V_.tensor_copy(V[:, 1, :], misc[:, 4, qs])
                V_.tensor_copy(mag, bc(misc[:, 2, qs], 2, NC))
                d()
                V_.memset(mag[:, :, 0:1], 0.0)
                n = 1
                while n < NC:
                    if n == 16:
                        dve.wait_ge(S["K_kept"], 5 * (b + 1))
                        tt(Kp[:, :, (L - 1) * GP:L * GP], Kp[:, :, (L - 1) * GP:L * GP], dI, ALU.add).then_inc(S["K_ready"], 1)
                    vr, vi = bc(V[:, 0, :], 2, n), bc(V[:, 1, :], 2, n)
                    a0, a1, a2, a3 = (t5[k][:, :, 0:n] for k in range(4))
                    tt(a0, Et[:, 0, :, 0:n], vr, ALU.mult)
                    tt(a1, Et[:, 1, :, 0:n], vi, ALU.mult)
                    tt(a2, Et[:, 0, :, 0:n], vi, ALU.mult)
                    tt(a3, Et[:, 1, :, 0:n], vr, ALU.mult)
                    if 2 * n < NC:
                        tt(V[:, 2, :], V[:, 0, :], V[:, 1, :], ALU.mult)
                        tt(V[:, 3, :], V[:, 1, :], V[:, 1, :], ALU.mult)
                    d()
                    tt(Et[:, 0, :, n:2 * n], a0, a1, ALU.subtract)
                    tt(Et[:, 1, :, n:2 * n], a2, a3, ALU.add)
                    if 2 * n < NC:
                        tt(V[:, 0, :], V[:, 0, :], V[:, 0, :], ALU.mult)
                        ts(V[:, 1, :], V[:, 2, :], 2.0, None, ALU.mult)
                        d()
                        tt(V[:, 0, :], V[:, 0, :], V[:, 3, :], ALU.subtract)
                    d()
                    n *= 2
                V_.memset(hp[:, :, :, 0:1].rearrange("p c q o -> p (c q) o"), 0.0)
                d()

            tables(0)
            for b in range(NB):
                for m in range(ML):
                    ch = ML * b + m
                    dve.wait_ge(S["conv_begun"], ch + 1)
                    for s in range(1, 4):
                        wc = (3 - s) * MR + ch
                        ins = stt(xc[:, m, s:], banks[m][:, 0:T - s], chan[:, wc:wc + 1], xc[:, m, s:], ALU.mult, ALU.add)
                        if s < 3:
                            d()
                    ins.then_inc(S["conv_done"], 1)
                turns(b)
                dve.wait_ge(S["S_put"], b + 1)
                sr, si = (banks[4 + c][:, :].rearrange("p (q n) -> p q n", q=QB) for c in range(2))
                er, ei = Et[:, 0], Et[:, 1]
                a0, a1, a2, a3 = t5
                tt(a0, er, sr, ALU.mult)
                tt(a1, ei, si, ALU.mult)
                tt(a2, er, si, ALU.mult)
                tt(a3, ei, sr, ALU.mult)
                d()
                tt(a0, a0, a1, ALU.add)
                tt(a2, a2, a3, ALU.subtract)
                d()
                flat = [v.rearrange("p q n -> p (q n)") for v in (mag, a0, a1, a2, a3)]
                V_.tensor_tensor_scan(flat[2], flat[0], flat[1], 0.0, ALU.mult, ALU.add)
                V_.tensor_tensor_scan(flat[4], flat[0], flat[3], 0.0, ALU.mult, ALU.add)
                d()
                hr, hi = hp[:, 0, :, 1:NC + 1], hp[:, 1, :, 1:NC + 1]
                tt(a0, er, a1, ALU.mult)
                tt(a2, ei, a3, ALU.mult)
                d()
                tt(hr, a0, a2, ALU.subtract)
                d()
                tt(a0, er, a3, ALU.mult)
                tt(a2, ei, a1, ALU.mult)
                d()
                tt(hi, a0, a2, ALU.add).then_inc(S["h_ready"], 1)
                for m in range(ML):
                    ch = ML * b + m
                    dve.wait_ge(S["square_ready"], ch + 1)
                    stt(rr[:, m], xc[:, m], 1.0, rr[:, m], ALU.add, ALU.mult).then_inc(S["mult2_ready"], 1)
                for m in range(ML):
                    ch = ML * b + m
                    dve.wait_ge(S["mult_ready"], ch + 1)
                    dve.wait_ge(S["ix_ready"], ch + 1)
                    V_.memset(rr[:, m, 0:1], 1.0)
                    d()
                    tt(ii[:, m], ii[:, m], rr[:, m], ALU.mult)
                    d()
                    V_.tensor_tensor_scan(rr[:, m], aa[:, m], ii[:, m], 0.0, ALU.mult, ALU.add)
                    d()
                    dve.wait_ge(S["g_kept"], ch + 1)
                    tt(ylru[:, ch], ylru[:, ch], rr[:, m], ALU.mult).then_inc(S["lru_done"], 1)
                if b + 1 < NB:
                    tables(b + 1)
            d()
            dve.wait_ge(S["yT_kept"], 2 * NB)
            for k in range(KD):
                low(yL[k], ysT[:, k], yH[k], KD + k)
            for k in range(MR):
                low(lL[k], ylru[:, k], lH[k], 2 * KD + k)
            for m in range(KD):
                s = sg[m % 2]
                dve.wait_ge(S["b_sig"], 3 * m + 3)
                dve.wait_ge(S["b_val"], 5 * m + 4)
                stt(s[3], banks[(5 * m + 3) % 8][:, :], chan[:, 8 * MR + m:8 * MR + m + 1], s[2], ALU.add, ALU.mult)
                dve.wait_ge(S["b_val"], 5 * m + 5)
                tt(s[4], banks[(5 * m + 4) % 8][:, :], s[0], ALU.mult)
                d()
                tt(s[3], s[3], s[1], ALU.mult)
                d()
                tt(merged[:, m], s[3], s[4], ALU.add).then_inc(S["b_done"], 1)

            def moments(v, t):
                bs = lnt[:, 12 * t:12 * t + 12]
                for h in range(2):
                    V_.bn_stats(bs[:, 6 * h:6 * h + 6], v[:, h * 512:(h + 1) * 512])
                d()
                V_.bn_aggr(stats[:, 4 * t:4 * t + 2], bs).then_inc(S["var_ready"], 1)

            def scale(v, t, gb, n):
                dve.wait_ge(S["std_ready"], n)
                V_.reciprocal(stats[:, 4 * t + 3:4 * t + 4], stats[:, 4 * t + 2:4 * t + 3])
                d()
                ts(v, v, stats[:, 4 * t:4 * t + 1], stats[:, 4 * t + 3:4 * t + 4], ALU.subtract, ALU.mult)
                d()
                return tt(v, v, lnp[:, gb, :], ALU.mult)

            for t in range(TT):
                dve.wait_ge(s_x[t], 32)
                for hf in range(2):
                    n = 2 * t + hf
                    hs = slice(hf * 512, (hf + 1) * 512)
                    dve.wait_ge(S["res_put"], n + 1)
                    stt(x1[:, t, hs], x1[:, t, hs], ALPHA, banks[n % 4][:, :], ALU.mult, ALU.add).then_inc(S["res_added"], 1)
                d()
                moments(x1[:, t, :], t)
                if t == 0:
                    dve.wait_ge(S["lnp_loaded"], 16 * 6)
                scale(x1[:, t, :], t, 0, t + 1)
                d()
                tt(x1[:, t, :], x1[:, t, :], lnp[:, 1, :], ALU.add).then_inc(S["x1_ready"], 1)
            dve.wait_ge(S["x1T_put"], TT)
            V_.tensor_copy(x1T[:, 4:8, (TT - 1) * P:T], banks[5][:, :].rearrange("p (k x) -> p k x", k=4)).then_inc(S["x1T_kept"], 1)
            dve.wait_ge(S["score_ready"], 1)
            dve.wait_ge(S["const_ready"], 2)
            tt(biased, score, bc(rbias, 1, TT), ALU.add)
            d()
            for t in range(TT):
                for g in range(EG):
                    V_.max(gtop[:, t * EG + g, :], biased[:, t, g * 8:(g + 1) * 8])
            d()
            tt(gsum.rearrange("p t g -> p (t g)").unsqueeze(2), gtop[:, :, 0:1], gtop[:, :, 1:2], ALU.add)
            d()
            for t in range(TT):
                mine, other = bc(gsum[:, t, :], 2, EG), bc(gsum[:, t, :], 1, EG)
                tt(pair[:, t], other, mine, ALU.is_gt)
                tt(pair2[:, t], other, mine, ALU.is_equal)
            d()
            tt(pair2, pair2, bc(lt, 1, TT), ALU.mult)
            d()
            tt(pair, pair, pair2, ALU.add)
            d()
            V_.tensor_reduce(gsel, pair, AX, ALU.add)
            d()
            ts(gsel, gsel, TOPG - 0.5, None, ALU.is_lt)
            d()
            gb_ = bc(gsel, 3, 8).rearrange("p t g x -> p (t g) x")
            m8 = lambda v: v.rearrange("p t (g x) -> p (t g) x", g=EG)
            tt(m8(biased), m8(biased), gb_, ALU.mult)
            ts(gsum, gsel, BIG, -BIG, ALU.mult, ALU.add)
            d()
            tt(m8(biased), m8(biased), bc(gsum, 3, 8).rearrange("p t g x -> p (t g) x"), ALU.add)
            d()
            for t in range(TT):
                V_.max(top8[:, t, :], biased[:, t, :])
            d()
            for t in range(TT):
                V_.match_replace(repl[:, t, :], top8[:, t, :], biased[:, t, :], -3 * BIG)
                V_.max_index(idx8[:, t, :].bitcast(u32), top8[:, t, :], biased[:, t, :])
            d()
            ts(mask, repl, -2 * BIG, None, ALU.is_lt)
            V_.tensor_copy(idx8f, idx8.bitcast(u32))
            d()
            dve.sem_inc(S["mask_ready"], 1)

            def ple_bias(t, hf):
                hs = slice(hf * 512, (hf + 1) * 512)
                dve.wait_ge(S["ple_put"], 2 * t + hf + 1)
                tt(tmpd[t % 2][:, hs], banks[hf][:, :], lnp[:, 4, hs], ALU.add).then_inc(S["pg_biased"], 1)

            def ple(t):
                v = tmpd[t % 2]
                for hf in range(1 if t == 2 else 0, 2):
                    ple_bias(t, hf)
                dve.wait_ge(S["pg_sig"], t + 1)
                dve.wait_ge(S["ple_val"], t + 1)
                for hf in range(2):
                    hs = slice(hf * 512, (hf + 1) * 512)
                    tt(v[:, hs], v[:, hs], banks[2 + hf][:, :], ALU.mult)
                d()
                stt(acc[:, t, :], x1[:, t, :], ALPHA, v, ALU.mult, ALU.add).then_inc(S["ple_done"], 1)

            dve.wait_ge(S["padded"], 32)
            ple(0)
            ple(1)
            dve.wait_ge(S["router_put"], 2)
            ranks = banks[7][:, 0:TT * E].rearrange("p (t e) -> p t e", t=TT)
            V_.tensor_copy(row, ranks)
            V_.tensor_copy(cnt, banks[7][:, TT * E:(TT + 1) * E])
            d()
            ts(ovc, cnt, SL + 0.5, None, ALU.is_gt)
            ts(repl, row, SL - 0.5, None, ALU.is_gt)
            d()
            for n in range(2, LEVELS + 1):
                ts(cbase, cnt, n * SL + 0.5, None, ALU.is_gt)
                d()
                tt(ovc, ovc, cbase, ALU.add)
                d()
            V_.tensor_tensor_scan(ovi, ones_e, ovc, 0.0, ALU.mult, ALU.add)
            d()
            tt(cbase, ovi, ovc, ALU.subtract)
            V_.tensor_copy(novi.bitcast(i32), ovi[:, E - 1:E])
            for h in range(2):
                tt(texw, bc(ovi[0:1, :], 1, 24), bc(iota_i[0:1, 24 * h:24 * h + 24], 2, E), ALU.is_le)
                d()
                V_.tensor_reduce(texpf[0:1, 24 * h:24 * h + 24], texw, AX, ALU.add)
                d()
            ts(cbase, cbase, float(SL), float((E - 1) * SL), ALU.mult, ALU.add)
            d()
            tt(cbase, cbase, e128, ALU.subtract)
            ts(texpf[0:1, :], texpf[0:1, :], float(E - 1), None, ALU.min)
            d()
            tt(repl, repl, bc(cbase, 1, TT), ALU.mult)
            V_.tensor_copy(texpi[0:1, :].bitcast(i32), texpf[0:1, :])
            tt(row, row, bc(e128, 1, TT), ALU.add)
            d()
            dve.sem_inc(S["texp_ready"], 1)
            tt(row, row, repl, ALU.add)
            for t in range(TT):
                tt(eqt[:, t], bc(iota_e, 1, K), bc(idx8f[:, t, :], 2, E), ALU.is_equal)
            d()
            for t in range(TT):
                tt(eqp[:, t], eqt[:, t], bc(row[:, t, :], 1, K), ALU.mult)
            d()
            V_.tensor_reduce(slotf, eqp, AX, ALU.add)
            d()
            V_.tensor_copy(sloti.bitcast(i32), slotf)
            ple_bias(2, 0)
            for t in range(TT):
                tt(eqp[:, t], eqt[:, t], bc(score[:, t, :], 1, K), ALU.mult)
            d()
            V_.tensor_reduce(gate, eqp, AX, ALU.add)
            d()
            V_.tensor_reduce(gsc, gate, AX, ALU.add)
            d()
            V_.reciprocal(gsc, gsc)
            d()
            for t in range(TT):
                ts(pairs[:, t, :, 1], gate[:, t, :], gsc[:, t:t + 1], SCALE, ALU.mult, ALU.mult)
            d()
            dve.sem_inc(S["slot_ready"], 1)
            ple(2)
            ple(3)
            def tables_kept():
                dve.wait_ge(S["tokT_put"], 1)
                V_.tensor_copy(gateT, banks[1][0:SL, P:P + NT])
                V_.tensor_copy(idxT.bitcast(i32), banks[1][0:SL, 0:NT])
                d()
                dve.sem_inc(S["idx_ready"], 1)

            for t in range(TT + 1):
                if t < TT:
                    dve.wait_ge(S["sh_silu"], t + 1)
                    if t >= 2:
                        dve.wait_ge(S["sh_hT_put"], t - 1)
                    tt(hdn[t % 2], sil[t % 2], banks[4 + t % 2][:, F:2 * F], ALU.mult).then_inc(S["sh_hid"], 1)
                if t:
                    s = t - 1
                    if s == TT - 1:
                        tables_kept()
                    dve.wait_ge(S["sh_hT_put"], s + 1)
                    V_.tensor_copy(hT[s % 2], banks[0][:, 0:F].rearrange("p (k x) -> p k x", k=2)).then_inc(S["sh_hT"], 1)
                    dve.wait_ge(S["sh_y_put"], s + 1)
                    for hf in range(2):
                        hs = slice(hf * 512, (hf + 1) * 512)
                        ins = tt(acc[:, s, hs], acc[:, s, hs], banks[6 + hf][:, :], ALU.add)
                    ins.then_inc(S["sh_done"], 1)
            def rows_kept(i, u):
                dve.wait_ge(S["xT_e_put"], 4 * i + u + 1)
                V_.tensor_copy(xgT[u % 2][:, 4:8, :], banks[1][:, 0:4 * SL].rearrange("p (k x) -> p k x", k=4)).then_inc(S["xT_e_dve"], 1)

            def y_kept(i, u):
                wait(dve, S["rows_added"], 64 * i + 16 * (u - 1))
                dve.wait_ge(S["y_e_put"], 4 * i + u + 1)
                V_.tensor_copy(yb[u % 2][:, 512:1024], banks[6][0:SL, :]).then_inc(S["y_e_dve"], 1)

            def expert(i, u, more=True):
                dve.wait_ge(S["silu_e"], 4 * i + u + 1)
                stt(hdn[u % 2][0:SL, :], sil[u % 2][0:SL, :], gateT[:, bass.ds(4 * i + u, 1)],
                    banks[2 + u % 2][0:SL, F:2 * F], ALU.mult, ALU.mult).then_inc(S["hid_e"], 1)
                if more:
                    rows_kept(i, u + 1)
                if not isinstance(i, int) or u >= 1:
                    y_kept(i, u - 1)
                dve.wait_ge(S["hT_e_put"], 4 * i + u + 1)
                V_.tensor_copy(hT[u % 2][:, :, 0:SL], banks[4][:, 0:2 * SL].rearrange("p (k x) -> p k x", k=2)).then_inc(S["hT_e_kept"], 1)

            rows_kept(0, 0)
            for u in range(0, 5):
                expert(0, u)
            with dve.Fori(1, E // 4 - 1) as i:
                for u in range(1, 5):
                    expert(i, u)
            for n in range(E - 3, E):
                expert(0, n, more=n + 1 < E)
            y_kept(0, E - 1)
            dve.wait_ge(S["rows_added"], 16 * E)
            dve.sem_inc(S["o_y_kept"], 1)
            n_over = dve.value_load(novi[0:1, 0:1].bitcast(i32), min_val=0, max_val=OV)
            with dve.If(n_over > 0):
                with dve.Fori(0, OV) as i:
                    with dve.If(i < n_over):
                        dve.wait_ge(S["o_xT_act"], i + 1)
                        V_.tensor_copy(xgT[0][:, 4:8, :], banks[1][:, 0:4 * SL].rearrange("p (k x) -> p k x", k=4)).then_inc(S["o_xT_kept"], 1)
                        dve.wait_ge(S["o_silu"], i + 1)
                        stt(hdn[0][0:SL, :], sil[0][0:SL, :], gateT[:, bass.ds(i + E, 1)], banks[2][0:SL, F:2 * F],
                            ALU.mult, ALU.mult).then_inc(S["o_hid"], 1)
                        dve.wait_ge(S["o_hT_put"], i + 1)
                        V_.tensor_copy(hT[0][:, :, 0:SL], banks[4][:, 0:2 * SL].rearrange("p (k x) -> p k x", k=2)).then_inc(S["o_hT_kept"], 1)
                        dve.wait_ge(S["o_y_put"], i + 1)
                        V_.tensor_copy(yb[0][:, 0:512], banks[5][0:SL, :])
                        V_.tensor_copy(yb[0][:, 512:1024], banks[6][0:SL, :])
                        d()
                        dve.sem_inc(S["o_y_kept"], 1)
                    dve.nop()
            for t in range(TT + 1):
                if t < TT:
                    dve.wait_ge(s_acc[t], 16)
                    moments(acc[:, t, :], t)
                if t:
                    scale(acc[:, t - 1, :], t - 1, 2, TT + t).then_inc(S["scaled"], 1)
            d()
            tt(acc[:, TT - 1, :], acc[:, TT - 1, :], lnp[:, 3, :], ALU.add).then_inc(S["last_ready"], 1)


def kernel(**inputs):
    import numpy as np
    import concourse.bacc as bacc
    from concourse.bass_utils import run_bass_kernel_spmd

    nc = bacc.Bacc("TRN2", target_bir_lowering=False, num_devices=1)
    arrays, args = {}, {}
    for name in INPUTS:
        a = np.ascontiguousarray(inputs[name])
        arrays[name + "_in"] = a
        args[name] = nc.dram_tensor(name + "_in", a.shape, mybir.dt.from_np(a.dtype), kind="ExternalInput").ap()
    out = nc.dram_tensor("out_dram", (1, T, D), mybir.dt.float32, kind="ExternalOutput").ap()
    decoder_layer(nc, args, out)
    r = run_bass_kernel_spmd(nc, [arrays], core_ids=[0])
    return r.results[0]["out_dram"]
```
